# Optimizing a Trainium2 kernel written in Bass

```python
import jax, jax.numpy as jnp
from jax import lax
import numpy as np

D_MODEL = 1024
BATCH = 1
SEQ = 2048
DEPTH = 1
DEC_BATCH = 8
DEC_SEQ = 1
PAST_LEN = 16384
PAGE_SIZE = 128

D_POOL = D_MODEL // 2
N_POOL_GROUPS = 4
POOL_GROUP_DIM = D_POOL // N_POOL_GROUPS
POOL_WINDOWS = (2, 4, 8, 16)
POOL_BUF = max(POOL_WINDOWS) - 1
D_SGU = D_MODEL // 2
SGU_HEADS = 4
SGU_HEAD_DIM = D_SGU // SGU_HEADS
CHUNK = 128
D_MIX = D_POOL + D_SGU
D_IN = D_POOL + 2 * D_SGU
N_GROUPS = 4
EXPERTS_PER_GROUP = 8
N_EXPERTS = N_GROUPS * EXPERTS_PER_GROUP
TOP_K_INNER = 2
D_EXPERT = 512
DISPATCH_BLOCK = 128
DEEPNORM_ALPHA = (2.0 * DEPTH) ** 0.25
DEEPNORM_BETA = (8.0 * DEPTH) ** -0.25
LN_EPS = 1e-5

kernel_name = "hymba_pool_sgu_hmoe_deepnorm_adaln_step"

def layer_norm(x, g, b):
    xf = x.astype(jnp.float32)
    mu = jnp.mean(xf, axis=-1, keepdims=True)
    var = jnp.mean(jnp.square(xf - mu), axis=-1, keepdims=True)
    y = (xf - mu) * lax.rsqrt(var + LN_EPS)
    return (y * g.astype(jnp.float32) + b.astype(jnp.float32)).astype(x.dtype)

def pool_mixer(p_ext, pos0, pool_w, pool_scale):
    B, Lx, _ = p_ext.shape
    L = Lx - POOL_BUF
    cs = jnp.cumsum(p_ext.astype(jnp.float32), axis=1)
    cs0 = jnp.concatenate([jnp.zeros((B, 1, D_POOL), jnp.float32), cs], axis=1)
    end = POOL_BUF + 1 + jnp.arange(L)
    pos = pos0 + jnp.arange(L)
    means = []
    for g, w in enumerate(POOL_WINDOWS):
        lo, hi = g * POOL_GROUP_DIM, (g + 1) * POOL_GROUP_DIM
        s = cs0[:, end, lo:hi] - cs0[:, end - w, lo:hi]
        cnt = jnp.minimum(pos + 1, w).astype(jnp.float32)
        means.append(s / cnt[None, :, None])
    mean = jnp.concatenate(means, axis=-1)
    d = (mean - p_ext[:, POOL_BUF:].astype(jnp.float32)).astype(p_ext.dtype)
    d = d.reshape(B, L, N_POOL_GROUPS, POOL_GROUP_DIM)
    out = jnp.einsum('blgc,gcd->blgd', d, pool_w).reshape(B, L, D_POOL)
    return out * pool_scale

def head_norm(v, g):
    B, L, _ = v.shape
    vf = v.reshape(B, L, SGU_HEADS, SGU_HEAD_DIM).astype(jnp.float32)
    mu = jnp.mean(vf, axis=-1, keepdims=True)
    var = jnp.mean(jnp.square(vf - mu), axis=-1, keepdims=True)
    vn = ((vf - mu) * lax.rsqrt(var + LN_EPS)).reshape(B, L, D_SGU)
    return (vn * g.astype(jnp.float32)).astype(v.dtype)

def spatial_gating(u, vn, sgu_w, sgu_b):
    B, L, _ = u.shape
    n = -(-L // CHUNK)
    pad = n * CHUNK - L
    vp = jnp.pad(vn, ((0, 0), (0, pad), (0, 0))).reshape(B, n, CHUNK, SGU_HEADS, SGU_HEAD_DIM)
    mask = jnp.tril(jnp.ones((CHUNK, CHUNK), dtype=bool))
    ws = jnp.where(mask[None], sgu_w, jnp.zeros_like(sgu_w))
    z = jnp.einsum('hts,bnshc->bnthc', ws, vp) + jnp.transpose(sgu_b)[None, None, :, :, None]
    z = z.reshape(B, n * CHUNK, D_SGU)[:, :L]
    return u * z

def expert_mlp(x, wg, wu, wd):
    return (jax.nn.silu(x @ wg) * (x @ wu)) @ wd

def routed_experts(h, expert_idx, weights, w_gate, w_up, w_down):
    T, D = h.shape
    A = T * TOP_K_INNER
    e_flat = expert_idx.reshape(A)
    tok = jnp.repeat(jnp.arange(T, dtype=jnp.int32), TOP_K_INNER)
    wt = weights.reshape(A).astype(h.dtype)
    order = jnp.argsort(e_flat)
    e_s, tok_s, wt_s = e_flat[order], tok[order], wt[order]
    counts = jnp.zeros((N_EXPERTS,), jnp.int32).at[e_flat].add(1)
    padded = ((counts + DISPATCH_BLOCK - 1) // DISPATCH_BLOCK) * DISPATCH_BLOCK
    starts = jnp.cumsum(counts) - counts
    pends = jnp.cumsum(padded)
    pstarts = pends - padded
    dest = pstarts[e_s] + (jnp.arange(A, dtype=jnp.int32) - starts[e_s])
    n_blocks = -(-A // DISPATCH_BLOCK) + N_EXPERTS
    slot_tok = jnp.full((n_blocks * DISPATCH_BLOCK,), T, jnp.int32).at[dest].set(tok_s)
    block_start = jnp.arange(n_blocks, dtype=jnp.int32) * DISPATCH_BLOCK
    block_expert = jnp.clip(jnp.searchsorted(pends, block_start, side='right'), 0, N_EXPERTS - 1)
    h_pad = jnp.concatenate([h, jnp.zeros((1, D), h.dtype)], axis=0)
    xb = h_pad[slot_tok].reshape(n_blocks, DISPATCH_BLOCK, D)

    def one_block(args):
        xblk, e = args
        return expert_mlp(xblk, w_gate[e], w_up[e], w_down[e])

    yb = lax.map(one_block, (xb, block_expert)).reshape(n_blocks * DISPATCH_BLOCK, D)
    y = yb[dest] * wt_s[:, None]
    return jax.ops.segment_sum(y, tok_s, num_segments=T)

def hierarchical_moe(h, rg_w, rg_b, re_w, re_b, w_gate, w_up, w_down):
    T = h.shape[0]
    gl = (h @ rg_w + rg_b).astype(jnp.float32)
    gp = jax.nn.softmax(gl, axis=-1)
    g_sel = jnp.argmax(gl, axis=-1).astype(jnp.int32)
    p_g = jnp.take_along_axis(gp, g_sel[:, None], axis=-1)
    el = (h @ re_w + re_b).astype(jnp.float32).reshape(T, N_GROUPS, EXPERTS_PER_GROUP)
    el_sel = jnp.take_along_axis(el, g_sel[:, None, None], axis=1)[:, 0]
    top_v, top_i = lax.top_k(el_sel, TOP_K_INNER)
    w2 = jax.nn.softmax(top_v, axis=-1) * p_g
    expert_idx = g_sel[:, None] * EXPERTS_PER_GROUP + top_i.astype(jnp.int32)
    return routed_experts(h, expert_idx, w2, w_gate, w_up, w_down)

def trunk_layer(x, c, buf, pos0, w_ada, b_ada, w_in, pool_w, pool_scale, sgu_norm_g, sgu_w, sgu_b,
                w_out, ln1_g, ln1_b, rg_w, rg_b, re_w, re_b, e_wg, e_wu, e_wd, ln2_g, ln2_b):
    B, L, D = x.shape
    mod = (jax.nn.silu(c) @ w_ada + b_ada)[:, None, :]
    sh1, sc1, g1, sh2, sc2, g2 = jnp.split(mod, 6, axis=-1)
    h = x * (1 + sc1) + sh1
    proj = h @ w_in
    p = proj[..., :D_POOL]
    u = proj[..., D_POOL:D_POOL + D_SGU]
    v = proj[..., D_POOL + D_SGU:]
    p_ext = jnp.concatenate([buf.astype(p.dtype), p], axis=1)
    a = pool_mixer(p_ext, pos0, pool_w, pool_scale)
    new_buf = p_ext[:, -POOL_BUF:]
    vn = head_norm(v, sgu_norm_g)
    gsp = spatial_gating(u, vn, sgu_w, sgu_b)
    mix = jnp.concatenate([a, gsp], axis=-1) @ w_out
    x = layer_norm(DEEPNORM_ALPHA * x + (1 + g1) * mix, ln1_g, ln1_b)
    h2 = x * (1 + sc2) + sh2
    f = hierarchical_moe(h2.reshape(B * L, D), rg_w, rg_b, re_w, re_b, e_wg, e_wu, e_wd).reshape(B, L, D)
    x = layer_norm(DEEPNORM_ALPHA * x + (1 + g2) * f, ln2_g, ln2_b)
    return x, new_buf, vn

def setup_inputs(seed: int = 0) -> dict:
    key = jax.random.key(seed)
    ks = jax.random.split(key, 32)
    nrm = lambda k, s, sc: jax.random.normal(k, s, jnp.float32) * sc
    Dm = D_MODEL
    return {
        "x_prompt": nrm(ks[0], (BATCH, SEQ, Dm), 1.0),
        "x_sample": nrm(ks[1], (DEC_BATCH, DEC_SEQ, Dm), 1.0),
        "state_pool": nrm(ks[2], (DEPTH, DEC_BATCH, POOL_BUF, D_POOL), 1.0),
        "c_prompt": nrm(ks[3], (BATCH, Dm), 1.0),
        "c_sample": nrm(ks[4], (DEC_BATCH, Dm), 1.0),
        "w_ada": nrm(ks[5], (DEPTH, Dm, 6 * Dm), 0.1 * Dm ** -0.5),
        "b_ada": nrm(ks[6], (DEPTH, 6 * Dm), 0.01),
        "w_in": nrm(ks[7], (DEPTH, Dm, D_IN), Dm ** -0.5),
        "pool_w": nrm(ks[8], (DEPTH, N_POOL_GROUPS, POOL_GROUP_DIM, POOL_GROUP_DIM), POOL_GROUP_DIM ** -0.5),
        "pool_scale": 1.0 + nrm(ks[9], (DEPTH, D_POOL), 0.1),
        "sgu_norm_g": 1.0 + nrm(ks[10], (DEPTH, D_SGU), 0.1),
        "sgu_w": nrm(ks[11], (DEPTH, SGU_HEADS, CHUNK, CHUNK), CHUNK ** -0.5),
        "sgu_b": 1.0 + nrm(ks[12], (DEPTH, SGU_HEADS, CHUNK), 0.1),
        "w_out": nrm(ks[13], (DEPTH, D_MIX, Dm), DEEPNORM_BETA * D_MIX ** -0.5),
        "ln1_g": 1.0 + nrm(ks[14], (DEPTH, Dm), 0.05),
        "ln1_b": nrm(ks[15], (DEPTH, Dm), 0.02),
        "router_g_w": nrm(ks[16], (DEPTH, Dm, N_GROUPS), Dm ** -0.5),
        "router_g_b": nrm(ks[17], (DEPTH, N_GROUPS), 0.01),
        "router_e_w": nrm(ks[18], (DEPTH, Dm, N_EXPERTS), Dm ** -0.5),
        "router_e_b": nrm(ks[19], (DEPTH, N_EXPERTS), 0.01),
        "exp_w_gate": nrm(ks[20], (DEPTH, N_EXPERTS, Dm, D_EXPERT), Dm ** -0.5),
        "exp_w_up": nrm(ks[21], (DEPTH, N_EXPERTS, Dm, D_EXPERT), Dm ** -0.5),
        "exp_w_down": nrm(ks[22], (DEPTH, N_EXPERTS, D_EXPERT, Dm), DEEPNORM_BETA * D_EXPERT ** -0.5),
        "ln2_g": 1.0 + nrm(ks[23], (DEPTH, Dm), 0.05),
        "ln2_b": nrm(ks[24], (DEPTH, Dm), 0.02),
    }

def reference(x_prompt, x_sample, state_pool, c_prompt, c_sample, w_ada, b_ada, w_in, pool_w, pool_scale,
              sgu_norm_g, sgu_w, sgu_b, w_out, ln1_g, ln1_b, router_g_w, router_g_b, router_e_w, router_e_b,
              exp_w_gate, exp_w_up, exp_w_down, ln2_g, ln2_b):
    xp, xs = x_prompt, x_sample
    pool_p, pool_s, v_s = [], [], []
    zero_buf = jnp.zeros((x_prompt.shape[0], POOL_BUF, D_POOL), x_prompt.dtype)
    for l in range(DEPTH):
        params = (w_ada[l], b_ada[l], w_in[l], pool_w[l], pool_scale[l], sgu_norm_g[l], sgu_w[l], sgu_b[l],
                  w_out[l], ln1_g[l], ln1_b[l], router_g_w[l], router_g_b[l], router_e_w[l], router_e_b[l],
                  exp_w_gate[l], exp_w_up[l], exp_w_down[l], ln2_g[l], ln2_b[l])
        xp, bp, _ = trunk_layer(xp, c_prompt, zero_buf, 0, *params)
        xs, bs, vs = trunk_layer(xs, c_sample, state_pool[l], PAST_LEN, *params)
        pool_p.append(bp)
        pool_s.append(bs)
        v_s.append(vs)
    pool_state_prompt = jnp.stack(pool_p, axis=0)
    pool_state_sample = jnp.stack(pool_s, axis=0)
    sgu_v_sample = jnp.stack(v_s, axis=0)
    return (xp, xs, pool_state_prompt, pool_state_sample, sgu_v_sample)


_drawn_inputs = setup_inputs


def setup_inputs(seed=0):
    import zlib

    import numpy as np

    out = dict(_drawn_inputs(seed))
    spreads = {}
    factors = {'b_ada': 3.41, 'router_g_b': 24.829, 'router_e_b': 6.404, 'ln2_b': 2.847}
    for name, (base, spread) in spreads.items():
        noise = np.random.default_rng([zlib.crc32(name.encode()), seed]).standard_normal(out[name].shape)
        drawn = base * np.exp(spread * noise) if base else spread * noise
        out[name] = __import__('jax').numpy.asarray(drawn.astype(out[name].dtype))
    for name, factor in factors.items():
        out[name] = (out[name] * factor).astype(out[name].dtype)
    return out
```

```python
import concourse.bass as bass
from concourse import mybir
from contextlib import ExitStack

ALU = mybir.AluOpType
ACT = mybir.ActivationFunctionType
AX_X = mybir.AxisListType.X
F32 = mybir.dt.float32
F32R = mybir.dt.float32r
BF16 = mybir.dt.bfloat16
I32 = mybir.dt.int32
U32 = mybir.dt.uint32
ds = bass.ds

P = 128
BANK = 512
WINDOWS = (2, 4, 8, 16)
LN_EPS = 1e-5
ALPHA = 2.0 ** 0.25
BIG = 1.0e30


class Region:

    def __init__(self, nc, start, end):
        self.nc, self.at, self.end = nc, start, end

    def take(self, name, shape, dtype):
        n = mybir.dt.size(dtype)
        for s in shape[1:]:
            n *= s
        t = self.nc.alloc_sbuf_tensor_at(name, shape, dtype, offset=self.at)
        self.at += (n + 31) // 32 * 32
        assert self.at <= self.end, (name, self.at - self.end)
        return t


class Chain:

    def __init__(self, eng, sem):
        self.eng, self.sem, self.n = eng, sem, 0

    def add(self, ins):
        self.n += 1
        ins.then_inc(self.sem, 1)

    def wait(self):
        self.eng.wait_ge(self.sem, self.n)

    def link(self, ins):
        self.add(ins)
        self.wait()

    def restart(self):
        if self.n:
            self.wait()
            self.eng.sem_clear(self.sem)
            self.n = 0


def hybrid_trunk(nc, x_prompt, x_sample, state_pool, c_prompt, c_sample, w_ada, b_ada, w_in, pool_w, pool_scale,
                 sgu_norm_g, sgu_w, sgu_b, w_out, ln1_g, ln1_b, router_g_w, router_g_b, router_e_w, router_e_b,
                 exp_w_gate, exp_w_up, exp_w_down, ln2_g, ln2_b,
                 y_prompt, y_sample, pool_prompt, pool_sample, sgu_v):
    SEQ, D = x_prompt.shape[1:]
    NS = x_sample.shape[0]
    NT = SEQ // P
    KD = D // P
    DP = state_pool.shape[3]
    BUF = state_pool.shape[2]
    NG = pool_w.shape[1]
    NH = sgu_w.shape[1]
    NRG = router_g_w.shape[2]
    NE = router_e_w.shape[2]
    EPG = NE // NRG
    FE = exp_w_gate.shape[3]
    KF = FE // P
    NC = NS + 1
    NA = 3
    NR = NRG + NE
    NTT = NT + 1
    MAXB = (2 * (SEQ + NS) - NE) // P + NE + 1
    PAIRS = (MAXB + 2) // 2
    NB = 2 * PAIRS + 2
    assert D == 8 * P and DP == BANK and FE == BANK and NG == NH == 4 and NT % 2 == 0 and NB <= P

    w_in_v = w_in[0].rearrange("(k p) n -> p k n", p=P)
    w_out_v = w_out[0].rearrange("(k p) n -> p k n", p=P)
    w_ada_v = w_ada[0].rearrange("(k p) (g n) -> k g p n", p=P, g=NA)
    gate_v = exp_w_gate[0].rearrange("e (k p) n -> e p k n", p=P)
    up_v = exp_w_up[0].rearrange("e (k p) n -> e p k n", p=P)
    down_v = exp_w_down[0].rearrange("e (k p) n -> e p k n", p=P)

    mod_d = nc.dram_tensor("mod_rows", [NC, 6 * D], F32).ap()
    h2_d = nc.dram_tensor("h2_rows", [SEQ + NS, D], F32).ap()
    x1_d = nc.dram_tensor("x1_rows", [SEQ + NS, D], F32).ap()
    ye_d = nc.dram_tensor("expert_rows", [NB * P, D], F32).ap()

    ctx = ExitStack()
    with ctx:
        def sem(name):
            return ctx.enter_context(nc.semaphore(name))

        def psum(name, cols=BANK):
            return ctx.enter_context(nc.psum_tensor(name, [P, cols], F32))

        base = (nc.sbuf_base + 127) // 128 * 128
        last = Region(nc, base, base + 21504)
        MIX0 = last.end
        W0 = MIX0 + (NT * 8 * P + 8 * NS) * 4
        W1 = W0 + 3 * KD * FE * 4
        W2 = W1 + 3 * KD * FE * 4
        END = nc.sbuf_usable_end

        ident = last.take("ident", [P, P], F32)
        ones = last.take("ones", [P, P], BF16)
        before = last.take("before", [P, P], BF16)
        iota = last.take("iota", [P, P], F32)
        iota_i = last.take("iota_i", [P, P], I32)
        pcol = last.take("pcol", [P, 1], F32)
        eps = last.take("eps", [P, 1], F32)
        cT = last.take("cT", [P, KD, NC], F32)
        cT_k = last.take("cT_k", [P, NC], F32)
        acc = last.take("acc", [P, NA, BANK], F32)
        rw = last.take("rw", [P, KD, NR], F32)
        rb = last.take("rb", [P, NR], F32)
        picked = last.take("picked", [P, NTT, 2, NE], F32)
        rank = last.take("rank", [P, NTT, 2], F32)
        tops = last.take("tops", [P, NTT, 3, 8], F32)
        top = last.take("top", [P, 3, 8], F32)
        seen = last.take("seen", [P, NE], F32)
        seen_b = last.take("seen_b", [P, NE], BF16)
        wt = last.take("wt", [P, NTT, 2], F32)
        dest_i = last.take("dest_i", [P, NTT, 2], I32)
        cum_f = last.take("cum_f", [P, NE], F32)
        cum_i = last.take("cum_i", [1, NE], I32)
        blk_e = last.take("blk_e", [1, NB], I32)
        tok_i = last.take("tok_i", [P, NB], I32)

        mixT = nc.alloc_sbuf_tensor_at("mixT", [P, NT, KD, P], F32, offset=MIX0)
        mixT_s = nc.alloc_sbuf_tensor_at("mixT_s", [P, KD, NS], F32, offset=MIX0 + NT * 8 * P * 4)
        ada0 = nc.alloc_sbuf_tensor_at("ada0", [P, KD, 4 * BANK], F32, offset=MIX0)

        w_in_sb = nc.alloc_sbuf_tensor_at("w_in_sb", [P, KD, 3 * BANK], F32, offset=W0)
        r = Region(nc, W1, W2)
        x_t = [r.take(f"x_t{i}", [P, D], F32) for i in range(2)]
        h_t = r.take("h_t", [P, D], F32)
        hT = [r.take(f"hT{i}", [P, KD, P], F32) for i in range(2)]
        p_sb = [r.take(f"p_sb{i}", [P, DP], F32) for i in range(2)]
        u_sb = r.take("u_sb", [P, DP], F32)
        vn = r.take("vn", [P, DP], F32)
        dT = r.take("dT", [P, NG, P], F32)
        g_sb = r.take("g_sb", [P, DP], F32)
        band = r.take("band", [P, NG, P], F32)
        band0 = r.take("band0", [P, NG, P], F32)
        bandp = r.take("bandp", [P, NG, P], F32)
        vstat = r.take("vstat", [P, NH, 6], F32)
        vmv = r.take("vmv", [P, NH, 2], F32)
        vstd = r.take("vstd", [P, NH], F32)
        vinv = r.take("vinv", [P, NH], F32)
        bt = r.take("bt", [P, NH], F32)
        psc = r.take("psc", [P, NG], F32)
        b0s = r.take("b0s", [P, NH], F32)
        w0s = r.take("w0s", [P, NH], F32)
        wsT = r.take("wsT", [P, NH, P], F32)
        pw = r.take("pw", [P, NG, P], F32)
        invc = r.take("invc", [P, P], F32)
        zrow = r.take("zrow", [P, D], F32)
        r = Region(nc, W2, END)
        ada_st = [r.take(f"ada_st{i}", [P, 4 * BANK], F32) for i in range(2)]
        sc1 = r.take("sc1", [P, D], F32)
        sh1 = r.take("sh1", [P, D], F32)
        sg_bc = r.take("sg_bc", [P, DP], F32)
        r = Region(nc, W1, W2)
        wst_raw = nc.alloc_sbuf_tensor_at("wst_raw", [P, NH, P], F32, offset=W1)
        c_raw = nc.alloc_sbuf_tensor_at("c_raw", [NC, D], F32, offset=W1 + 4096)
        hist_len = [w - 1 for w in WINDOWS]
        hist = [None] * NG
        at = W2
        for g in range(NG):
            hist[g] = nc.alloc_sbuf_tensor_at(f"hist{g}", [NS, hist_len[g], P], F32, offset=at)
            at += hist_len[g] * P * 4

        w_out_sb = nc.alloc_sbuf_tensor_at("w_out_sb", [P, KD, D], F32, offset=W0 + KD * FE * 4)
        r = Region(nc, W1, W2)
        g1 = r.take("g1", [P, D], F32)
        sc2 = r.take("sc2", [P, D], F32)
        sh2 = r.take("sh2", [P, D], F32)
        lg1 = r.take("lg1", [P, D], F32)
        lb1 = r.take("lb1", [P, D], F32)
        x_r = [r.take(f"x_r{i}", [P, D], F32) for i in range(2)]
        t_r = r.take("t_r", [P, D], F32)
        x1 = r.take("x1", [P, D], F32)
        h2 = [r.take(f"h2_{i}", [P, D], F32) for i in range(2)]
        h2T = r.take("h2T", [P, KD, P], F32)
        small = Region(nc, W2, END)
        mix_cur = [small.take(f"mix_cur{i}", [P, KD, P], F32) for i in range(2)]
        bst = small.take("bst", [P, 2, 6], F32)
        mv = small.take("mv", [P, 2], F32)
        std = small.take("std", [P, 1], F32)
        inv = small.take("inv", [P, 1], F32)
        lgT = small.take("lgT", [P, P], F32)
        el = small.take("el", [P, NE], F32)
        gidx = small.take("gidx", [P, 8], U32)
        gidf = small.take("gidf", [P, 1], F32)
        gm = small.take("gm", [P, NRG], F32)
        eidx = small.take("eidx", [P, 8], U32)
        eidf = small.take("eidf", [P, 2], F32)
        m_b = small.take("m_b", [P, NE], BF16)
        rk = small.take("rk", [P, 2, NE], F32)

        UNIT = 2 * FE
        GU, DN = KD, KF
        NU = GU + DN
        LOW_UNITS = 6
        BLK_END = W0 - LOW_UNITS * UNIT * 4
        r = Region(nc, MIX0, BLK_END)
        pos = r.take("pos", [P, NTT, 2, NE], F32)
        cnt = r.take("cnt", [P, NE], F32)
        cnt_i = r.take("cnt_i", [P, NE], I32)
        nblk = r.take("nblk", [P, NE], F32)
        first = r.take("first", [P, NE], F32)
        zero = r.take("zero", [P, NE], F32)
        dest = r.take("dest", [P, NTT * 2], F32)
        lo_i = r.take("lo_i", [P, NTT * 2], I32)
        hi_i = r.take("hi_i", [P, NTT * 2], I32)
        lo_f = r.take("lo_f", [P, NTT * 2], F32)
        hi_f = r.take("hi_f", [P, NTT * 2], F32)
        oh_lo = r.take("oh_lo", [P, NTT * 2, P], BF16)
        oh_hi = r.take("oh_hi", [P, NTT * 2, 2, NB], BF16)
        tile_f = r.take("tile_f", [P, NTT * 2], F32)
        cmp = r.take("cmp", [1, NB, NE], F32)
        blk_f = r.take("blk_f", [1, NB], F32)
        ex = r.take("ex", [P, NTT], F32)
        tok_a = r.take("tok_a", [P, 2, NB], F32)
        gd = r.take("gd", [P, NTT, 8], F32)
        gsum = r.take("gsum", [P, NTT], F32)
        den = r.take("den", [P, NTT], F32)

        wraw = nc.alloc_sbuf_tensor_at("wraw", [P, NU, UNIT], F32, offset=W0)
        lows = Region(nc, BLK_END, W0)
        highs = Region(nc, W0 + NU * UNIT * 4, END)
        halves = [(lows if n < LOW_UNITS else highs).take(f"w_half{n}", [P, UNIT], F32R) for n in range(2 * NU)]
        w_hi, w_lo = halves[0::2], halves[1::2]
        r = Region(nc, MIX0, BLK_END)
        xg = [r.take(f"xg{i}", [P, D], F32) for i in range(2)]
        xT_hi = [r.take(f"xT_hi{i}", [P, KD, P], F32R) for i in range(2)]
        xT_lo = [r.take(f"xT_lo{i}", [P, KD, P], F32R) for i in range(2)]
        sgate = r.take("sgate", [P, FE], F32)
        act_t = r.take("act_t", [P, FE], F32)
        actT_hi = r.take("actT_hi", [P, KF, P], F32R)
        actT_lo = r.take("actT_lo", [P, KF, P], F32R)
        y_sb = [r.take(f"y_sb{i}", [P, D], F32) for i in range(2)]
        idx = [r.take(f"idx{i}", [P, 1], I32) for i in range(2)]

        r = Region(nc, W0, END)
        ya = [r.take(f"ya{i}", [P, D], F32) for i in range(2)]
        yb = [r.take(f"yb{i}", [P, D], F32) for i in range(2)]
        xf = [r.take(f"xf{i}", [P, D], F32) for i in range(2)]
        fo = [r.take(f"fo{i}", [P, D], F32) for i in range(2)]
        f_a = r.take("f_a", [P, D], F32)
        f_b = [r.take(f"f_b{i}", [P, D], F32) for i in range(2)]
        g2 = r.take("g2", [P, D], F32)
        lg2 = r.take("lg2", [P, D], F32)
        lb2 = r.take("lb2", [P, D], F32)
        idy = [r.take(f"idy{i}", [P, 2], I32) for i in range(2)]
        bs2 = r.take("bs2", [P, 2, 6], F32)
        mv2 = [r.take(f"mv2_{i}", [P, 2], F32) for i in range(2)]
        sd2 = r.take("sd2", [P, 1], F32)
        iv2 = [r.take(f"iv2_{i}", [P, 1], F32) for i in range(2)]
        nb2 = [r.take(f"nb2_{i}", [P, 1], F32) for i in range(2)]

        ps2 = [ctx.enter_context(nc.psum_tensor(f"ps2_{i}", [P, 2 * BANK], F32)) for i in range(4)]
        bank = [ps2[i // 2][:, (i % 2) * BANK:(i % 2 + 1) * BANK] for i in range(8)]

        def mod_row(j):
            return mod_d[NS:NS + 1, j * D:(j + 1) * D].partition_broadcast(P)

        def row(v, n=P):
            return v.rearrange("(a n) -> a n", a=1).partition_broadcast(n)

        s_small = sem("small_loaded")
        s_ws = sem("sgu_w_loaded")
        s_c = sem("c_loaded")
        s_win = sem("w_in_loaded")
        s_ada0 = [sem(f"ada0_loaded{k}") for k in range(KD)]
        s_const = sem("constants_built")
        s_chp = sem("pool_chain")
        s_chv = sem("vector_chain")
        s_cha = sem("scalar_chain")
        s_cs = sem("c_silu")
        s_cTp = sem("cT_in_psum")
        s_cT = sem("cT_ready")
        s_wsp = sem("wsT_in_psum")
        s_wsT = sem("wsT_ready")
        s_adap = sem("ada_in_psum")
        s_modr = sem("mod_rows_ready")
        s_mods = sem("mod_rows_stored")

        with nc.Block() as block:
            @block.sync
            def _(sp):
                sp.dma_start(c_raw[0:NS, :], c_sample).then_inc(s_c, 16)
                sp.dma_start(c_raw[NS:NC, :], c_prompt).then_inc(s_c, 16)
                for k in range(KD):
                    sp.dma_start(ada0[:, k, :], w_ada_v[k, 0]).then_inc(s_ada0[k], 16)
                sp.dma_start(w_in_sb[:, :, :], w_in_v).then_inc(s_win, 16)
                sp.wait_ge(s_modr, 1)
                for j in range(4):
                    sp.dma_start(mod_d[:, j * BANK:(j + 1) * BANK], acc[32 * j:32 * j + NC, 0, :]).then_inc(s_mods, 16)
                sp.wait_ge(s_mods, 64)

            @block.scalar
            def _(act):
                act.dma_start(wst_raw[:, :, :], sgu_w[0].rearrange("h t s -> t h s")).then_inc(s_ws, 16)
                for g in range(NA):
                    for j in range(4):
                        at = (4 * g + j) * BANK
                        act.dma_start(acc[32 * j:32 * j + NC, g, :],
                                      row(b_ada[0, at:at + BANK], NC)).then_inc(s_small, 16)
                act.dma_start(pw[:, :, :], pool_w[0].rearrange("g c d -> c g d")).then_inc(s_small, 16)
                act.dma_start(psc[:, :], pool_scale[0].rearrange("(g d) -> d g", g=NG),
                              allow_slow_non_contiguous=True).then_inc(s_small, 16)
                act.dma_start(bt[:, :], sgu_b[0].rearrange("h t -> t h"),
                              allow_slow_non_contiguous=True).then_inc(s_small, 16)
                act.dma_start(b0s[0:NS, :], sgu_b[0, :, 0:1].rearrange("h a -> a h").partition_broadcast(NS),
                              allow_slow_non_contiguous=True).then_inc(s_small, 16)
                act.dma_start(w0s[0:NS, :], sgu_w[0, :, 0, 0:1].rearrange("h a -> a h").partition_broadcast(NS),
                              allow_slow_non_contiguous=True).then_inc(s_small, 16)
                act.dma_start(sg_bc[:, :], row(sgu_norm_g[0])).then_inc(s_small, 16)
                act.dma_start(rw[:, :, 0:NRG], router_g_w[0].rearrange("(k p) n -> p k n", p=P)).then_inc(s_small, 16)
                act.dma_start(rw[:, :, NRG:NR], router_e_w[0].rearrange("(k p) n -> p k n", p=P)).then_inc(s_small, 16)
                act.dma_start(rb[:, 0:NRG], row(router_g_b[0])).then_inc(s_small, 16)
                act.dma_start(rb[:, NRG:NR], row(router_e_b[0])).then_inc(s_small, 16)
                act.wait_ge(s_c, 32)
                nc.scalar.activation(c_raw[:, :], c_raw[:, :], ACT.Silu).then_inc(s_cs, 1)
                act.wait_ge(s_cTp, 1)
                nc.scalar.copy(cT[:, :, :], bank[0][:, 0:KD * NC].rearrange("p (k c) -> p k c", c=NC)).then_inc(s_cT, 1)
                act.wait_ge(s_wsp, 1)
                nc.scalar.copy(wsT[:, :, :], bank[1].rearrange("p (h s) -> p h s", s=P)).then_inc(s_wsT, 1)

            @block.gpsimd
            def _(pool):
                ch = Chain(pool, s_chp)
                ch.add(nc.gpsimd.memset(ident[:, :], 0.0))
                ch.add(nc.gpsimd.memset(before[:, :], 1.0))
                ch.add(nc.gpsimd.memset(ones[:, :], 1.0))
                for g, w in enumerate(WINDOWS):
                    ch.add(nc.gpsimd.memset(band[:, g, :], 1.0))
                    ch.add(nc.gpsimd.memset(bandp[:, g, :], 1.0 / w))
                ch.add(nc.gpsimd.iota(iota_i[:, :], pattern=[[1, P]], base=0, channel_multiplier=0))
                ch.add(nc.gpsimd.memset(p_sb[1][:, :], 0.0))
                ch.add(nc.gpsimd.memset(picked[:, NT, :, :], 0.0))
                ch.add(nc.gpsimd.memset(rank[:, NT, :], 0.0))
                ch.add(nc.gpsimd.memset(tops[:, NT, :, :], 0.0))
                ch.add(nc.gpsimd.memset(top[:, :, :], -BIG))
                ch.add(nc.gpsimd.memset(seen[:, :], 0.0))
                ch.add(nc.gpsimd.memset(seen_b[:, :], 0.0))
                ch.add(nc.gpsimd.memset(zrow[:, :], 0.0))
                ch.add(nc.gpsimd.memset(eps[:, :], LN_EPS))
                ch.wait()
                ch.add(nc.gpsimd.affine_select(out=ident[:, :], in_=ident[:, :], compare_op=ALU.not_equal, fill=1.0,
                                               base=0, pattern=[[-1, P]], channel_multiplier=1))
                ch.add(nc.gpsimd.affine_select(out=before[:, :], in_=before[:, :], compare_op=ALU.is_gt, fill=0.0,
                                               base=0, pattern=[[1, P]], channel_multiplier=-1))
                for g, w in enumerate(WINDOWS):
                    ch.add(nc.gpsimd.affine_select(out=bandp[:, g, :], in_=bandp[:, g, :], compare_op=ALU.is_ge,
                                                   fill=0.0, base=w - 1 - P, pattern=[[-1, P]], channel_multiplier=1))
                    ch.link(nc.gpsimd.affine_select(out=band[:, g, :], in_=band[:, g, :], compare_op=ALU.is_ge,
                                                    fill=0.0, base=0, pattern=[[1, P]], channel_multiplier=-1))
                    ch.add(nc.gpsimd.affine_select(out=band[:, g, :], in_=band[:, g, :], compare_op=ALU.is_ge,
                                                   fill=0.0, base=w - 1, pattern=[[-1, P]], channel_multiplier=1))
                ch.wait()
                pool.sem_inc(s_const, 1)
                pool.wait_ge(s_wsT, 1)
                nc.gpsimd.affine_select(out=wsT[:, :, :], in_=wsT[:, :, :], compare_op=ALU.is_ge, fill=0.0,
                                        base=0, pattern=[[0, NH], [1, P]], channel_multiplier=-1).then_inc(s_const, 1)
                pool.wait_ge(s_const, 2)
                ch.restart()

            @block.vector
            def _(dve):
                ch = Chain(dve, s_chv)
                dve.wait_ge(s_const, 1)
                ch.link(nc.vector.tensor_copy(iota[:, :], iota_i[:, :]))
                for g, w in enumerate(WINDOWS):
                    ch.link(nc.vector.tensor_scalar(invc[:, :], iota[:, :], 1.0, float(w), ALU.add, ALU.min))
                    ch.link(nc.vector.reciprocal(invc[:, :], invc[:, :]))
                    ch.link(nc.vector.tensor_tensor(band0[:, g, :], band[:, g, :], invc[:, :], ALU.mult))
                    ch.add(nc.vector.tensor_tensor(band0[:, g, :], band0[:, g, :], ident[:, :], ALU.subtract))
                    ch.add(nc.vector.scalar_tensor_tensor(band[:, g, :], band[:, g, :], 1.0 / w, ident[:, :],
                                                          ALU.mult, ALU.subtract))
                dve.wait_ge(s_small, 16 * (4 * NA + 10))
                dve.wait_ge(s_adap, 1)
                for j in range(4):
                    q = slice(32 * j, 32 * j + NC)
                    ch.add(nc.vector.tensor_tensor(acc[q, 0, :], bank[2][q, :], acc[q, 0, :], ALU.add))
                ch.restart()
                dve.sem_inc(s_modr, 1)

            @block.tensor
            def _(pe):
                pe.wait_ge(s_const, 1)
                pe.wait_ge(s_ws, 16)
                for h in range(NH):
                    ins = nc.tensor.transpose(bank[1][:, h * P:(h + 1) * P], wst_raw[:, h, :], ident[:, :])
                ins.then_inc(s_wsp, 1)
                pe.wait_ge(s_cs, 1)
                for k in range(KD):
                    ins = nc.tensor.transpose(bank[0][:, k * NC:(k + 1) * NC], c_raw[:, k * P:(k + 1) * P],
                                              ident[0:NC, 0:NC])
                ins.then_inc(s_cTp, 1)
                pe.wait_ge(s_cT, 1)
                for k in range(KD):
                    pe.wait_ge(s_ada0[k], 16)
                    for j in range(4):
                        ins = nc.tensor.matmul(bank[2][32 * j:32 * j + NC, :], cT[:, k, :],
                                               ada0[:, k, j * BANK:(j + 1) * BANK], start=(k == 0), stop=(k == KD - 1))
                ins.then_inc(s_adap, 1)

        s_sc1 = sem("scale1_loaded")
        s_sc1r = sem("scale1_ready")
        s_x = [sem(f"x_loaded{i}") for i in range(2)]
        s_adal = [sem(f"ada_loaded{i}") for i in range(2)]
        s_ck = sem("c_tile_ready")
        s_h = sem("h_ready")
        s_hTp = sem("hT_in_psum")
        s_hT = sem("hT_ready")
        s_pp = sem("p_in_psum")
        s_up = sem("u_in_psum")
        s_vp = sem("v_in_psum")
        s_p = sem("p_saved")
        s_u = sem("u_saved")
        s_bd = sem("band_done")
        s_dT = sem("dT_saved")
        s_am = sem("pool_mm_done")
        s_a = sem("a_saved")
        s_var = sem("v_var_ready")
        s_std = sem("v_std_ready")
        s_vn = sem("vn_ready")
        s_z = sem("z_done")
        s_g = sem("g_ready")
        s_gTp = sem("gT_in_psum")
        s_gT = sem("gT_saved")
        s_ad = sem("ada_unit_done")
        s_aa = sem("ada_unit_added")
        s_ps = sem("pool_state_stored")
        s_hist = sem("history_loaded")
        s_hs = sem("history_used")
        s_vs = sem("sgu_v_stored")
        s_sc1s = sem("sample_scale1_loaded")
        s_sc1sr = sem("sample_scale1_ready")
        s_smu = sem("sample_g_ready")
        s_zf = sem("spare_blocks_zeroed")

        xp = x_prompt[0]

        with nc.Block() as block:
            @block.gpsimd
            def _(pool):
                with pool.Fori(0, (NB - NE) // 2) as i:
                    pool.dma_start(ye_d[ds((i * 2 + NE) * P, P), :], zrow[:, :]).then_inc(s_zf, 16)
                    pool.dma_start(ye_d[ds((i * 2 + NE + 1) * P, P), :], zrow[:, :]).then_inc(s_zf, 16)
                    pool.wait_ge(s_zf, i * 32 + 32)
                    pool.wait_ge(s_h, 1)

            @block.sync
            def _(sp):
                sp.dma_start(sh1[:, :], mod_row(0)).then_inc(s_sc1, 16)
                sp.dma_start(sc1[:, :], mod_row(1)).then_inc(s_sc1, 16)
                for t in range(2):
                    sp.dma_start(x_t[t][:, :], xp[t * P:(t + 1) * P, :]).then_inc(s_x[t], 16)
                for t in range(2):
                    sp.dma_start(ada_st[t][:, :], w_ada_v[0, 1 + t]).then_inc(s_adal[t], 16)

                with sp.Fori(0, NT // 2 - 1) as i:
                    for b in range(2):
                        sp.wait_ge(s_h, i * 2 + b + 1)
                        sp.dma_start(x_t[b][:, :], xp[ds((i * 2 + b + 2) * P, P), :]).then_inc(s_x[b], 16)
                        sp.wait_ge(s_ad, i * 2 + b + 1)
                        sp.dma_start(ada_st[b][:, :], w_ada_v[ds(i + 1, 1), 1 + b].rearrange("a p n -> p (a n)")).then_inc(s_adal[b], 16)
                sp.wait_ge(s_h, NT - 1)
                sp.dma_start(x_t[0][0:NS, :], x_sample[:, 0, :]).then_inc(s_x[0], 16)
                sp.wait_ge(s_h, NT)
                sp.dma_start(sh1[0:NS, :], mod_d[0:NS, 0:D]).then_inc(s_sc1s, 16)
                sp.dma_start(sc1[0:NS, :], mod_d[0:NS, D:2 * D]).then_inc(s_sc1s, 16)
                sp.wait_ge(s_ad, NT)
                for g in range(NG):
                    sp.dma_start(hist[g][:, :, :], state_pool[0, :, BUF - hist_len[g]:BUF, g * P:(g + 1) * P]).then_inc(s_hist, 16)
                sp.dma_start(pool_sample[0, :, 0:BUF - 1, :], state_pool[0, :, 1:BUF, :]).then_inc(s_ps, 16)
                sp.wait_ge(s_p, NT)
                sp.dma_start(pool_prompt[0, 0], p_sb[(NT - 1) % 2][P - BUF:P, :]).then_inc(s_ps, 16)
                sp.wait_ge(s_p, NT + 1)
                sp.dma_start(pool_sample[0, :, BUF - 1, :], p_sb[NT % 2][0:NS, :]).then_inc(s_ps, 16)
                sp.wait_ge(s_vn, NT + 1)
                sp.dma_start(sgu_v[0, :, 0, :], vn[0:NS, :]).then_inc(s_vs, 16)
                sp.wait_ge(s_aa, NT)
                for g in range(1, NA):
                    for j in range(4):
                        at = (4 * g + j) * BANK
                        sp.dma_start(mod_d[:, at:at + BANK], acc[32 * j:32 * j + NC, g, :]).then_inc(s_mods, 16)
                sp.wait_ge(s_mods, 64 * NA)
                sp.wait_ge(s_ps, 48)
                sp.wait_ge(s_vs, 16)

            @block.tensor
            def _(pe):
                def h_transposes(t, b, rows=P):
                    pe.wait_ge(s_h, t + 1)
                    if not (isinstance(t, int) and t == 0):
                        pe.wait_ge(s_hT, t)
                    for k in range(KD):
                        ins = nc.tensor.transpose(ps2[0][:, k * P:k * P + rows], h_t[0:rows, k * P:(k + 1) * P],
                                                  ident[0:rows, 0:rows])
                    ins.then_inc(s_hTp, 1)

                def project(t, b, part, out, signal, free, rows=P):
                    if free is not None:
                        pe.wait_ge(free, t)
                    for k in range(KD):
                        ins = nc.tensor.matmul(out[0:rows, :], hT[b][:, k, 0:rows],
                                               w_in_sb[:, k, part * BANK:(part + 1) * BANK],
                                               start=(k == 0), stop=(k == KD - 1))
                    ins.then_inc(signal, 1)

                def bands(t, b, mats):
                    pe.wait_ge(s_p, t + 1)
                    if not (isinstance(t, int) and t == 0):
                        pe.wait_ge(s_gT, t)
                    for g in range(NG):
                        q = slice(g * P, (g + 1) * P)
                        nc.tensor.matmul(bank[5][:, q], p_sb[b][:, q], mats[:, g, :], start=True, stop=False)
                        ins = nc.tensor.matmul(bank[5][:, q], p_sb[1 - b][:, q], bandp[:, g, :], start=False, stop=True)
                    ins.then_inc(s_bd, 1)

                def pool_linear(t):
                    pe.wait_ge(s_dT, t + 1)
                    if not (isinstance(t, int) and t == 0):
                        pe.wait_ge(s_a, t)
                    for g in range(NG):
                        ins = nc.tensor.matmul(bank[7][:, g * P:(g + 1) * P], pw[:, g, :], dT[:, g, :],
                                               start=True, stop=True)
                    ins.then_inc(s_am, 1)

                def gating(t):
                    pe.wait_ge(s_vn, t + 1)
                    pe.wait_ge(s_aa, t + 1)
                    for h in range(NH):
                        q = slice(h * P, (h + 1) * P)
                        ins = nc.tensor.matmul(bank[6][:, q], wsT[:, h, :], vn[:, q], start=True, stop=True)
                    ins.then_inc(s_z, 1)

                def g_transposes(t):
                    pe.wait_ge(s_g, t + 1)
                    pe.wait_ge(s_dT, t + 1)
                    for h in range(NH):
                        ins = nc.tensor.transpose(bank[5][:, h * P:(h + 1) * P], g_sb[:, h * P:(h + 1) * P], ident[:, :])
                    ins.then_inc(s_gTp, 1)

                def ada_pair_unit(i, b):
                    pe.wait_ge(s_adal[b], i * 16 + 16)
                    for j in range(4):
                        ins = nc.tensor.matmul(bank[6][32 * j:32 * j + NC, :], cT_k[:, :],
                                               ada_st[b][:, j * BANK:(j + 1) * BANK], start=True, stop=True)
                    ins.then_inc(s_ad, 1)

                def tile(t, b, i):
                    pe.wait_ge(s_hT, t + 1)
                    lead = isinstance(t, int) and t == 0
                    project(t, b, 0, bank[2], s_pp, None if lead else s_p)
                    if not lead:
                        bands(t - 1, 1 - b, band0 if isinstance(t, int) and t == 1 else band)
                    project(t, b, 1, bank[3], s_up, None if lead else s_u)
                    if not lead:
                        pool_linear(t - 1)
                        gating(t - 1)
                    project(t, b, 2, bank[4], s_vp, None if lead else s_vn)
                    if not lead:
                        g_transposes(t - 1)
                    if not (isinstance(t, int) and t == NT - 1):
                        h_transposes(t + 1, 1 - b)
                    if not lead:
                        pe.wait_ge(s_g, t)
                    pe.wait_ge(s_ck, t + 1)
                    ada_pair_unit(i, b)

                pe.wait_ge(s_win, 16)
                h_transposes(0, 0)
                tile(0, 0, 0)
                tile(1, 1, 0)
                with pe.Fori(1, NT // 2 - 1) as i:
                    for b in range(2):
                        tile(i * 2 + b, b, i)
                tile(NT - 2, 0, NT // 2 - 1)
                tile(NT - 1, 1, NT // 2 - 1)
                bands(NT - 1, 1, band)
                h_transposes(NT, 0, NS)
                pool_linear(NT - 1)
                gating(NT - 1)
                g_transposes(NT - 1)
                pe.wait_ge(s_hT, NT + 1)
                project(NT, 0, 0, bank[2], s_pp, s_p, NS)
                project(NT, 0, 1, bank[3], s_up, s_u, NS)
                project(NT, 0, 2, bank[4], s_vp, s_vn, NS)
                pe.wait_ge(s_gT, NT)
                pe.wait_ge(s_hs, 1)
                for g in range(NG):
                    ins = nc.tensor.transpose(bank[5][:, g * NS:(g + 1) * NS], g_sb[0:NS, g * P:(g + 1) * P],
                                              ident[0:NS, 0:NS])
                ins.then_inc(s_bd, 1)
                pe.wait_ge(s_dT, NT + 1)
                pe.wait_ge(s_a, NT)
                for g in range(NG):
                    ins = nc.tensor.matmul(bank[7][:, g * NS:(g + 1) * NS], pw[:, g, :], dT[:, g, 0:NS],
                                           start=True, stop=True)
                ins.then_inc(s_am, 1)
                pe.wait_ge(s_smu, 1)
                for h in range(NH):
                    ins = nc.tensor.transpose(bank[5][:, h * NS:(h + 1) * NS], u_sb[0:NS, h * P:(h + 1) * P],
                                              ident[0:NS, 0:NS])
                ins.then_inc(s_gTp, 1)

            @block.vector
            def _(dve):
                ch = Chain(dve, s_chv)

                def modulate(t, b, rows=P):
                    dve.wait_ge(s_x[b], x_count(t, b))
                    if not (isinstance(t, int) and t == 0):
                        dve.wait_ge(s_hTp, t)
                    ch.link(nc.vector.tensor_tensor(h_t[0:rows, :], x_t[b][0:rows, :], sc1[0:rows, :], ALU.mult))
                    nc.vector.tensor_tensor(h_t[0:rows, :], h_t[0:rows, :], sh1[0:rows, :], ALU.add).then_inc(s_h, 1)

                def x_count(t, b):
                    return (t - b) * 8 + 16

                def save_dT(t):
                    dve.wait_ge(s_bd, t + 1)
                    if not (isinstance(t, int) and t == 0):
                        dve.wait_ge(s_am, t)
                    nc.vector.tensor_copy(dT[:, :, :], bank[5].rearrange("p (g t) -> p g t", g=NG)).then_inc(s_dT, 1)

                def gate(t):
                    dve.wait_ge(s_z, t + 1)
                    dve.wait_ge(s_u, t + 1)
                    if not (isinstance(t, int) and t == 0):
                        dve.wait_ge(s_gTp, t)
                    for h in range(NH):
                        q = slice(h * P, (h + 1) * P)
                        ch.add(nc.vector.scalar_tensor_tensor(g_sb[:, q], bank[6][:, q], bt[:, h:h + 1], u_sb[:, q],
                                                              ALU.add, ALU.mult))
                    ch.wait()
                    dve.sem_inc(s_g, 1)

                def add_unit(t, b):
                    dve.wait_ge(s_ad, t + 1)
                    for j in range(4):
                        q = slice(32 * j, 32 * j + NC)
                        ch.add(nc.vector.tensor_tensor(acc[q, 1 + b, :], bank[6][q, :], acc[q, 1 + b, :], ALU.add))
                    ch.wait()
                    dve.sem_inc(s_aa, 1)

                def copy_c(i):
                    nc.vector.tensor_scalar(cT_k[:, :], cT[:, ds(i, 1), :].rearrange("p a c -> p (a c)"), 1.0, None,
                                            ALU.mult).then_inc(s_ck, 1)

                def head_norm(t, rows=P):
                    dve.wait_ge(s_vp, t + 1)
                    if not (isinstance(t, int) and t == 0):
                        dve.wait_ge(s_z, t)
                    v = bank[4]
                    for h in range(NH):
                        ch.add(nc.vector.bn_stats(vstat[0:rows, h, :], v[0:rows, h * P:(h + 1) * P]))
                    ch.wait()
                    for h in range(NH):
                        ch.add(nc.vector.bn_aggr(vmv[0:rows, h, :], vstat[0:rows, h, :]))
                    ch.wait()
                    dve.sem_inc(s_var, 1)
                    dve.wait_ge(s_std, t + 1)
                    ch.link(nc.vector.reciprocal(vinv[0:rows, :], vstd[0:rows, :]))
                    for h in range(NH):
                        q = slice(h * P, (h + 1) * P)
                        ch.add(nc.vector.tensor_scalar(vn[0:rows, q], v[0:rows, q], vmv[0:rows, h, 0:1],
                                                       vinv[0:rows, h:h + 1], ALU.subtract, ALU.mult))
                    ch.wait()
                    nc.vector.tensor_tensor(vn[0:rows, :], vn[0:rows, :], sg_bc[0:rows, :], ALU.mult).then_inc(s_vn, 1)

                def tile(t, b, i):
                    lead = isinstance(t, int) and t == 0
                    if not lead:
                        save_dT(t - 1)
                        dve.wait_ge(s_ad, t)
                    copy_c(i)
                    if not (isinstance(t, int) and t == NT - 1):
                        modulate(t + 1, 1 - b)
                    if not lead:
                        gate(t - 1)
                    add_unit(t, b)
                    head_norm(t)
                    ch.restart()

                dve.wait_ge(s_sc1, 32)
                nc.vector.tensor_scalar_add(sc1[:, :], sc1[:, :], 1.0).then_inc(s_sc1r, 1)
                dve.wait_ge(s_sc1r, 1)
                modulate(0, 0)
                tile(0, 0, 0)
                tile(1, 1, 0)
                with dve.Fori(1, NT // 2 - 1) as i:
                    for b in range(2):
                        tile(i * 2 + b, b, i)
                tile(NT - 2, 0, NT // 2 - 1)
                tile(NT - 1, 1, NT // 2 - 1)
                save_dT(NT - 1)
                dve.wait_ge(s_sc1s, 32)
                nc.vector.tensor_scalar_add(sc1[0:NS, :], sc1[0:NS, :], 1.0).then_inc(s_sc1r, 1)
                dve.wait_ge(s_sc1r, 2)
                modulate(NT, 0, NS)
                gate(NT - 1)
                dve.wait_ge(s_hist, 16 * NG)
                dve.wait_ge(s_gTp, NT)
                for g in range(NG):
                    ch.add(nc.vector.tensor_reduce(g_sb[0:NS, g * P:(g + 1) * P],
                                                   hist[g][:, :, :].rearrange("b w c -> b c w"), AX_X, ALU.add))
                ch.wait()
                dve.wait_ge(s_p, NT + 1)
                p_s = p_sb[NT % 2]
                ch.link(nc.vector.tensor_tensor(g_sb[0:NS, :], g_sb[0:NS, :], p_s[0:NS, :], ALU.add))
                for g, w in enumerate(WINDOWS):
                    q = slice(g * P, (g + 1) * P)
                    ch.add(nc.vector.scalar_tensor_tensor(g_sb[0:NS, q], g_sb[0:NS, q], 1.0 / w, p_s[0:NS, q],
                                                          ALU.mult, ALU.subtract))
                ch.wait()
                dve.sem_inc(s_hs, 1)
                dve.wait_ge(s_bd, NT + 1)
                dve.wait_ge(s_am, NT)
                nc.vector.tensor_copy(dT[:, :, 0:NS], bank[5][:, 0:NG * NS].rearrange("p (g t) -> p g t", g=NG)).then_inc(s_dT, 1)
                head_norm(NT, NS)
                dve.wait_ge(s_vn, NT + 1)
                dve.wait_ge(s_u, NT + 1)
                for h in range(NH):
                    q = slice(h * P, (h + 1) * P)
                    ch.link(nc.vector.tensor_scalar(h_t[0:NS, q], vn[0:NS, q], w0s[0:NS, h:h + 1], b0s[0:NS, h:h + 1],
                                                    ALU.mult, ALU.add))
                    ch.add(nc.vector.tensor_tensor(u_sb[0:NS, q], u_sb[0:NS, q], h_t[0:NS, q], ALU.mult))
                ch.wait()
                dve.sem_inc(s_smu, 1)
                ch.restart()

            @block.scalar
            def _(act):
                ch = Chain(act, s_cha)

                def save_p(t, b, rows=P):
                    act.wait_ge(s_pp, t + 1)
                    if not (isinstance(t, int) and t == 0):
                        act.wait_ge(s_bd, t)
                    nc.scalar.copy(p_sb[b][0:rows, :], bank[2][0:rows, :]).then_inc(s_p, 1)

                def save_u(t, rows=P):
                    act.wait_ge(s_up, t + 1)
                    if not (isinstance(t, int) and t == 0):
                        act.wait_ge(s_g, t)
                    nc.scalar.copy(u_sb[0:rows, :], bank[3][0:rows, :]).then_inc(s_u, 1)

                def save_a(t, n=P):
                    act.wait_ge(s_am, t + 1)
                    for g in range(NG):
                        if isinstance(t, int) and t == NT:
                            out = mixT_s[:, g, :]
                        else:
                            out = mixT[:, ds(t, 1), g, :].rearrange("p a c -> p (a c)")
                        ch.add(nc.scalar.activation(out, bank[7][:, g * n:(g + 1) * n], ACT.Copy, scale=psc[:, g:g + 1]))
                    ch.wait()
                    act.sem_inc(s_a, 1)

                def save_gT(t):
                    act.wait_ge(s_gTp, t + 1)
                    nc.scalar.copy(mixT[:, ds(t, 1), NG:NG + NH, :].rearrange("p a h c -> p (a h) c"),
                                   bank[5].rearrange("p (h c) -> p h c", h=NH)).then_inc(s_gT, 1)

                def save_hT(t, b, rows=P):
                    act.wait_ge(s_hTp, t + 1)
                    if not (isinstance(t, int) and t < 2):
                        act.wait_ge(s_vp, t - 1)
                    nc.scalar.copy(hT[b][:, :, 0:rows],
                                   ps2[0][:, :].rearrange("p (k t) -> p k t", k=KD)[:, :, 0:rows]).then_inc(s_hT, 1)

                def std_v(t, rows=P):
                    act.wait_ge(s_var, t + 1)
                    nc.scalar.activation(vstd[0:rows, :], vmv[0:rows, :, 1], ACT.Sqrt, bias=eps[0:rows, :]).then_inc(s_std, 1)

                def tile(t, b):
                    lead = isinstance(t, int) and t == 0
                    save_p(t, b)
                    save_u(t)
                    if not lead:
                        save_a(t - 1)
                        save_gT(t - 1)
                    if not (isinstance(t, int) and t == NT - 1):
                        save_hT(t + 1, 1 - b)
                    std_v(t)
                    ch.restart()

                save_hT(0, 0)
                tile(0, 0)
                tile(1, 1)
                with act.Fori(1, NT // 2 - 1) as i:
                    for b in range(2):
                        tile(i * 2 + b, b)
                tile(NT - 2, 0)
                tile(NT - 1, 1)
                save_hT(NT, 0, NS)
                save_a(NT - 1)
                save_gT(NT - 1)
                save_p(NT, 0, NS)
                save_u(NT, NS)
                std_v(NT, NS)
                save_a(NT, NS)
                act.wait_ge(s_gTp, NT + 1)
                nc.scalar.copy(mixT_s[:, NG:NG + NH, :],
                               bank[5][:, 0:NH * NS].rearrange("p (h c) -> p h c", h=NH)).then_inc(s_gT, 1)
                act.wait_ge(s_gT, NT + 1)
                ch.restart()

        s_bc = sem("norm_rows_loaded")
        s_wo = sem("w_out_loaded")
        s_one = sem("scale_rows_ready")
        s_xr = [sem(f"x_reloaded{i}") for i in range(2)]
        s_mix = sem("mix_in_psum")
        s_mixr = sem("mix_read")
        s_xu = sem("x_used")
        s_v1 = sem("x1_var_ready")
        s_s1 = sem("x1_std_ready")
        s_x1 = sem("x1_ready")
        s_x1s = sem("x1_stored")
        s_h2 = sem("h2_ready")
        s_h2s = [sem(f"h2_stored{i}") for i in range(2)]
        s_h2p = sem("h2T_in_psum")
        s_h2T = sem("h2T_ready")
        s_rt = sem("router_in_psum")
        s_lgT = sem("logitsT_ready")
        s_lg = sem("logits_in_psum")
        s_lr = sem("logits_read")
        s_m = sem("mask_ready")
        s_rk = sem("rank_in_psum")
        s_rkr = sem("rank_read")
        s_bcs = sem("sample_norm_rows_loaded")
        s_lz = sem("logitsT_zeroed")
        s_mc = sem("mix_placed")
        s_raw = [sem(f"raw_units_loaded{i}") for i in range(NU // 2)]

        def load_units(eng, e, pair):
            k = 2 * pair
            if k < GU:
                for half, w_v in enumerate((gate_v, up_v)):
                    eng.dma_start(wraw[:, k:k + 2, half * FE:(half + 1) * FE],
                                  w_v[ds(e, 1), :, k:k + 2, :].rearrange("a p k n -> p (a k) n")).then_inc(s_raw[pair], 16)
            else:
                k -= GU
                eng.dma_start(wraw[:, GU + k:GU + k + 2, :],
                              down_v[ds(e, 1), :, k:k + 2, :].rearrange("a p k n -> p (a k) n")).then_inc(s_raw[pair], 16)

        def raw_count(pair, e):
            return e * 32 + 32 if 2 * pair < GU else e * 16 + 16

        EARLY = 2

        with nc.Block() as block:
            @block.sync
            def _(sp):
                sp.dma_start(w_out_sb[:, :, :], w_out_v).then_inc(s_wo, 16)
                for t in range(2):
                    sp.dma_start(x_r[t][:, :], xp[t * P:(t + 1) * P, :]).then_inc(s_xr[t], 16)
                for dst, j in ((g1, 2), (sh2, 3), (sc2, 4)):
                    sp.dma_start(dst[:, :], mod_row(j)).then_inc(s_bc, 16)
                sp.dma_start(lg1[:, :], row(ln1_g[0])).then_inc(s_bc, 16)
                sp.dma_start(lb1[:, :], row(ln1_b[0])).then_inc(s_bc, 16)
                for pair in range(EARLY):
                    load_units(sp, 0, pair)

                def store(t, b):
                    sp.wait_ge(s_x1, t + 1)
                    sp.dma_start(x1_d[ds(t * P, P), :], x1[:, :]).then_inc(s_x1s, 16)
                    sp.wait_ge(s_h2, t + 1)
                    sp.dma_start(h2_d[ds(t * P, P), :], h2[b][:, :]).then_inc(s_h2s[b], 16)

                with sp.Fori(0, NT // 2 - 1) as i:
                    for b in range(2):
                        t = i * 2 + b
                        sp.wait_ge(s_xu, t + 1)
                        sp.dma_start(x_r[b][:, :], xp[ds((t + 2) * P, P), :]).then_inc(s_xr[b], 16)
                        store(t, b)
                sp.wait_ge(s_xu, NT - 1)
                sp.dma_start(x_r[0][0:NS, :], x_sample[:, 0, :]).then_inc(s_xr[0], 16)
                store(NT - 2, 0)
                store(NT - 1, 1)
                for dst, j in ((g1, 2), (sh2, 3), (sc2, 4)):
                    sp.dma_start(dst[0:NS, :], mod_d[0:NS, j * D:(j + 1) * D]).then_inc(s_bcs, 16)
                sp.wait_ge(s_x1, NT + 1)
                sp.dma_start(x1_d[NT * P:NT * P + NS, :], x1[0:NS, :]).then_inc(s_x1s, 16)
                sp.wait_ge(s_h2, NT + 1)
                sp.dma_start(h2_d[NT * P:NT * P + NS, :], h2[0][0:NS, :]).then_inc(s_h2s[0], 16)
                sp.wait_ge(s_x1s, 16 * NTT)
                sp.wait_ge(s_h2s[0], 16 * (NT // 2 + 1))
                sp.wait_ge(s_h2s[1], 16 * (NT // 2))

            @block.tensor
            def _(pe):
                def project(t, b, half, rows=P):
                    if half == 0 and not (isinstance(t, int) and t < 2):
                        pe.wait_ge(s_mixr, t - 1)
                    for k in range(KD):
                        if isinstance(t, int) and t == NT:
                            m = mixT_s[:, k, :]
                        else:
                            m = mix_cur[b][:, k, :]
                        ins = nc.tensor.matmul(ps2[b][0:rows, half * BANK:(half + 1) * BANK], m,
                                               w_out_sb[:, k, half * BANK:(half + 1) * BANK],
                                               start=(k == 0), stop=(k == KD - 1))
                    if half == 1:
                        ins.then_inc(s_mix, 1)

                def h2_transposes(t, b, rows=P):
                    pe.wait_ge(s_h2, t + 1)
                    if not (isinstance(t, int) and t == 0):
                        pe.wait_ge(s_h2T, t)
                    for k in range(KD):
                        ins = nc.tensor.transpose(ps2[2][:, k * P:k * P + rows], h2[b][0:rows, k * P:(k + 1) * P],
                                                  ident[0:rows, 0:rows])
                    ins.then_inc(s_h2p, 1)

                def router(t, rows=P):
                    pe.wait_ge(s_h2T, t + 1)
                    if not (isinstance(t, int) and t == 0):
                        pe.wait_ge(s_lgT, t)
                    for k in range(KD):
                        ins = nc.tensor.matmul(bank[6][0:NR, 0:rows], rw[:, k, :], h2T[:, k, 0:rows],
                                               start=(k == 0), stop=(k == KD - 1))
                    ins.then_inc(s_rt, 1)

                def logits(t, rows=P):
                    pe.wait_ge(s_lgT, t + 1)
                    if not (isinstance(t, int) and t == 0):
                        pe.wait_ge(s_rkr, t)
                    nc.tensor.transpose(bank[7][0:rows, 0:P], lgT[:, 0:rows], ident[:, :]).then_inc(s_lg, 1)

                def ranks(t, rows=P):
                    pe.wait_ge(s_m, t + 1)
                    q = bank[7][0:rows, P:P + NE]
                    nc.tensor.matmul(q, before[0:rows, 0:rows], m_b[0:rows, :], start=True, stop=False)
                    nc.tensor.matmul(q, ones[:, 0:rows], seen_b[:, :], start=False, stop=True).then_inc(s_rk, 1)

                def tile(t, b):
                    at = isinstance(t, int)
                    if not (at and t >= NT):
                        pe.wait_ge(s_mc, t + 1)
                        project(t, b, 0)
                    elif t == NT:
                        project(t, b, 0, NS)
                    if not (at and (t < 1 or t > NTT)):
                        h2_transposes(t - 1, 1 - b, NS if at and t - 1 == NT else P)
                    if not (at and t < 2):
                        logits(t - 2, NS if at and t - 2 == NT else P)
                    if not (at and t >= NT):
                        project(t, b, 1)
                    elif t == NT:
                        project(t, b, 1, NS)
                    if not (at and (t < 1 or t > NTT)):
                        router(t - 1, NS if at and t - 1 == NT else P)
                    if not (at and t < 2):
                        ranks(t - 2, NS if at and t - 2 == NT else P)

                pe.wait_ge(s_wo, 16)
                tile(0, 0)
                tile(1, 1)
                with pe.Fori(1, NT // 2) as i:
                    for b in range(2):
                        tile(i * 2 + b, b)
                tile(NT, 0)
                tile(NT + 1, 1)
                tile(NT + 2, 0)

            @block.gpsimd
            def _(pool):
                def place(t, b):
                    if not (isinstance(t, int) and t < 2):
                        pool.wait_ge(s_mix, t - 1)
                    nc.gpsimd.tensor_copy(mix_cur[b][:, :, :],
                                          mixT[:, ds(t, 1), :, :].rearrange("p a k c -> p (a k) c")).then_inc(s_mc, 1)
                nc.gpsimd.memset(lgT[:, :], 0.0).then_inc(s_lz, 1)
                place(0, 0)
                place(1, 1)
                with pool.Fori(1, NT // 2) as i:
                    for b in range(2):
                        place(i * 2 + b, b)

            @block.vector
            def _(dve):
                ch = Chain(dve, s_chv)

                def norm(t, b, rows=P):
                    q = slice(0, rows)
                    dve.wait_ge(s_xr[b], (t - b) * 8 + 16)
                    dve.wait_ge(s_mix, t + 1)
                    ins = nc.vector.tensor_tensor(t_r[q, :], ps2[b][q, :], g1[q, :], ALU.mult)
                    ch.link(ins)
                    dve.sem_inc(s_mixr, 1)
                    ch.link(nc.vector.scalar_tensor_tensor(t_r[q, :], x_r[b][q, :], ALPHA, t_r[q, :], ALU.mult, ALU.add))
                    dve.sem_inc(s_xu, 1)
                    for n in range(2):
                        ch.add(nc.vector.bn_stats(bst[q, n, :], t_r[q, n * BANK:(n + 1) * BANK]))
                    ch.wait()
                    nc.vector.bn_aggr(mv[q, :], bst[q, :, :].rearrange("p a s -> p (a s)")).then_inc(s_v1, 1)
                    dve.wait_ge(s_s1, t + 1)
                    ch.link(nc.vector.reciprocal(inv[q, :], std[q, :]))
                    ch.link(nc.vector.tensor_scalar(t_r[q, :], t_r[q, :], mv[q, 0:1], inv[q, 0:1], ALU.subtract, ALU.mult))
                    ch.link(nc.vector.tensor_tensor(t_r[q, :], t_r[q, :], lg1[q, :], ALU.mult))
                    if not (isinstance(t, int) and t == 0):
                        dve.wait_ge(s_x1s, t * 16)
                    nc.vector.tensor_tensor(x1[q, :], t_r[q, :], lb1[q, :], ALU.add).then_inc(s_x1, 1)
                    dve.wait_ge(s_x1, t + 1)
                    if not (isinstance(t, int) and t < 2):
                        dve.wait_ge(s_h2s[b], (t - b) * 8)
                        dve.wait_ge(s_h2p, t - 1)
                    ch.link(nc.vector.tensor_tensor(h2[b][q, :], x1[q, :], sc2[q, :], ALU.mult))
                    nc.vector.tensor_tensor(h2[b][q, :], h2[b][q, :], sh2[q, :], ALU.add).then_inc(s_h2, 1)

                def route(t, rows=P):
                    q = slice(0, rows)
                    gl, gt, et = (top[q, n, :] for n in range(3))
                    dve.wait_ge(s_lg, t + 1)
                    ch.add(nc.vector.tensor_tensor(gl[:, 0:NRG], bank[7][q, 0:NRG], rb[q, 0:NRG], ALU.add))
                    ch.link(nc.vector.tensor_tensor(el[q, :], bank[7][q, NRG:NR], rb[q, NRG:NR], ALU.add))
                    ch.link(nc.vector.max(gt, gl))
                    ch.link(nc.vector.max_index(gidx[q, :], gt, gl))
                    ch.link(nc.vector.tensor_copy(gidf[q, :], gidx[q, 0:1]))
                    ch.link(nc.vector.tensor_scalar(gm[q, :], iota[q, 0:NRG], gidf[q, 0:1], -BIG, ALU.not_equal, ALU.mult))
                    ch.link(nc.vector.tensor_tensor(el[q, :].rearrange("p (g e) -> p g e", g=NRG),
                                                    el[q, :].rearrange("p (g e) -> p g e", g=NRG),
                                                    gm[q, :].unsqueeze(2).to_broadcast([rows, NRG, EPG]), ALU.add))
                    ch.link(nc.vector.max(et, el[q, :]))
                    ch.link(nc.vector.max_index(eidx[q, :], et, el[q, :]))
                    ch.add(nc.vector.tensor_copy(tops[q, ds(t, 1), :, :].rearrange("p a m n -> p (a m n)"),
                                                 top[q, :, :].rearrange("p m n -> p (m n)")))
                    ch.link(nc.vector.tensor_copy(eidf[q, :], eidx[q, 0:2]))
                    for n in range(2):
                        ch.add(nc.vector.tensor_scalar(pick(t, n, q), iota[q, 0:NE], eidf[q, n:n + 1], None, ALU.is_equal))
                    ch.wait()
                    nc.vector.tensor_tensor(m_b[q, :], pick(t, 0, q), pick(t, 1, q), ALU.add).then_inc(s_m, 1)
                    dve.wait_ge(s_rk, t + 1)
                    for n in range(2):
                        ch.add(nc.vector.tensor_tensor(rk[q, n, :], pick(t, n, q), bank[7][q, P:P + NE], ALU.mult))
                    ch.link(nc.vector.tensor_tensor(seen[q, :], seen[q, :], m_b[q, :], ALU.add))
                    ch.add(nc.vector.tensor_copy(seen_b[q, :], seen[q, :]))
                    ch.add(nc.vector.tensor_reduce(rank[q, ds(t, 1), :].rearrange("p a n -> p (a n)"), rk[q, :, :], AX_X, ALU.add))
                    ch.wait()
                    dve.sem_inc(s_rkr, 1)

                def pick(t, n, q):
                    return picked[q, ds(t, 1), n, :].rearrange("p a e -> p (a e)")

                def tile(t, b):
                    at = isinstance(t, int)
                    if not (at and t >= NT):
                        norm(t, b)
                    if at and t == NT:
                        norm(t, b, NS)
                    if not (at and t < 2):
                        route(t - 2, NS if at and t - 2 == NT else P)
                    ch.restart()

                dve.wait_ge(s_bc, 80)
                ch.add(nc.vector.tensor_scalar_add(g1[:, :], g1[:, :], 1.0))
                ch.add(nc.vector.tensor_scalar_add(sc2[:, :], sc2[:, :], 1.0))
                ch.wait()
                tile(0, 0)
                tile(1, 1)
                with dve.Fori(1, NT // 2) as i:
                    for b in range(2):
                        tile(i * 2 + b, b)
                dve.wait_ge(s_bcs, 48)
                ch.add(nc.vector.tensor_scalar_add(g1[0:NS, :], g1[0:NS, :], 1.0))
                ch.add(nc.vector.tensor_scalar_add(sc2[0:NS, :], sc2[0:NS, :], 1.0))
                ch.wait()
                tile(NT, 0)
                tile(NT + 1, 1)
                tile(NT + 2, 0)

            @block.scalar
            def _(act):
                def save_h2T(t, rows=P):
                    act.wait_ge(s_h2p, t + 1)
                    if not (isinstance(t, int) and t == 0):
                        act.wait_ge(s_rt, t)
                    nc.scalar.copy(h2T[:, :, 0:rows],
                                   ps2[2][:, :].rearrange("p (k t) -> p k t", k=KD)[:, :, 0:rows]).then_inc(s_h2T, 1)

                def std_x(t, rows=P):
                    act.wait_ge(s_v1, t + 1)
                    nc.scalar.activation(std[0:rows, :], mv[0:rows, 1:2], ACT.Sqrt, bias=eps[0:rows, :]).then_inc(s_s1, 1)

                def save_lgT(t, rows=P):
                    act.wait_ge(s_rt, t + 1)
                    if not (isinstance(t, int) and t == 0):
                        act.wait_ge(s_lg, t)
                    nc.scalar.copy(lgT[0:NR, 0:rows], bank[6][0:NR, 0:rows]).then_inc(s_lgT, 1)

                def tile(t):
                    at = isinstance(t, int)
                    if not (at and (t < 1 or t > NTT)):
                        save_h2T(t - 1, NS if at and t - 1 == NT else P)
                        save_lgT(t - 1, NS if at and t - 1 == NT else P)
                    if not (at and t > NT):
                        std_x(t, NS if at and t == NT else P)

                act.wait_ge(s_lz, 1)
                tile(0)
                tile(1)
                with act.Fori(1, NT // 2) as i:
                    for b in range(2):
                        tile(i * 2 + b)
                tile(NT)
                tile(NT + 1)

        s_cnt = sem("counts_in_psum")
        s_oh = sem("one_hots_ready")
        s_tok = sem("slot_table_in_psum")
        s_tab = sem("tables_ready")
        s_exi = sem("exponents_ready")
        s_exo = sem("exponentials_ready")
        s_inval = sem("unused_marked")

        M = NTT * 2
        with nc.Block() as block:
            @block.tensor
            def _(pe):
                nc.tensor.matmul(bank[0][:, 0:NE], ones[:, :], seen_b[:, :], start=True, stop=True).then_inc(s_cnt, 1)
                pe.wait_ge(s_oh, 1)
                for m in range(M):
                    ins = nc.tensor.matmul(bank[1][:, 0:2 * NB], oh_lo[:, m, :], oh_hi[:, m, :, :].rearrange("p a b -> p (a b)"),
                                           start=(m == 0), stop=(m == M - 1))
                ins.then_inc(s_tok, 1)

            @block.gpsimd
            def _(pool):
                ch = Chain(pool, s_chp)
                ch.link(nc.gpsimd.iota(lo_i[:, :], pattern=[[1, NTT], [0, 2]], base=0, channel_multiplier=0))
                ch.link(nc.gpsimd.tensor_copy(tile_f[:, :], lo_i[:, :]))
                ch.link(nc.gpsimd.iota(cnt_i[:, 0:1], pattern=[[1, 1]], base=0, channel_multiplier=1))
                ch.link(nc.gpsimd.tensor_copy(pcol[:, :], cnt_i[:, 0:1]))
                ch.restart()
                pool.sem_inc(s_inval, 1)

            @block.vector
            def _(dve):
                ch = Chain(dve, s_chv)
                V = nc.vector
                dve.wait_ge(s_inval, 1)
                dve.wait_ge(s_cnt, 1)
                ch.link(V.tensor_scalar(cnt[:, :], bank[0][:, 0:NE], float(P - 1), float(P), ALU.add, ALU.max))
                ch.link(V.tensor_copy(cnt_i[:, :], cnt[:, :]))
                ch.link(V.tensor_scalar(cnt_i[:, :], cnt_i[:, :], 7, None, ALU.arith_shift_right))
                ch.add(V.tensor_copy(nblk[:, :], cnt_i[:, :]))
                ch.link(V.memset(zero[:, :], 0.0))
                ch.link(V.tensor_tensor_scan(cum_f[:, :], nblk[:, :], zero[:, :], 0.0, ALU.add, ALU.add))
                ch.link(V.tensor_tensor(first[:, :], cum_f[:, :], nblk[:, :], ALU.subtract))
                ch.link(V.tensor_scalar(first[:, :], first[:, :], float(P), None, ALU.mult))
                pf = picked[:, :, :, :].rearrange("p t n e -> p (t n) e")
                po = pos[:, :, :, :].rearrange("p t n e -> p (t n) e")
                ch.link(V.tensor_tensor(po, pf, first[:, :].unsqueeze(1).to_broadcast([P, M, NE]), ALU.mult))
                ch.link(V.tensor_reduce(dest[:, :], po, AX_X, ALU.add))
                ch.link(V.tensor_tensor(dest[:, :], dest[:, :], rank[:, :, :].rearrange("p t n -> p (t n)"), ALU.add))
                di = dest_i[:, :, :].rearrange("p t n -> p (t n)")
                ch.link(V.tensor_copy(di, dest[:, :]))
                ch.add(V.tensor_scalar(lo_i[:, :], di, P - 1, None, ALU.bitwise_and))
                ch.add(V.tensor_scalar(hi_i[:, :], di, 7, None, ALU.arith_shift_right))
                ch.wait()
                ch.add(V.tensor_copy(lo_f[:, :], lo_i[:, :]))
                ch.add(V.tensor_copy(hi_f[:, :], hi_i[:, :]))
                ch.add(V.tensor_scalar(gsum[:, 0:1], pcol[:, :], float(NS), 1.0e4, ALU.is_ge, ALU.mult))
                ch.wait()
                ch.link(V.tensor_scalar(hi_f[:, M - 2:M], hi_f[:, M - 2:M], gsum[:, 0:1], None, ALU.add))
                ch.add(V.tensor_tensor(oh_lo[:, :, :], iota[:, :].unsqueeze(1).to_broadcast([P, M, P]),
                                       lo_f[:, :].unsqueeze(2).to_broadcast([P, M, P]), ALU.is_equal))
                ch.add(V.tensor_tensor(oh_hi[:, :, 0, :], iota[:, 0:NB].unsqueeze(1).to_broadcast([P, M, NB]),
                                       hi_f[:, :].unsqueeze(2).to_broadcast([P, M, NB]), ALU.is_equal))
                ch.wait()
                ch.link(V.tensor_tensor(oh_hi[:, :, 1, :], oh_hi[:, :, 0, :],
                                        tile_f[:, :].unsqueeze(2).to_broadcast([P, M, NB]), ALU.mult))
                ch.link(V.tensor_scalar(oh_hi[:, :, 0, :], oh_hi[:, :, 0, :], pcol[:, 0:1], None, ALU.mult))
                dve.sem_inc(s_oh, 1)
                ch.link(V.tensor_tensor(cmp[:, :, :], cum_f[0:1, :].unsqueeze(1).to_broadcast([1, NB, NE]),
                                        iota[0:1, 0:NB].unsqueeze(2).to_broadcast([1, NB, NE]), ALU.is_le))
                ch.link(V.tensor_reduce(blk_f[:, :], cmp[:, :, :], AX_X, ALU.add))
                ch.link(V.tensor_scalar(blk_f[:, :], blk_f[:, :], float(NE - 1), None, ALU.min))
                ch.link(V.tensor_copy(blk_e[:, :], blk_f[:, :]))
                ch.link(V.tensor_copy(cum_i[:, :], cum_f[0:1, :]))
                dve.wait_ge(s_tok, 1)
                ch.link(V.tensor_copy(tok_a[:, :, :], bank[1][:, 0:2 * NB].rearrange("p (a b) -> p a b", a=2)))
                ch.link(V.scalar_tensor_tensor(tok_a[:, 0, :], tok_a[:, 1, :], float(P), tok_a[:, 0, :], ALU.mult, ALU.add))
                ch.link(V.tensor_copy(tok_i[:, :], tok_a[:, 0, :]))
                dve.sem_inc(s_tab, 1)
                ch.add(V.tensor_tensor(gd[:, :, :], tops[:, :, 0, :], tops[:, :, 1, 0:1].to_broadcast([P, NTT, 8]), ALU.subtract))
                ch.add(V.tensor_tensor(ex[:, :], tops[:, :, 2, 1], tops[:, :, 2, 0], ALU.subtract))
                ch.wait()
                dve.sem_inc(s_exi, 1)
                dve.wait_ge(s_exo, 2)
                ch.link(V.tensor_reduce(gsum[:, :], gd[:, :, 0:NRG], AX_X, ALU.add))
                ch.link(V.tensor_scalar(den[:, :], ex[:, :], 1.0, None, ALU.add))
                ch.link(V.tensor_tensor(den[:, :], den[:, :], gsum[:, :], ALU.mult))
                ch.link(V.reciprocal(wt[:, :, 0], den[:, :]))
                ch.link(V.tensor_tensor(wt[:, :, 1], wt[:, :, 0], ex[:, :], ALU.mult))
                ch.restart()

            @block.scalar
            def _(act):
                act.wait_ge(s_exi, 1)
                nc.scalar.activation(gd[:, :, :], gd[:, :, :], ACT.Exp).then_inc(s_exo, 1)
                nc.scalar.activation(ex[:, :], ex[:, :], ACT.Exp).then_inc(s_exo, 1)

            @block.sync
            def _(sp):
                for pair in range(EARLY, NU // 2):
                    load_units(sp, 0, pair)

        s_hi = [sem("gate_up_hi_ready"), sem("down_hi_ready")]
        s_lo = [sem("gate_up_lo_ready"), sem("down_lo_ready")]
        s_gu = sem("gate_up_units_passed")
        s_dn = sem("down_units_passed")
        s_xg = [sem(f"rows_gathered{i}") for i in range(2)]
        s_xTp = sem("xT_in_psum")
        s_xh = sem("xT_hi_ready")
        s_xT = sem("xT_ready")
        s_sg = sem("silu_ready")
        s_act = sem("act_ready")
        s_aTp = sem("actT_in_psum")
        s_ah = sem("actT_hi_ready")
        s_aT = sem("actT_ready")
        s_y = sem("y_saved")
        s_ys = [sem(f"y_stored{i}") for i in range(2)]

        def halves_count(j, e):
            return (0, e * GU + j + 1) if j < GU else (1, e * DN + j - GU + 1)

        def is0(s):
            return isinstance(s, int) and s == 0

        def pairs(eng, step):
            blocks = eng.value_load(cum_i[0:1, NE - 1:NE], min_val=NE, max_val=MAXB)
            step(0, 0)
            step(1, 1)
            with eng.Fori(1, PAIRS) as i:
                with eng.If(i * 2 < blocks + 1):
                    for b in range(2):
                        step(i * 2 + b, b)

        def expert_of(eng, s):
            return eng.value_load(blk_e[0:1, ds(s, 1)], min_val=0, max_val=NE - 1)

        def refills(eng, split, s, e, gate_up):
            if gate_up:
                nxt = expert_of(eng, s + 1)
                with eng.If(e < nxt):
                    for j in range(GU):
                        eng.wait_ge(s_gu, s * GU + j + 1)
                        split(j, nxt)
            else:
                prev = expert_of(eng, s - 1)
                with eng.If(prev < e):
                    for j in range(DN):
                        eng.wait_ge(s_dn, (s - 1) * DN + j + 1)
                        split(GU + j, e)

        with nc.Block() as block:
            @block.sync
            def _(sp):
                def load(e, units):
                    for pair in range(units.start // 2, units.stop // 2):
                        kind, count = halves_count(2 * pair + 1, e - 1)
                        sp.wait_ge(s_lo[kind], count)
                        load_units(sp, e, pair)

                load(1, range(0, GU))
                with sp.Fori(1, NE - 1) as e:
                    load(e + 1, range(0, GU))
                    load(e, range(GU, NU))
                load(NE - 1, range(GU, NU))

            @block.tensor
            def _(pe):
                def x_transposes(s, b):
                    pe.wait_ge(s_xg[b], (s - b) * 8 + 16)
                    if not is0(s):
                        pe.wait_ge(s_xT, s)
                    for k in range(KD):
                        ins = nc.tensor.transpose(ps2[0][:, k * P:(k + 1) * P], xg[b][:, k * P:(k + 1) * P], ident[:, :])
                    ins.then_inc(s_xTp, 1)

                def unit(outs, a_hi, a_lo, u, first, last):
                    for n in range(2):
                        q = slice(n * BANK, (n + 1) * BANK)
                        nc.tensor.matmul(outs[n], a_hi, w_hi[u][:, q], start=first, stop=False)
                    for n in range(2):
                        q = slice(n * BANK, (n + 1) * BANK)
                        nc.tensor.matmul(outs[n], a_hi, w_lo[u][:, q], start=False, stop=False)
                    for n in range(2):
                        q = slice(n * BANK, (n + 1) * BANK)
                        ins = nc.tensor.matmul(outs[n], a_lo, w_hi[u][:, q], start=False, stop=last)
                    return ins

                def step(s, b):
                    e = expert_of(pe, s)
                    pe.wait_ge(s_xT, s + 1)
                    if not is0(s):
                        pe.wait_ge(s_sg, s)
                        pe.wait_ge(s_act, s)
                    for k in range(GU):
                        pe.wait_ge(s_lo[0], e * GU + k + 1)
                        unit((bank[2], bank[3]), xT_hi[b][:, k, :], xT_lo[b][:, k, :], k, k == 0, k == GU - 1).then_inc(s_gu, 1)
                    x_transposes(s + 1, 1 - b)
                    if not is0(s):
                        prev = expert_of(pe, s - 1)
                        pe.wait_ge(s_aT, s)
                        if not (isinstance(s, int) and s == 1):
                            pe.wait_ge(s_y, s - 1)
                        for k in range(DN):
                            pe.wait_ge(s_lo[1], prev * DN + k + 1)
                            unit((bank[4], bank[5]), actT_hi[:, k, :], actT_lo[:, k, :], GU + k, k == 0, k == DN - 1).then_inc(s_dn, 1)
                    pe.wait_ge(s_act, s + 1)
                    if not is0(s):
                        pe.wait_ge(s_aT, s)
                    for k in range(KF):
                        ins = nc.tensor.transpose(bank[6][:, k * P:(k + 1) * P], act_t[:, k * P:(k + 1) * P], ident[:, :])
                    ins.then_inc(s_aTp, 1)

                x_transposes(0, 0)
                pairs(pe, step)

            @block.scalar
            def _(act):
                def split_hi(j, e):
                    act.wait_ge(s_raw[j // 2], raw_count(j // 2, e))
                    nc.scalar.copy(w_hi[j][:, :], wraw[:, j, :]).then_inc(s_hi[j >= GU], 1)

                def save_xT(s, b):
                    act.wait_ge(s_xTp, s + 1)
                    if not (isinstance(s, int) and s < 2):
                        act.wait_ge(s_gu, (s - 1) * GU)
                    nc.scalar.copy(xT_hi[b][:, :, :], ps2[0][:, :].rearrange("p (k t) -> p k t", k=KD)).then_inc(s_xh, 1)

                def step(s, b):
                    e = expert_of(act, s)
                    refills(act, split_hi, s, e, True)
                    act.wait_ge(s_gu, s * GU + GU)
                    if not is0(s):
                        act.wait_ge(s_act, s)
                    nc.scalar.activation(sgate[:, :], bank[2], ACT.Silu).then_inc(s_sg, 1)
                    save_xT(s + 1, 1 - b)
                    if not is0(s):
                        refills(act, split_hi, s, e, False)
                        act.wait_ge(s_dn, s * DN)
                        if not (isinstance(s, int) and s < 3):
                            act.wait_ge(s_ys[1 - b], (s - 1 - (1 - b)) * 8)
                        nc.scalar.copy(y_sb[1 - b][:, :], ps2[2][:, :]).then_inc(s_y, 1)
                    act.wait_ge(s_aTp, s + 1)
                    nc.scalar.copy(actT_hi[:, :, :], bank[6].rearrange("p (k t) -> p k t", k=KF)).then_inc(s_ah, 1)

                save_xT(0, 0)
                for j in range(NU):
                    split_hi(j, 0)
                pairs(act, step)

            @block.vector
            def _(dve):
                def split_lo(j, e):
                    kind, count = halves_count(j, e)
                    dve.wait_ge(s_hi[kind], count)
                    nc.vector.tensor_tensor(w_lo[j][:, :], wraw[:, j, :], w_hi[j][:, :].bitcast(F32), ALU.subtract).then_inc(s_lo[kind], 1)

                def save_xT(s, b):
                    dve.wait_ge(s_xh, s + 1)
                    if not (isinstance(s, int) and s < 2):
                        dve.wait_ge(s_gu, (s - 1) * GU)
                    nc.vector.tensor_tensor(xT_lo[b][:, :, :], ps2[0][:, :].rearrange("p (k t) -> p k t", k=KD),
                                            xT_hi[b][:, :, :].bitcast(F32), ALU.subtract).then_inc(s_xT, 1)

                def step(s, b):
                    e = expert_of(dve, s)
                    refills(dve, split_lo, s, e, True)
                    dve.wait_ge(s_sg, s + 1)
                    dve.wait_ge(s_gu, s * GU + GU)
                    if not is0(s):
                        dve.wait_ge(s_aTp, s)
                    nc.vector.tensor_tensor(act_t[:, :], sgate[:, :], bank[3], ALU.mult).then_inc(s_act, 1)
                    save_xT(s + 1, 1 - b)
                    if not is0(s):
                        refills(dve, split_lo, s, e, False)
                        dve.wait_ge(s_dn, s * DN)
                    dve.wait_ge(s_ah, s + 1)
                    nc.vector.tensor_tensor(actT_lo[:, :, :], bank[6].rearrange("p (k t) -> p k t", k=KF),
                                            actT_hi[:, :, :].bitcast(F32), ALU.subtract).then_inc(s_aT, 1)

                save_xT(0, 0)
                for j in range(NU):
                    split_lo(j, 0)
                pairs(dve, step)

            @block.gpsimd
            def _(pool):
                ch = Chain(pool, s_chp)

                def gather(s, b):
                    if not (isinstance(s, int) and s < 2):
                        pool.wait_ge(s_xTp, s - 1)
                        pool.wait_ge(s_xg[b], (s - b) * 8)
                    ch.link(nc.gpsimd.tensor_copy(idx[b][:, :], tok_i[:, ds(s, 1)]))
                    nc.gpsimd.indirect_dma_start(out=xg[b][:, :], out_offset=None, in_=h2_d[:, :],
                                                 in_offset=bass.IndirectOffsetOnAxis(ap=idx[b][:, 0:1], axis=0)).then_inc(s_xg[b], 16)

                def step(s, b):
                    gather(s + 2, b)
                    if not is0(s):
                        pool.wait_ge(s_y, s)
                        pool.dma_start(ye_d[ds((s - 1) * P, P), :], y_sb[1 - b][:, :]).then_inc(s_ys[1 - b], 16)
                    ch.restart()

                gather(0, 0)
                gather(1, 1)
                pairs(pool, step)
                blocks = pool.value_load(cum_i[0:1, NE - 1:NE], min_val=NE, max_val=MAXB)
                more = pool.snap(blocks // 2)
                pool.wait_ge(s_ys[0], more * 16 + 16)
                pool.wait_ge(s_ys[1], more * 16)
                pool.wait_ge(s_xg[0], more * 16 + 32)
                pool.wait_ge(s_xg[1], more * 16 + 32)

        s_tb = sem("last_rows_loaded")
        s_ya = [sem(f"y_rows_gathered{i}") for i in range(2)]
        s_xl = [sem(f"x1_loaded{i}") for i in range(2)]
        s_g2 = sem("gate2_ready")
        s_g2s = sem("sample_gate2_loaded")
        s_f1 = sem("rows_combined")
        s_v2 = sem("x2_var_ready")
        s_s2 = sem("x2_std_ready")
        s_n2 = sem("x2_scale_ready")
        s_nm = sem("x2_normed")
        s_u0 = sem("first_pick_weighted")
        s_x2 = sem("x2_scaled")
        s_fo = sem("out_ready")
        s_fs = [sem(f"out_stored{i}") for i in range(2)]

        with nc.Block() as block:
            @block.sync
            def _(sp):
                sp.dma_start(g2[:, :], mod_row(5)).then_inc(s_tb, 16)
                sp.dma_start(lg2[:, :], row(ln2_g[0])).then_inc(s_tb, 16)
                sp.dma_start(lb2[:, :], row(ln2_b[0])).then_inc(s_tb, 16)
                for b in range(2):
                    sp.dma_start(xf[b][:, :], x1_d[b * P:(b + 1) * P, :]).then_inc(s_xl[b], 16)
                with sp.Fori(0, NT // 2 - 1) as i:
                    for b in range(2):
                        t = i * 2 + b
                        sp.wait_ge(s_f1, t + 1)
                        sp.dma_start(xf[b][:, :], x1_d[ds((t + 2) * P, P), :]).then_inc(s_xl[b], 16)
                        sp.wait_ge(s_fo, t + 1)
                        sp.dma_start(y_prompt[0, ds(t * P, P), :], fo[b][:, :]).then_inc(s_fs[b], 16)
                sp.wait_ge(s_f1, NT - 1)
                sp.dma_start(xf[0][0:NS, :], x1_d[NT * P:NT * P + NS, :]).then_inc(s_xl[0], 16)
                sp.wait_ge(s_f1, NT)
                sp.dma_start(g2[0:NS, :], mod_d[0:NS, 5 * D:6 * D]).then_inc(s_g2s, 16)
                for b in range(2):
                    sp.wait_ge(s_fo, NT - 1 + b)
                    sp.dma_start(y_prompt[0, (NT - 2 + b) * P:(NT - 1 + b) * P, :], fo[b][:, :]).then_inc(s_fs[b], 16)
                sp.wait_ge(s_fo, NT + 1)
                sp.dma_start(y_sample[:, 0, :], fo[0][0:NS, :]).then_inc(s_fs[0], 16)
                sp.wait_ge(s_fs[0], 16 * (NT // 2 + 1))
                sp.wait_ge(s_fs[1], 16 * (NT // 2))

            @block.gpsimd
            def _(pool):
                ch = Chain(pool, s_chp)

                def gathers(t, b, rows=P):
                    if not (isinstance(t, int) and t < 2):
                        pool.wait_ge(s_f1, t - 1)
                    ch.link(nc.gpsimd.tensor_copy(idy[b][0:rows, :], dest_i[0:rows, ds(t, 1), :].rearrange("p a n -> p (a n)")))
                    for n, y in enumerate((ya, yb)):
                        nc.gpsimd.indirect_dma_start(out=y[b][0:rows, :], out_offset=None, in_=ye_d[:, :],
                                                     in_offset=bass.IndirectOffsetOnAxis(ap=idy[b][0:rows, n:n + 1], axis=0)).then_inc(s_ya[b], 16)
                    ch.restart()

                def add_bias(t, b, rows=P):
                    pool.wait_ge(s_x2, t + 1)
                    if not (isinstance(t, int) and t < 2):
                        pool.wait_ge(s_fs[b], (t - b) * 8)
                    nc.gpsimd.tensor_tensor(fo[b][0:rows, :], f_b[b][0:rows, :], lb2[0:rows, :], ALU.add).then_inc(s_fo, 1)

                pool.wait_ge(s_tb, 48)
                gathers(0, 0)
                gathers(1, 1)
                with pool.Fori(1, NT // 2) as i:
                    for b in range(2):
                        gathers(i * 2 + b, b)
                        add_bias(i * 2 + b - 2, b)
                gathers(NT, 0, NS)
                add_bias(NT - 2, 0)
                add_bias(NT - 1, 1)
                add_bias(NT, 0, NS)

            @block.vector
            def _(dve):
                ch = Chain(dve, s_chv)

                def weight(t, n, q):
                    return wt[q, ds(t, 1), n:n + 1].rearrange("p a n -> p (a n)")

                def combine(t, b, rows=P):
                    q = slice(0, rows)
                    dve.wait_ge(s_ya[b], (t - b) * 16 + 32)
                    dve.wait_ge(s_u0, t + 1)
                    ch.link(nc.vector.scalar_tensor_tensor(f_a[q, :], yb[b][q, :], weight(t, 1, q), ya[b][q, :], ALU.mult, ALU.add))
                    ch.link(nc.vector.tensor_tensor(f_a[q, :], f_a[q, :], g2[q, :], ALU.mult))
                    dve.wait_ge(s_xl[b], (t - b) * 8 + 16)
                    if not (isinstance(t, int) and t < 2):
                        dve.wait_ge(s_fo, t - 1)
                    ch.link(nc.vector.scalar_tensor_tensor(f_b[b][q, :], xf[b][q, :], ALPHA, f_a[q, :], ALU.mult, ALU.add))
                    dve.sem_inc(s_f1, 1)
                    for n in range(2):
                        ch.add(nc.vector.bn_stats(bs2[q, n, :], f_b[b][q, n * BANK:(n + 1) * BANK]))
                    ch.wait()
                    nc.vector.bn_aggr(mv2[b][q, :], bs2[q, :, :].rearrange("p a s -> p (a s)")).then_inc(s_v2, 1)

                def scale(t, b, rows=P):
                    q = slice(0, rows)
                    dve.wait_ge(s_nm, t + 1)
                    ch.link(nc.vector.tensor_tensor(f_b[b][q, :], f_b[b][q, :], lg2[q, :], ALU.mult))
                    dve.sem_inc(s_x2, 1)

                def moments(t, b, rows=P):
                    q = slice(0, rows)
                    dve.wait_ge(s_s2, t + 1)
                    ch.link(nc.vector.reciprocal(iv2[b][q, :], sd2[q, :]))
                    nc.vector.tensor_scalar(nb2[b][q, :], mv2[b][q, 0:1], iv2[b][q, 0:1], -1.0, ALU.mult, ALU.mult).then_inc(s_n2, 1)

                def tile(t, b):
                    combine(t, b)
                    if not is0(t):
                        scale(t - 1, 1 - b)
                    moments(t, b)
                    ch.restart()

                dve.wait_ge(s_tb, 48)
                ch.link(nc.vector.tensor_scalar_add(g2[:, :], g2[:, :], 1.0))
                tile(0, 0)
                tile(1, 1)
                with dve.Fori(1, NT // 2) as i:
                    for b in range(2):
                        tile(i * 2 + b, b)
                dve.wait_ge(s_g2s, 16)
                ch.link(nc.vector.tensor_scalar_add(g2[0:NS, :], g2[0:NS, :], 1.0))
                combine(NT, 0, NS)
                scale(NT - 1, 1)
                moments(NT, 0, NS)
                scale(NT, 0, NS)
                ch.restart()

            @block.scalar
            def _(act):
                def first_pick(t, b, rows=P):
                    act.wait_ge(s_ya[b], (t - b) * 16 + 32)
                    nc.scalar.activation(ya[b][0:rows, :], ya[b][0:rows, :], ACT.Copy,
                                         scale=wt[0:rows, ds(t, 1), 0:1].rearrange("p a n -> p (a n)")).then_inc(s_u0, 1)

                def norm(t, b, rows=P):
                    act.wait_ge(s_v2, t + 1)
                    nc.scalar.activation(sd2[0:rows, :], mv2[b][0:rows, 1:2], ACT.Sqrt, bias=eps[0:rows, :]).then_inc(s_s2, 1)
                    act.wait_ge(s_n2, t + 1)
                    nc.scalar.activation(f_b[b][0:rows, :], f_b[b][0:rows, :], ACT.Identity, bias=nb2[b][0:rows, :],
                                         scale=iv2[b][0:rows, :]).then_inc(s_nm, 1)

                first_pick(0, 0)
                for t in range(2):
                    first_pick(t + 1, 1 - t)
                    norm(t, t)
                with act.Fori(1, NT // 2 - 1) as i:
                    for b in range(2):
                        first_pick(i * 2 + b + 1, 1 - b)
                        norm(i * 2 + b, b)
                first_pick(NT - 1, 1)
                norm(NT - 2, 0)
                first_pick(NT, 0, NS)
                norm(NT - 1, 1)
                norm(NT, 0, NS)


_INS = ["x_prompt", "x_sample", "state_pool", "c_prompt", "c_sample", "w_ada", "b_ada", "w_in", "pool_w", "pool_scale",
        "sgu_norm_g", "sgu_w", "sgu_b", "w_out", "ln1_g", "ln1_b", "router_g_w", "router_g_b", "router_e_w",
        "router_e_b", "exp_w_gate", "exp_w_up", "exp_w_down", "ln2_g", "ln2_b"]
_OUTS = [(1, 2048, 1024), (8, 1, 1024), (1, 1, 15, 512), (1, 8, 15, 512), (1, 8, 1, 512)]


def kernel(**inputs):
    import numpy as _np
    import concourse.bacc as _bacc
    from concourse import mybir as _mybir
    from concourse.bass_utils import run_bass_kernel_spmd as _run

    nc = _bacc.Bacc("TRN2", target_bir_lowering=False, num_devices=1)
    arrays, args = {}, []
    for name in _INS:
        a = _np.ascontiguousarray(inputs[name])
        arrays[f"in_{name}_dram"] = a
        args.append(nc.dram_tensor(f"in_{name}_dram", a.shape, _mybir.dt.from_np(a.dtype), kind="ExternalInput").ap())
    for i, shape in enumerate(_OUTS):
        args.append(nc.dram_tensor(f"out_{i}_dram", shape, _mybir.dt.float32, kind="ExternalOutput").ap())
    hybrid_trunk(nc, *args)
    r = _run(nc, [arrays], core_ids=[0])
    return tuple(r.results[0][f"out_{i}_dram"] for i in range(len(_OUTS)))
```

```python
import concourse.bass as bass
from concourse import mybir
from contextlib import ExitStack

ALU = mybir.AluOpType
ACT = mybir.ActivationFunctionType
AX_X = mybir.AxisListType.X
F32 = mybir.dt.float32
F32R = mybir.dt.float32r
BF16 = mybir.dt.bfloat16
I32 = mybir.dt.int32
U32 = mybir.dt.uint32
ds = bass.ds

P = 128
BANK = 512
WINDOWS = (2, 4, 8, 16)
LN_EPS = 1e-5
ALPHA = 2.0 ** 0.25
BIG = 1.0e30


class Region:

    def __init__(self, nc, start, end):
        self.nc, self.at, self.end = nc, start, end

    def take(self, name, shape, dtype):
        n = mybir.dt.size(dtype)
        for s in shape[1:]:
            n *= s
        t = self.nc.alloc_sbuf_tensor_at(name, shape, dtype, offset=self.at)
        self.at += (n + 31) // 32 * 32
        assert self.at <= self.end, (name, self.at - self.end)
        return t


class Chain:

    def __init__(self, eng, sem):
        self.eng, self.sem, self.n = eng, sem, 0

    def add(self, ins):
        self.n += 1
        ins.then_inc(self.sem, 1)

    def wait(self):
        self.eng.wait_ge(self.sem, self.n)

    def link(self, ins):
        self.add(ins)
        self.wait()

    def restart(self):
        if self.n:
            self.wait()
            self.eng.sem_clear(self.sem)
            self.n = 0


def hybrid_trunk(nc, x_prompt, x_sample, state_pool, c_prompt, c_sample, w_ada, b_ada, w_in, pool_w, pool_scale,
                 sgu_norm_g, sgu_w, sgu_b, w_out, ln1_g, ln1_b, router_g_w, router_g_b, router_e_w, router_e_b,
                 exp_w_gate, exp_w_up, exp_w_down, ln2_g, ln2_b,
                 y_prompt, y_sample, pool_prompt, pool_sample, sgu_v):
    SEQ, D = x_prompt.shape[1:]
    NS = x_sample.shape[0]
    NT = SEQ // P
    KD = D // P
    DP = state_pool.shape[3]
    BUF = state_pool.shape[2]
    NG = pool_w.shape[1]
    NH = sgu_w.shape[1]
    NRG = router_g_w.shape[2]
    NE = router_e_w.shape[2]
    EPG = NE // NRG
    FE = exp_w_gate.shape[3]
    KF = FE // P
    NC = NS + 1
    NA = 3
    NR = NRG + NE
    NTT = NT + 1
    MAXB = (2 * (SEQ + NS) - NE) // P + NE + 1
    PAIRS = (MAXB + 2) // 2
    NB = 2 * PAIRS + 2
    assert D == 8 * P and DP == BANK and FE == BANK and NG == NH == 4 and NT % 2 == 0 and NB <= P

    w_in_v = w_in[0].rearrange("(k p) n -> p k n", p=P)
    w_out_v = w_out[0].rearrange("(k p) n -> p k n", p=P)
    w_ada_v = w_ada[0].rearrange("(k p) (g n) -> k g p n", p=P, g=NA)
    gate_v = exp_w_gate[0].rearrange("e (k p) n -> e p k n", p=P)
    up_v = exp_w_up[0].rearrange("e (k p) n -> e p k n", p=P)
    down_v = exp_w_down[0].rearrange("e (k p) n -> e p k n", p=P)

    mod_d = nc.dram_tensor("mod_rows", [NC, 6 * D], F32).ap()
    mix_d = nc.dram_tensor("mixer_tiles", [NT * P, KD * P], F32).ap()
    h2_d = nc.dram_tensor("h2_rows", [SEQ + NS, D], F32).ap()
    x1_d = nc.dram_tensor("x1_rows", [SEQ + NS, D], F32).ap()
    ye_d = nc.dram_tensor("expert_rows", [NB * P, D], F32).ap()

    ctx = ExitStack()
    with ctx:
        def sem(name):
            return ctx.enter_context(nc.semaphore(name))

        def psum(name, cols=BANK):
            return ctx.enter_context(nc.psum_tensor(name, [P, cols], F32))

        base = (nc.sbuf_base + 127) // 128 * 128
        last = Region(nc, base, base + 21504)
        MIX0 = last.end
        W0 = MIX0 + 2 * KD * D * 4 + 64
        W1 = W0 + 3 * KD * FE * 4
        W2 = W1 + 3 * KD * FE * 4
        END = nc.sbuf_usable_end // 32 * 32 - KD * NS * 4

        ident = last.take("ident", [P, P], F32)
        ones = last.take("ones", [P, P], BF16)
        before = last.take("before", [P, P], BF16)
        iota = last.take("iota", [P, P], F32)
        iota_i = last.take("iota_i", [P, P], I32)
        pcol = last.take("pcol", [P, 1], F32)
        eps = last.take("eps", [P, 1], F32)
        cT = last.take("cT", [P, KD, NC], F32)
        cT_k = last.take("cT_k", [P, NC], F32)
        acc = last.take("acc", [P, NA, BANK], F32)
        rw = last.take("rw", [P, KD, NR], F32)
        rb = last.take("rb", [P, NR], F32)
        picked = last.take("picked", [P, NTT, 2, NE], F32)
        rank = last.take("rank", [P, NTT, 2], F32)
        tops = last.take("tops", [P, NTT, 3, 8], F32)
        top = last.take("top", [P, 3, 8], F32)
        seen = last.take("seen", [P, NE], F32)
        seen_b = last.take("seen_b", [P, NE], BF16)
        wt = last.take("wt", [P, NTT, 2], F32)
        dest_i = last.take("dest_i", [P, NTT, 2], I32)
        cum_f = last.take("cum_f", [P, NE], F32)
        cum_i = last.take("cum_i", [1, NE], I32)
        blk_e = last.take("blk_e", [1, NB], I32)
        tok_i = last.take("tok_i", [P, NB], I32)

        mixT_s = nc.alloc_sbuf_tensor_at("mixT_s", [P, KD, NS], F32, offset=END)
        mix_o = nc.alloc_sbuf_tensor_at("mix_o", [P, KD, P], F32, offset=MIX0)
        ada0 = nc.alloc_sbuf_tensor_at("ada0", [P, KD, 4 * BANK], F32, offset=MIX0)

        w_in_sb = nc.alloc_sbuf_tensor_at("w_in_sb", [P, KD, 3 * BANK], F32, offset=W0)
        r = Region(nc, W1, W2)
        x_t = [r.take(f"x_t{i}", [P, D], F32) for i in range(2)]
        h_t = r.take("h_t", [P, D], F32)
        hT = [r.take(f"hT{i}", [P, KD, P], F32) for i in range(2)]
        p_sb = [r.take(f"p_sb{i}", [P, DP], F32) for i in range(2)]
        u_sb = r.take("u_sb", [P, DP], F32)
        vn = r.take("vn", [P, DP], F32)
        dT = r.take("dT", [P, NG, P], F32)
        g_sb = r.take("g_sb", [P, DP], F32)
        band = r.take("band", [P, NG, P], F32)
        band0 = r.take("band0", [P, NG, P], F32)
        bandp = r.take("bandp", [P, NG, P], F32)
        vstat = r.take("vstat", [P, NH, 6], F32)
        vmv = r.take("vmv", [P, NH, 2], F32)
        vstd = r.take("vstd", [P, NH], F32)
        vinv = r.take("vinv", [P, NH], F32)
        bt = r.take("bt", [P, NH], F32)
        psc = r.take("psc", [P, NG], F32)
        b0s = r.take("b0s", [P, NH], F32)
        w0s = r.take("w0s", [P, NH], F32)
        wsT = r.take("wsT", [P, NH, P], F32)
        pw = r.take("pw", [P, NG, P], F32)
        invc = r.take("invc", [P, P], F32)
        zrow = r.take("zrow", [P, D], F32)
        r = Region(nc, W2, END)
        ada_st = [r.take(f"ada_st{i}", [P, 4 * BANK], F32) for i in range(2)]
        sc1 = r.take("sc1", [P, D], F32)
        sh1 = r.take("sh1", [P, D], F32)
        sg_bc = r.take("sg_bc", [P, DP], F32)
        r = Region(nc, W1, W2)
        wst_raw = nc.alloc_sbuf_tensor_at("wst_raw", [P, NH, P], F32, offset=W1)
        c_raw = nc.alloc_sbuf_tensor_at("c_raw", [NC, D], F32, offset=W1 + 4096)
        hist_len = [w - 1 for w in WINDOWS]
        hist = [None] * NG
        at = W2
        for g in range(NG):
            hist[g] = nc.alloc_sbuf_tensor_at(f"hist{g}", [NS, hist_len[g], P], F32, offset=at)
            at += hist_len[g] * P * 4

        EARLY = 2
        r = Region(nc, MIX0, W0)
        wo_hi = [r.take(f"wo_hi{k}", [P, D], F32R) for k in range(KD)]
        wo_lo = [r.take(f"wo_lo{k}", [P, D], F32R) for k in range(KD)]
        w_out_raw = nc.alloc_sbuf_tensor_at("w_out_raw", [P, KD, D], F32, offset=W0)
        small = Region(nc, W0 + EARLY * 2 * 2 * FE * 4, END)
        g1_s = small.take("g1_s", [NS, D], F32)
        sc2_s = small.take("sc2_s", [NS, D], F32)
        sh2_s = small.take("sh2_s", [NS, D], F32)
        tmp_s = small.take("tmp_s", [NS, D], F32)
        assert small.at == W0 + KD * D * 4
        g1 = small.take("g1", [P, D], F32)
        sc2 = small.take("sc2", [P, D], F32)
        sh2 = small.take("sh2", [P, D], F32)
        lg1 = small.take("lg1", [P, D], F32)
        lb1 = small.take("lb1", [P, D], F32)
        x_r = [small.take(f"x_r{i}", [P, D], F32) for i in range(2)]
        t_r = small.take("t_r", [P, D], F32)
        x1 = [small.take(f"x1_{i}", [P, D], F32) for i in range(2)]
        h2 = [small.take(f"h2_{i}", [P, D], F32) for i in range(2)]
        h2T = small.take("h2T", [P, KD, P], F32)
        mix_r = [small.take(f"mix_r{i}", [P, KD, P], F32) for i in range(2)]
        mix_hi = [small.take(f"mix_hi{i}", [P, KD, P], F32R) for i in range(2)]
        mix_lo = [small.take(f"mix_lo{i}", [P, KD, P], F32R) for i in range(2)]
        nb1 = small.take("nb1", [P, 1], F32)
        bst = small.take("bst", [P, 2, 6], F32)
        mv = small.take("mv", [P, 2], F32)
        std = small.take("std", [P, 1], F32)
        inv = small.take("inv", [P, 1], F32)
        lgT = small.take("lgT", [P, P], F32)
        el = small.take("el", [P, NE], F32)
        gidx = small.take("gidx", [P, 8], U32)
        gidf = small.take("gidf", [P, 1], F32)
        gm = small.take("gm", [P, NRG], F32)
        eidx = small.take("eidx", [P, 8], U32)
        eidf = small.take("eidf", [P, 2], F32)
        m_b = small.take("m_b", [P, NE], BF16)
        rk = small.take("rk", [P, 2, NE], F32)

        UNIT = 2 * FE
        GU, DN = KD, KF
        NU = GU + DN
        LOW_UNITS = 6
        BLK_END = W0 - LOW_UNITS * UNIT * 4
        r = Region(nc, MIX0, BLK_END)
        pos = r.take("pos", [P, NTT, 2, NE], F32)
        cnt = r.take("cnt", [P, NE], F32)
        cnt_i = r.take("cnt_i", [P, NE], I32)
        nblk = r.take("nblk", [P, NE], F32)
        first = r.take("first", [P, NE], F32)
        zero = r.take("zero", [P, NE], F32)
        dest = r.take("dest", [P, NTT * 2], F32)
        lo_i = r.take("lo_i", [P, NTT * 2], I32)
        hi_i = r.take("hi_i", [P, NTT * 2], I32)
        lo_f = r.take("lo_f", [P, NTT * 2], F32)
        hi_f = r.take("hi_f", [P, NTT * 2], F32)
        oh_lo = r.take("oh_lo", [P, NTT * 2, P], BF16)
        oh_hi = r.take("oh_hi", [P, NTT * 2, 2, NB], BF16)
        tile_f = r.take("tile_f", [P, NTT * 2], F32)
        cmp = r.take("cmp", [1, NB, NE], F32)
        blk_f = r.take("blk_f", [1, NB], F32)
        ex = r.take("ex", [P, NTT], F32)
        tok_a = r.take("tok_a", [P, 2, NB], F32)
        gd = r.take("gd", [P, NTT, 8], F32)
        gsum = r.take("gsum", [P, NTT], F32)
        den = r.take("den", [P, NTT], F32)

        wraw = nc.alloc_sbuf_tensor_at("wraw", [P, NU, UNIT], F32, offset=W0)
        lows = Region(nc, BLK_END, W0)
        highs = Region(nc, W0 + NU * UNIT * 4, END)
        halves = [(lows if n < LOW_UNITS else highs).take(f"w_half{n}", [P, UNIT], F32R) for n in range(2 * NU)]
        w_hi, w_lo = halves[0::2], halves[1::2]
        r = Region(nc, MIX0, BLK_END)
        xg = [r.take(f"xg{i}", [P, D], F32) for i in range(2)]
        xT_hi = [r.take(f"xT_hi{i}", [P, KD, P], F32R) for i in range(2)]
        xT_lo = [r.take(f"xT_lo{i}", [P, KD, P], F32R) for i in range(2)]
        sgate = r.take("sgate", [P, FE], F32)
        act_t = r.take("act_t", [P, FE], F32)
        actT_hi = r.take("actT_hi", [P, KF, P], F32R)
        actT_lo = r.take("actT_lo", [P, KF, P], F32R)
        y_sb = [r.take(f"y_sb{i}", [P, D], F32) for i in range(2)]
        idx = [r.take(f"idx{i}", [P, 1], I32) for i in range(2)]

        r = Region(nc, W0, END)
        ya = [r.take(f"ya{i}", [P, D], F32) for i in range(2)]
        yb = [r.take(f"yb{i}", [P, D], F32) for i in range(2)]
        xf = [r.take(f"xf{i}", [P, D], F32) for i in range(2)]
        fo = [r.take(f"fo{i}", [P, D], F32) for i in range(2)]
        f_a = r.take("f_a", [P, D], F32)
        f_b = [r.take(f"f_b{i}", [P, D], F32) for i in range(2)]
        g2 = r.take("g2", [P, D], F32)
        lg2 = r.take("lg2", [P, D], F32)
        lb2 = r.take("lb2", [P, D], F32)
        idy = [r.take(f"idy{i}", [P, 2], I32) for i in range(2)]
        bs2 = r.take("bs2", [P, 2, 6], F32)
        mv2 = [r.take(f"mv2_{i}", [P, 2], F32) for i in range(2)]
        sd2 = r.take("sd2", [P, 1], F32)
        iv2 = [r.take(f"iv2_{i}", [P, 1], F32) for i in range(2)]
        nb2 = [r.take(f"nb2_{i}", [P, 1], F32) for i in range(2)]

        ps2 = [ctx.enter_context(nc.psum_tensor(f"ps2_{i}", [P, 2 * BANK], F32)) for i in range(4)]
        bank = [ps2[i // 2][:, (i % 2) * BANK:(i % 2 + 1) * BANK] for i in range(8)]

        def mod_row(j):
            return mod_d[NS:NS + 1, j * D:(j + 1) * D].partition_broadcast(P)

        def is0(s):
            return isinstance(s, int) and s == 0

        def row(v, n=P):
            return v.rearrange("(a n) -> a n", a=1).partition_broadcast(n)

        s_small = sem("small_loaded")
        s_ws = sem("sgu_w_loaded")
        s_c = sem("c_loaded")
        s_win = sem("w_in_loaded")
        s_ada0 = [sem(f"ada0_loaded{k}") for k in range(KD)]
        s_const = sem("constants_built")
        s_chp = sem("pool_chain")
        s_chv = sem("vector_chain")
        s_cha = sem("scalar_chain")
        s_cs = sem("c_silu")
        s_cTp = sem("cT_in_psum")
        s_cT = sem("cT_ready")
        s_wsp = sem("wsT_in_psum")
        s_wsT = sem("wsT_ready")
        s_adap = sem("ada_in_psum")
        s_modr = sem("mod_rows_ready")
        s_mods = sem("mod_rows_stored")

        with nc.Block() as block:
            @block.sync
            def _(sp):
                sp.dma_start(c_raw[0:NS, :], c_sample).then_inc(s_c, 16)
                sp.dma_start(c_raw[NS:NC, :], c_prompt).then_inc(s_c, 16)
                for k in range(KD):
                    sp.dma_start(ada0[:, k, :], w_ada_v[k, 0]).then_inc(s_ada0[k], 16)
                sp.dma_start(w_in_sb[:, :, :], w_in_v).then_inc(s_win, 16)
                sp.wait_ge(s_modr, 1)
                for j in range(4):
                    sp.dma_start(mod_d[:, j * BANK:(j + 1) * BANK], acc[32 * j:32 * j + NC, 0, :]).then_inc(s_mods, 16)
                sp.wait_ge(s_mods, 64)

            @block.scalar
            def _(act):
                act.dma_start(wst_raw[:, :, :], sgu_w[0].rearrange("h t s -> t h s")).then_inc(s_ws, 16)
                for g in range(NA):
                    for j in range(4):
                        at = (4 * g + j) * BANK
                        act.dma_start(acc[32 * j:32 * j + NC, g, :],
                                      row(b_ada[0, at:at + BANK], NC)).then_inc(s_small, 16)
                act.dma_start(pw[:, :, :], pool_w[0].rearrange("g c d -> c g d")).then_inc(s_small, 16)
                act.dma_start(psc[:, :], pool_scale[0].rearrange("(g d) -> d g", g=NG),
                              allow_slow_non_contiguous=True).then_inc(s_small, 16)
                act.dma_start(bt[:, :], sgu_b[0].rearrange("h t -> t h"),
                              allow_slow_non_contiguous=True).then_inc(s_small, 16)
                act.dma_start(b0s[0:NS, :], sgu_b[0, :, 0:1].rearrange("h a -> a h").partition_broadcast(NS),
                              allow_slow_non_contiguous=True).then_inc(s_small, 16)
                act.dma_start(w0s[0:NS, :], sgu_w[0, :, 0, 0:1].rearrange("h a -> a h").partition_broadcast(NS),
                              allow_slow_non_contiguous=True).then_inc(s_small, 16)
                act.dma_start(sg_bc[:, :], row(sgu_norm_g[0])).then_inc(s_small, 16)
                act.dma_start(rw[:, :, 0:NRG], router_g_w[0].rearrange("(k p) n -> p k n", p=P)).then_inc(s_small, 16)
                act.dma_start(rw[:, :, NRG:NR], router_e_w[0].rearrange("(k p) n -> p k n", p=P)).then_inc(s_small, 16)
                act.dma_start(rb[:, 0:NRG], row(router_g_b[0])).then_inc(s_small, 16)
                act.dma_start(rb[:, NRG:NR], row(router_e_b[0])).then_inc(s_small, 16)
                act.wait_ge(s_c, 32)
                nc.scalar.activation(c_raw[:, :], c_raw[:, :], ACT.Silu).then_inc(s_cs, 1)
                act.wait_ge(s_cTp, 1)
                nc.scalar.copy(cT[:, :, :], bank[0][:, 0:KD * NC].rearrange("p (k c) -> p k c", c=NC)).then_inc(s_cT, 1)
                act.wait_ge(s_wsp, 1)
                nc.scalar.copy(wsT[:, :, :], bank[1].rearrange("p (h s) -> p h s", s=P)).then_inc(s_wsT, 1)

            @block.gpsimd
            def _(pool):
                ch = Chain(pool, s_chp)
                ch.add(nc.gpsimd.memset(ident[:, :], 0.0))
                ch.add(nc.gpsimd.memset(before[:, :], 1.0))
                ch.add(nc.gpsimd.memset(ones[:, :], 1.0))
                for g, w in enumerate(WINDOWS):
                    ch.add(nc.gpsimd.memset(band[:, g, :], 1.0))
                    ch.add(nc.gpsimd.memset(bandp[:, g, :], 1.0 / w))
                ch.add(nc.gpsimd.iota(iota_i[:, :], pattern=[[1, P]], base=0, channel_multiplier=0))
                ch.add(nc.gpsimd.memset(p_sb[1][:, :], 0.0))
                ch.add(nc.gpsimd.memset(picked[:, NT, :, :], 0.0))
                ch.add(nc.gpsimd.memset(rank[:, NT, :], 0.0))
                ch.add(nc.gpsimd.memset(tops[:, NT, :, :], 0.0))
                ch.add(nc.gpsimd.memset(top[:, :, :], -BIG))
                ch.add(nc.gpsimd.memset(seen[:, :], 0.0))
                ch.add(nc.gpsimd.memset(seen_b[:, :], 0.0))
                ch.add(nc.gpsimd.memset(zrow[:, :], 0.0))
                ch.add(nc.gpsimd.memset(eps[:, :], LN_EPS))
                ch.wait()
                ch.add(nc.gpsimd.affine_select(out=ident[:, :], in_=ident[:, :], compare_op=ALU.not_equal, fill=1.0,
                                               base=0, pattern=[[-1, P]], channel_multiplier=1))
                ch.add(nc.gpsimd.affine_select(out=before[:, :], in_=before[:, :], compare_op=ALU.is_gt, fill=0.0,
                                               base=0, pattern=[[1, P]], channel_multiplier=-1))
                for g, w in enumerate(WINDOWS):
                    ch.add(nc.gpsimd.affine_select(out=bandp[:, g, :], in_=bandp[:, g, :], compare_op=ALU.is_ge,
                                                   fill=0.0, base=w - 1 - P, pattern=[[-1, P]], channel_multiplier=1))
                    ch.link(nc.gpsimd.affine_select(out=band[:, g, :], in_=band[:, g, :], compare_op=ALU.is_ge,
                                                    fill=0.0, base=0, pattern=[[1, P]], channel_multiplier=-1))
                    ch.add(nc.gpsimd.affine_select(out=band[:, g, :], in_=band[:, g, :], compare_op=ALU.is_ge,
                                                   fill=0.0, base=w - 1, pattern=[[-1, P]], channel_multiplier=1))
                ch.wait()
                pool.sem_inc(s_const, 1)
                pool.wait_ge(s_wsT, 1)
                nc.gpsimd.affine_select(out=wsT[:, :, :], in_=wsT[:, :, :], compare_op=ALU.is_ge, fill=0.0,
                                        base=0, pattern=[[0, NH], [1, P]], channel_multiplier=-1).then_inc(s_const, 1)
                pool.wait_ge(s_const, 2)
                ch.restart()

            @block.vector
            def _(dve):
                ch = Chain(dve, s_chv)
                dve.wait_ge(s_const, 1)
                ch.link(nc.vector.tensor_copy(iota[:, :], iota_i[:, :]))
                for g, w in enumerate(WINDOWS):
                    ch.link(nc.vector.tensor_scalar(invc[:, :], iota[:, :], 1.0, float(w), ALU.add, ALU.min))
                    ch.link(nc.vector.reciprocal(invc[:, :], invc[:, :]))
                    ch.link(nc.vector.tensor_tensor(band0[:, g, :], band[:, g, :], invc[:, :], ALU.mult))
                    ch.add(nc.vector.tensor_tensor(band0[:, g, :], band0[:, g, :], ident[:, :], ALU.subtract))
                    ch.add(nc.vector.scalar_tensor_tensor(band[:, g, :], band[:, g, :], 1.0 / w, ident[:, :],
                                                          ALU.mult, ALU.subtract))
                dve.wait_ge(s_small, 16 * (4 * NA + 10))
                dve.wait_ge(s_adap, 1)
                for j in range(4):
                    q = slice(32 * j, 32 * j + NC)
                    ch.add(nc.vector.tensor_tensor(acc[q, 0, :], bank[2][q, :], acc[q, 0, :], ALU.add))
                ch.restart()
                dve.sem_inc(s_modr, 1)

            @block.tensor
            def _(pe):
                pe.wait_ge(s_const, 1)
                pe.wait_ge(s_ws, 16)
                for h in range(NH):
                    ins = nc.tensor.transpose(bank[1][:, h * P:(h + 1) * P], wst_raw[:, h, :], ident[:, :])
                ins.then_inc(s_wsp, 1)
                pe.wait_ge(s_cs, 1)
                for k in range(KD):
                    ins = nc.tensor.transpose(bank[0][:, k * NC:(k + 1) * NC], c_raw[:, k * P:(k + 1) * P],
                                              ident[0:NC, 0:NC])
                ins.then_inc(s_cTp, 1)
                pe.wait_ge(s_cT, 1)
                for k in range(KD):
                    pe.wait_ge(s_ada0[k], 16)
                    for j in range(4):
                        ins = nc.tensor.matmul(bank[2][32 * j:32 * j + NC, :], cT[:, k, :],
                                               ada0[:, k, j * BANK:(j + 1) * BANK], start=(k == 0), stop=(k == KD - 1))
                ins.then_inc(s_adap, 1)

        s_sc1 = sem("scale1_loaded")
        s_sc1r = sem("scale1_ready")
        s_x = [sem(f"x_loaded{i}") for i in range(2)]
        s_adal = [sem(f"ada_loaded{i}") for i in range(2)]
        s_ck = sem("c_tile_ready")
        s_h = sem("h_ready")
        s_hTp = sem("hT_in_psum")
        s_hT = sem("hT_ready")
        s_pp = sem("p_in_psum")
        s_up = sem("u_in_psum")
        s_vp = sem("v_in_psum")
        s_p = sem("p_saved")
        s_u = sem("u_saved")
        s_bd = sem("band_done")
        s_dT = sem("dT_saved")
        s_am = sem("pool_mm_done")
        s_a = sem("a_saved")
        s_var = sem("v_var_ready")
        s_std = sem("v_std_ready")
        s_vn = sem("vn_ready")
        s_z = sem("z_done")
        s_g = sem("g_ready")
        s_gTp = sem("gT_in_psum")
        s_gT = sem("gT_saved")
        s_ad = sem("ada_unit_done")
        s_aa = sem("ada_unit_added")
        s_ps = sem("pool_state_stored")
        s_hist = sem("history_loaded")
        s_hs = sem("history_used")
        s_vs = sem("sgu_v_stored")
        s_sc1s = sem("sample_scale1_loaded")
        s_sc1sr = sem("sample_scale1_ready")
        s_smu = sem("sample_g_ready")
        s_zf = sem("spare_blocks_zeroed")
        s_mos = sem("mixer_tile_stored")
        PER = (NB - NE) // NT

        xp = x_prompt[0]

        with nc.Block() as block:
            @block.gpsimd
            def _(pool):
                def zero_block(n):
                    pool.dma_start(ye_d[ds((n + NE) * P, P), :], zrow[:, :]).then_inc(s_zf, 16)

                with pool.Fori(0, NT) as t:
                    pool.wait_ge(s_a, t + 1)
                    pool.wait_ge(s_gT, t + 1)
                    pool.dma_start(mix_d[ds(t * P, P), :], mix_o[:, :, :].rearrange("p k c -> p (k c)")).then_inc(s_mos, 16)
                    for n in range(PER):
                        zero_block(t * PER + n)
                for n in range(NT * PER, NB - NE):
                    zero_block(n)
                pool.wait_ge(s_zf, 16 * (NB - NE))
                pool.wait_ge(s_mos, 16 * NT)

            @block.sync
            def _(sp):
                sp.dma_start(sh1[:, :], mod_row(0)).then_inc(s_sc1, 16)
                sp.dma_start(sc1[:, :], mod_row(1)).then_inc(s_sc1, 16)
                for t in range(2):
                    sp.dma_start(x_t[t][:, :], xp[t * P:(t + 1) * P, :]).then_inc(s_x[t], 16)
                for t in range(2):
                    sp.dma_start(ada_st[t][:, :], w_ada_v[0, 1 + t]).then_inc(s_adal[t], 16)

                with sp.Fori(0, NT // 2 - 1) as i:
                    for b in range(2):
                        sp.wait_ge(s_h, i * 2 + b + 1)
                        sp.dma_start(x_t[b][:, :], xp[ds((i * 2 + b + 2) * P, P), :]).then_inc(s_x[b], 16)
                        sp.wait_ge(s_ad, i * 2 + b + 1)
                        sp.dma_start(ada_st[b][:, :], w_ada_v[ds(i + 1, 1), 1 + b].rearrange("a p n -> p (a n)")).then_inc(s_adal[b], 16)
                sp.wait_ge(s_h, NT - 1)
                sp.dma_start(x_t[0][0:NS, :], x_sample[:, 0, :]).then_inc(s_x[0], 16)
                sp.wait_ge(s_h, NT)
                sp.dma_start(sh1[0:NS, :], mod_d[0:NS, 0:D]).then_inc(s_sc1s, 16)
                sp.dma_start(sc1[0:NS, :], mod_d[0:NS, D:2 * D]).then_inc(s_sc1s, 16)
                sp.wait_ge(s_ad, NT)
                for g in range(NG):
                    sp.dma_start(hist[g][:, :, :], state_pool[0, :, BUF - hist_len[g]:BUF, g * P:(g + 1) * P]).then_inc(s_hist, 16)
                sp.dma_start(pool_sample[0, :, 0:BUF - 1, :], state_pool[0, :, 1:BUF, :]).then_inc(s_ps, 16)
                sp.wait_ge(s_p, NT)
                sp.dma_start(pool_prompt[0, 0], p_sb[(NT - 1) % 2][P - BUF:P, :]).then_inc(s_ps, 16)
                sp.wait_ge(s_p, NT + 1)
                sp.dma_start(pool_sample[0, :, BUF - 1, :], p_sb[NT % 2][0:NS, :]).then_inc(s_ps, 16)
                sp.wait_ge(s_vn, NT + 1)
                sp.dma_start(sgu_v[0, :, 0, :], vn[0:NS, :]).then_inc(s_vs, 16)
                sp.wait_ge(s_aa, NT)
                for g in range(1, NA):
                    for j in range(4):
                        at = (4 * g + j) * BANK
                        sp.dma_start(mod_d[:, at:at + BANK], acc[32 * j:32 * j + NC, g, :]).then_inc(s_mods, 16)
                sp.wait_ge(s_mods, 64 * NA)
                sp.wait_ge(s_ps, 48)
                sp.wait_ge(s_vs, 16)

            @block.tensor
            def _(pe):
                def h_transposes(t, b, rows=P):
                    pe.wait_ge(s_h, t + 1)
                    if not (isinstance(t, int) and t == 0):
                        pe.wait_ge(s_hT, t)
                    for k in range(KD):
                        ins = nc.tensor.transpose(ps2[0][:, k * P:k * P + rows], h_t[0:rows, k * P:(k + 1) * P],
                                                  ident[0:rows, 0:rows])
                    ins.then_inc(s_hTp, 1)

                def project(t, b, part, out, signal, free, rows=P):
                    if free is not None:
                        pe.wait_ge(free, t)
                    for k in range(KD):
                        ins = nc.tensor.matmul(out[0:rows, :], hT[b][:, k, 0:rows],
                                               w_in_sb[:, k, part * BANK:(part + 1) * BANK],
                                               start=(k == 0), stop=(k == KD - 1))
                    ins.then_inc(signal, 1)

                def bands(t, b, mats):
                    pe.wait_ge(s_p, t + 1)
                    if not (isinstance(t, int) and t == 0):
                        pe.wait_ge(s_gT, t)
                    for g in range(NG):
                        q = slice(g * P, (g + 1) * P)
                        nc.tensor.matmul(bank[5][:, q], p_sb[b][:, q], mats[:, g, :], start=True, stop=False)
                        ins = nc.tensor.matmul(bank[5][:, q], p_sb[1 - b][:, q], bandp[:, g, :], start=False, stop=True)
                    ins.then_inc(s_bd, 1)

                def pool_linear(t):
                    pe.wait_ge(s_dT, t + 1)
                    if not (isinstance(t, int) and t == 0):
                        pe.wait_ge(s_a, t)
                    for g in range(NG):
                        ins = nc.tensor.matmul(bank[7][:, g * P:(g + 1) * P], pw[:, g, :], dT[:, g, :],
                                               start=True, stop=True)
                    ins.then_inc(s_am, 1)

                def gating(t):
                    pe.wait_ge(s_vn, t + 1)
                    pe.wait_ge(s_aa, t + 1)
                    for h in range(NH):
                        q = slice(h * P, (h + 1) * P)
                        ins = nc.tensor.matmul(bank[6][:, q], wsT[:, h, :], vn[:, q], start=True, stop=True)
                    ins.then_inc(s_z, 1)

                def g_transposes(t):
                    pe.wait_ge(s_g, t + 1)
                    pe.wait_ge(s_dT, t + 1)
                    for h in range(NH):
                        ins = nc.tensor.transpose(bank[5][:, h * P:(h + 1) * P], g_sb[:, h * P:(h + 1) * P], ident[:, :])
                    ins.then_inc(s_gTp, 1)

                def ada_pair_unit(i, b):
                    pe.wait_ge(s_adal[b], i * 16 + 16)
                    for j in range(4):
                        ins = nc.tensor.matmul(bank[6][32 * j:32 * j + NC, :], cT_k[:, :],
                                               ada_st[b][:, j * BANK:(j + 1) * BANK], start=True, stop=True)
                    ins.then_inc(s_ad, 1)

                def tile(t, b, i):
                    pe.wait_ge(s_hT, t + 1)
                    lead = isinstance(t, int) and t == 0
                    project(t, b, 0, bank[2], s_pp, None if lead else s_p)
                    if not lead:
                        bands(t - 1, 1 - b, band0 if isinstance(t, int) and t == 1 else band)
                    project(t, b, 1, bank[3], s_up, None if lead else s_u)
                    if not lead:
                        pool_linear(t - 1)
                        gating(t - 1)
                    project(t, b, 2, bank[4], s_vp, None if lead else s_vn)
                    if not lead:
                        g_transposes(t - 1)
                    if not (isinstance(t, int) and t == NT - 1):
                        h_transposes(t + 1, 1 - b)
                    if not lead:
                        pe.wait_ge(s_g, t)
                    pe.wait_ge(s_ck, t + 1)
                    ada_pair_unit(i, b)

                pe.wait_ge(s_win, 16)
                h_transposes(0, 0)
                tile(0, 0, 0)
                tile(1, 1, 0)
                with pe.Fori(1, NT // 2 - 1) as i:
                    for b in range(2):
                        tile(i * 2 + b, b, i)
                tile(NT - 2, 0, NT // 2 - 1)
                tile(NT - 1, 1, NT // 2 - 1)
                bands(NT - 1, 1, band)
                h_transposes(NT, 0, NS)
                pool_linear(NT - 1)
                gating(NT - 1)
                g_transposes(NT - 1)
                pe.wait_ge(s_hT, NT + 1)
                project(NT, 0, 0, bank[2], s_pp, s_p, NS)
                project(NT, 0, 1, bank[3], s_up, s_u, NS)
                project(NT, 0, 2, bank[4], s_vp, s_vn, NS)
                pe.wait_ge(s_gT, NT)
                pe.wait_ge(s_hs, 1)
                for g in range(NG):
                    ins = nc.tensor.transpose(bank[5][:, g * NS:(g + 1) * NS], g_sb[0:NS, g * P:(g + 1) * P],
                                              ident[0:NS, 0:NS])
                ins.then_inc(s_bd, 1)
                pe.wait_ge(s_dT, NT + 1)
                pe.wait_ge(s_a, NT)
                for g in range(NG):
                    ins = nc.tensor.matmul(bank[7][:, g * NS:(g + 1) * NS], pw[:, g, :], dT[:, g, 0:NS],
                                           start=True, stop=True)
                ins.then_inc(s_am, 1)
                pe.wait_ge(s_smu, 1)
                for h in range(NH):
                    ins = nc.tensor.transpose(bank[5][:, h * NS:(h + 1) * NS], u_sb[0:NS, h * P:(h + 1) * P],
                                              ident[0:NS, 0:NS])
                ins.then_inc(s_gTp, 1)

            @block.vector
            def _(dve):
                ch = Chain(dve, s_chv)

                def modulate(t, b, rows=P):
                    dve.wait_ge(s_x[b], x_count(t, b))
                    if not (isinstance(t, int) and t == 0):
                        dve.wait_ge(s_hTp, t)
                    ch.link(nc.vector.tensor_tensor(h_t[0:rows, :], x_t[b][0:rows, :], sc1[0:rows, :], ALU.mult))
                    nc.vector.tensor_tensor(h_t[0:rows, :], h_t[0:rows, :], sh1[0:rows, :], ALU.add).then_inc(s_h, 1)

                def x_count(t, b):
                    return (t - b) * 8 + 16

                def save_dT(t):
                    dve.wait_ge(s_bd, t + 1)
                    if not (isinstance(t, int) and t == 0):
                        dve.wait_ge(s_am, t)
                    nc.vector.tensor_copy(dT[:, :, :], bank[5].rearrange("p (g t) -> p g t", g=NG)).then_inc(s_dT, 1)

                def gate(t):
                    dve.wait_ge(s_z, t + 1)
                    dve.wait_ge(s_u, t + 1)
                    if not (isinstance(t, int) and t == 0):
                        dve.wait_ge(s_gTp, t)
                    for h in range(NH):
                        q = slice(h * P, (h + 1) * P)
                        ch.add(nc.vector.scalar_tensor_tensor(g_sb[:, q], bank[6][:, q], bt[:, h:h + 1], u_sb[:, q],
                                                              ALU.add, ALU.mult))
                    ch.wait()
                    dve.sem_inc(s_g, 1)

                def add_unit(t, b):
                    dve.wait_ge(s_ad, t + 1)
                    for j in range(4):
                        q = slice(32 * j, 32 * j + NC)
                        ch.add(nc.vector.tensor_tensor(acc[q, 1 + b, :], bank[6][q, :], acc[q, 1 + b, :], ALU.add))
                    ch.wait()
                    dve.sem_inc(s_aa, 1)

                def copy_c(i):
                    nc.vector.tensor_scalar(cT_k[:, :], cT[:, ds(i, 1), :].rearrange("p a c -> p (a c)"), 1.0, None,
                                            ALU.mult).then_inc(s_ck, 1)

                def head_norm(t, rows=P):
                    dve.wait_ge(s_vp, t + 1)
                    if not (isinstance(t, int) and t == 0):
                        dve.wait_ge(s_z, t)
                    v = bank[4]
                    for h in range(NH):
                        ch.add(nc.vector.bn_stats(vstat[0:rows, h, :], v[0:rows, h * P:(h + 1) * P]))
                    ch.wait()
                    for h in range(NH):
                        ch.add(nc.vector.bn_aggr(vmv[0:rows, h, :], vstat[0:rows, h, :]))
                    ch.wait()
                    dve.sem_inc(s_var, 1)
                    dve.wait_ge(s_std, t + 1)
                    ch.link(nc.vector.reciprocal(vinv[0:rows, :], vstd[0:rows, :]))
                    for h in range(NH):
                        q = slice(h * P, (h + 1) * P)
                        ch.add(nc.vector.tensor_scalar(vn[0:rows, q], v[0:rows, q], vmv[0:rows, h, 0:1],
                                                       vinv[0:rows, h:h + 1], ALU.subtract, ALU.mult))
                    ch.wait()
                    nc.vector.tensor_tensor(vn[0:rows, :], vn[0:rows, :], sg_bc[0:rows, :], ALU.mult).then_inc(s_vn, 1)

                def tile(t, b, i):
                    lead = isinstance(t, int) and t == 0
                    if not lead:
                        save_dT(t - 1)
                        dve.wait_ge(s_ad, t)
                    copy_c(i)
                    if not (isinstance(t, int) and t == NT - 1):
                        modulate(t + 1, 1 - b)
                    if not lead:
                        gate(t - 1)
                    add_unit(t, b)
                    head_norm(t)
                    ch.restart()

                dve.wait_ge(s_sc1, 32)
                nc.vector.tensor_scalar_add(sc1[:, :], sc1[:, :], 1.0).then_inc(s_sc1r, 1)
                dve.wait_ge(s_sc1r, 1)
                modulate(0, 0)
                tile(0, 0, 0)
                tile(1, 1, 0)
                with dve.Fori(1, NT // 2 - 1) as i:
                    for b in range(2):
                        tile(i * 2 + b, b, i)
                tile(NT - 2, 0, NT // 2 - 1)
                tile(NT - 1, 1, NT // 2 - 1)
                save_dT(NT - 1)
                dve.wait_ge(s_sc1s, 32)
                nc.vector.tensor_scalar_add(sc1[0:NS, :], sc1[0:NS, :], 1.0).then_inc(s_sc1r, 1)
                dve.wait_ge(s_sc1r, 2)
                modulate(NT, 0, NS)
                gate(NT - 1)
                dve.wait_ge(s_hist, 16 * NG)
                dve.wait_ge(s_gTp, NT)
                for g in range(NG):
                    ch.add(nc.vector.tensor_reduce(g_sb[0:NS, g * P:(g + 1) * P],
                                                   hist[g][:, :, :].rearrange("b w c -> b c w"), AX_X, ALU.add))
                ch.wait()
                dve.wait_ge(s_p, NT + 1)
                p_s = p_sb[NT % 2]
                ch.link(nc.vector.tensor_tensor(g_sb[0:NS, :], g_sb[0:NS, :], p_s[0:NS, :], ALU.add))
                for g, w in enumerate(WINDOWS):
                    q = slice(g * P, (g + 1) * P)
                    ch.add(nc.vector.scalar_tensor_tensor(g_sb[0:NS, q], g_sb[0:NS, q], 1.0 / w, p_s[0:NS, q],
                                                          ALU.mult, ALU.subtract))
                ch.wait()
                dve.sem_inc(s_hs, 1)
                dve.wait_ge(s_bd, NT + 1)
                dve.wait_ge(s_am, NT)
                nc.vector.tensor_copy(dT[:, :, 0:NS], bank[5][:, 0:NG * NS].rearrange("p (g t) -> p g t", g=NG)).then_inc(s_dT, 1)
                head_norm(NT, NS)
                dve.wait_ge(s_vn, NT + 1)
                dve.wait_ge(s_u, NT + 1)
                for h in range(NH):
                    q = slice(h * P, (h + 1) * P)
                    ch.link(nc.vector.tensor_scalar(h_t[0:NS, q], vn[0:NS, q], w0s[0:NS, h:h + 1], b0s[0:NS, h:h + 1],
                                                    ALU.mult, ALU.add))
                    ch.add(nc.vector.tensor_tensor(u_sb[0:NS, q], u_sb[0:NS, q], h_t[0:NS, q], ALU.mult))
                ch.wait()
                dve.sem_inc(s_smu, 1)
                ch.restart()

            @block.scalar
            def _(act):
                ch = Chain(act, s_cha)

                def save_p(t, b, rows=P):
                    act.wait_ge(s_pp, t + 1)
                    if not (isinstance(t, int) and t == 0):
                        act.wait_ge(s_bd, t)
                    nc.scalar.copy(p_sb[b][0:rows, :], bank[2][0:rows, :]).then_inc(s_p, 1)

                def save_u(t, rows=P):
                    act.wait_ge(s_up, t + 1)
                    if not (isinstance(t, int) and t == 0):
                        act.wait_ge(s_g, t)
                    nc.scalar.copy(u_sb[0:rows, :], bank[3][0:rows, :]).then_inc(s_u, 1)

                def save_a(t, n=P):
                    act.wait_ge(s_am, t + 1)
                    if not (isinstance(t, int) and t in (0, NT)):
                        act.wait_ge(s_mos, t * 16)
                    for g in range(NG):
                        if isinstance(t, int) and t == NT:
                            out = mixT_s[:, g, :]
                        else:
                            out = mix_o[:, g, :]
                        ch.add(nc.scalar.activation(out, bank[7][:, g * n:(g + 1) * n], ACT.Copy, scale=psc[:, g:g + 1]))
                    ch.wait()
                    act.sem_inc(s_a, 1)

                def save_gT(t):
                    act.wait_ge(s_gTp, t + 1)
                    nc.scalar.copy(mix_o[:, NG:NG + NH, :], bank[5].rearrange("p (h c) -> p h c", h=NH)).then_inc(s_gT, 1)

                def save_hT(t, b, rows=P):
                    act.wait_ge(s_hTp, t + 1)
                    if not (isinstance(t, int) and t < 2):
                        act.wait_ge(s_vp, t - 1)
                    nc.scalar.copy(hT[b][:, :, 0:rows],
                                   ps2[0][:, :].rearrange("p (k t) -> p k t", k=KD)[:, :, 0:rows]).then_inc(s_hT, 1)

                def std_v(t, rows=P):
                    act.wait_ge(s_var, t + 1)
                    nc.scalar.activation(vstd[0:rows, :], vmv[0:rows, :, 1], ACT.Sqrt, bias=eps[0:rows, :]).then_inc(s_std, 1)

                def tile(t, b):
                    lead = isinstance(t, int) and t == 0
                    save_p(t, b)
                    save_u(t)
                    if not lead:
                        save_a(t - 1)
                        save_gT(t - 1)
                    if not (isinstance(t, int) and t == NT - 1):
                        save_hT(t + 1, 1 - b)
                    std_v(t)
                    ch.restart()

                save_hT(0, 0)
                tile(0, 0)
                tile(1, 1)
                with act.Fori(1, NT // 2 - 1) as i:
                    for b in range(2):
                        tile(i * 2 + b, b)
                tile(NT - 2, 0)
                tile(NT - 1, 1)
                save_hT(NT, 0, NS)
                save_a(NT - 1)
                save_gT(NT - 1)
                save_p(NT, 0, NS)
                save_u(NT, NS)
                std_v(NT, NS)
                save_a(NT, NS)
                act.wait_ge(s_gTp, NT + 1)
                nc.scalar.copy(mixT_s[:, NG:NG + NH, :],
                               bank[5][:, 0:NH * NS].rearrange("p (h c) -> p h c", h=NH)).then_inc(s_gT, 1)
                act.wait_ge(s_gT, NT + 1)
                ch.restart()

        s_bc = sem("norm_rows_loaded")
        s_wo = [sem(f"w_out_loaded{k}") for k in range(KD // 2)]
        s_woh = sem("w_out_hi_ready")
        s_wol = sem("w_out_lo_ready")
        s_g1 = sem("gate_rows_ready")
        s_sc2 = sem("scale_rows_ready")
        s_nrow = sem("norm_rows_ready")
        s_mr = [sem(f"mix_loaded{i}") for i in range(2)]
        s_mh = sem("mix_hi_ready")
        s_ml = sem("mix_lo_ready")
        s_xr = [sem(f"x_reloaded{i}") for i in range(2)]
        s_mix = sem("mix_in_psum")
        s_mixr = sem("mix_read")
        s_xu = sem("x_used")
        s_v1 = sem("x1_var_ready")
        s_s1 = sem("x1_std_ready")
        s_mo = sem("x1_moments_ready")
        s_nrm = sem("x1_normed")
        s_x1p = sem("x1_scaled")
        s_x1 = sem("x1_ready")
        s_x1s = [sem(f"x1_stored{i}") for i in range(2)]
        s_h2q = sem("h2_scaled")
        s_h2 = sem("h2_ready")
        s_h2s = [sem(f"h2_stored{i}") for i in range(2)]
        s_h2p = sem("h2T_in_psum")
        s_h2T = sem("h2T_ready")
        s_rt = sem("router_in_psum")
        s_lgT = sem("logitsT_ready")
        s_lg = sem("logits_in_psum")
        s_m = sem("mask_ready")
        s_rk = sem("rank_in_psum")
        s_rkr = sem("rank_read")
        s_bcs = sem("sample_norm_rows_loaded")
        s_lz = sem("logitsT_zeroed")
        s_raw = [sem(f"raw_units_loaded{i}") for i in range(NU // 2)]

        def load_units(eng, e, pair):
            k = 2 * pair
            if k < GU:
                for half, w_v in enumerate((gate_v, up_v)):
                    eng.dma_start(wraw[:, k:k + 2, half * FE:(half + 1) * FE],
                                  w_v[ds(e, 1), :, k:k + 2, :].rearrange("a p k n -> p (a k) n")).then_inc(s_raw[pair], 16)
            else:
                k -= GU
                eng.dma_start(wraw[:, GU + k:GU + k + 2, :],
                              down_v[ds(e, 1), :, k:k + 2, :].rearrange("a p k n -> p (a k) n")).then_inc(s_raw[pair], 16)

        def raw_count(pair, e):
            return e * 32 + 32 if 2 * pair < GU else e * 16 + 16

        def rows_of(t):
            return NS if isinstance(t, int) and t == NT else P

        def frames(eng, frame):
            for t in range(4):
                frame(t, t % 2)
            with eng.Fori(2, NT // 2 - 1) as i:
                for b in range(2):
                    frame(i * 2 + b, b)
            for t in range(NT - 2, NT + 5):
                frame(t, t % 2)

        def there(t):
            return not isinstance(t, int) or 0 <= t <= NT

        with nc.Block() as block:
            @block.sync
            def _(sp):
                for t in range(2):
                    sp.dma_start(mix_r[t][:, :, :].rearrange("p k c -> p (k c)"),
                                 mix_d[t * P:(t + 1) * P, :]).then_inc(s_mr[t], 16)
                for k in range(KD // 2):
                    sp.dma_start(w_out_raw[:, 2 * k:2 * k + 2, :], w_out_v[:, 2 * k:2 * k + 2, :]).then_inc(s_wo[k], 16)
                for dst, src in ((g1, mod_row(2)), (sc2, mod_row(4)), (sh2, mod_row(3)),
                                 (lg1, row(ln1_g[0])), (lb1, row(ln1_b[0]))):
                    sp.dma_start(dst[:, :], src).then_inc(s_bc, 16)
                for t in range(2):
                    sp.dma_start(x_r[t][:, :], xp[t * P:(t + 1) * P, :]).then_inc(s_xr[t], 16)
                sp.wait_ge(s_wol, KD)
                for dst, j in ((g1_s, 2), (sc2_s, 4), (sh2_s, 3)):
                    sp.dma_start(dst[:, :], mod_d[0:NS, j * D:(j + 1) * D]).then_inc(s_bcs, 16)
                for pair in range(EARLY):
                    load_units(sp, 0, pair)

                def frame(t, b):
                    if not isinstance(t, int) or t + 1 < NT and t >= 1:
                        sp.wait_ge(s_ml, t)
                        sp.dma_start(mix_r[1 - b][:, :, :].rearrange("p k c -> p (k c)"),
                                     mix_d[ds((t + 1) * P, P), :]).then_inc(s_mr[1 - b], 16)
                    if isinstance(t, int) and (t < 1 or t > NT + 1):
                        return
                    if not (isinstance(t, int) and t >= NT):
                        sp.wait_ge(s_xu, t)
                        if isinstance(t, int) and t == NT - 1:
                            sp.dma_start(x_r[1 - b][0:NS, :], x_sample[:, 0, :]).then_inc(s_xr[1 - b], 16)
                        else:
                            sp.dma_start(x_r[1 - b][:, :], xp[ds((t + 1) * P, P), :]).then_inc(s_xr[1 - b], 16)
                    n = rows_of(t - 1)
                    sp.wait_ge(s_x1, t)
                    sp.dma_start(x1_d[ds((t - 1) * P, n), :], x1[1 - b][0:n, :]).then_inc(s_x1s[1 - b], 16)
                    sp.wait_ge(s_h2, t)
                    sp.dma_start(h2_d[ds((t - 1) * P, n), :], h2[1 - b][0:n, :]).then_inc(s_h2s[1 - b], 16)

                frames(sp, frame)
                for b in range(2):
                    sp.wait_ge(s_x1s[b], 16 * (NT // 2 + 1 - b))
                    sp.wait_ge(s_h2s[b], 16 * (NT // 2 + 1 - b))

            @block.tensor
            def _(pe):
                def project(t, b, units):
                    rows = rows_of(t)
                    if units.start == 0:
                        pe.wait_ge(s_ml, t + 1)
                        if not (isinstance(t, int) and t < 2):
                            pe.wait_ge(s_mixr, t - 1)
                    for k in units:
                        if is0(t):
                            pe.wait_ge(s_wol, k + 1)
                        terms = ((mix_hi, wo_hi), (mix_hi, wo_lo), (mix_lo, wo_hi))
                        for m, (a, w) in enumerate(terms):
                            for n in range(2):
                                q = slice(n * BANK, (n + 1) * BANK)
                                ins = nc.tensor.matmul(ps2[b][0:rows, q], a[b][:, k, 0:rows], w[k][:, q],
                                                       start=(k == 0 and m == 0), stop=(k == KD - 1 and m == 2))
                    if units.stop == KD:
                        ins.then_inc(s_mix, 1)

                def h2_transposes(t, b):
                    rows = rows_of(t)
                    pe.wait_ge(s_h2, t + 1)
                    if not is0(t):
                        pe.wait_ge(s_h2T, t)
                    for k in range(KD):
                        ins = nc.tensor.transpose(ps2[2][:, k * P:k * P + rows], h2[b][0:rows, k * P:(k + 1) * P],
                                                  ident[0:rows, 0:rows])
                    ins.then_inc(s_h2p, 1)

                def router(t, rows=P):
                    pe.wait_ge(s_h2T, t + 1)
                    if not (isinstance(t, int) and t == 0):
                        pe.wait_ge(s_lgT, t)
                    for k in range(KD):
                        ins = nc.tensor.matmul(bank[6][0:NR, 0:rows], rw[:, k, :], h2T[:, k, 0:rows],
                                               start=(k == 0), stop=(k == KD - 1))
                    ins.then_inc(s_rt, 1)

                def logits(t, rows=P):
                    pe.wait_ge(s_lgT, t + 1)
                    if not (isinstance(t, int) and t == 0):
                        pe.wait_ge(s_rkr, t)
                    nc.tensor.transpose(bank[7][0:rows, 0:P], lgT[:, 0:rows], ident[:, :]).then_inc(s_lg, 1)

                def ranks(t, rows=P):
                    pe.wait_ge(s_m, t + 1)
                    q = bank[7][0:rows, P:P + NE]
                    nc.tensor.matmul(q, before[0:rows, 0:rows], m_b[0:rows, :], start=True, stop=False)
                    nc.tensor.matmul(q, ones[:, 0:rows], seen_b[:, :], start=False, stop=True).then_inc(s_rk, 1)

                def frame(t, b):
                    if there(t):
                        project(t, b, range(0, KD // 2))
                    if there(t - 2):
                        h2_transposes(t - 2, b)
                    if there(t - 3):
                        logits(t - 3, rows_of(t - 3))
                    if there(t):
                        project(t, b, range(KD // 2, KD))
                    if there(t - 2):
                        router(t - 2, rows_of(t - 2))
                    if there(t - 3):
                        ranks(t - 3, rows_of(t - 3))

                frames(pe, frame)

            @block.gpsimd
            def _(pool):
                ch = Chain(pool, s_chp)

                def split_lo(t, b):
                    rows = rows_of(t)
                    src = mixT_s if rows == NS else mix_r[b]
                    pool.wait_ge(s_mh, t + 1)
                    if not (isinstance(t, int) and t < 2):
                        pool.wait_ge(s_mix, t - 1)
                    nc.gpsimd.tensor_tensor(mix_lo[b][:, :, 0:rows], src[:, :, 0:rows],
                                            mix_hi[b][:, :, 0:rows].bitcast(F32), ALU.subtract).then_inc(s_ml, 1)

                def add_biases(t, b):
                    n = rows_of(t)
                    pool.wait_ge(s_x1p, t + 1)
                    nc.gpsimd.tensor_tensor(x1[b][0:n, :], x1[b][0:n, :], lb1[0:n, :], ALU.add).then_inc(s_x1, 1)
                    pool.wait_ge(s_h2q, t + 1)
                    nc.gpsimd.tensor_tensor(h2[b][0:n, :], h2[b][0:n, :], (sh2_s if n == NS else sh2)[0:n, :],
                                            ALU.add).then_inc(s_h2, 1)

                def fold_rows(scale, shift, tmp, n):
                    ch.link(nc.gpsimd.tensor_tensor(tmp[0:n, :], lb1[0:n, :], scale[0:n, :], ALU.mult))
                    ch.add(nc.gpsimd.tensor_tensor(shift[0:n, :], tmp[0:n, :], shift[0:n, :], ALU.add))
                    ch.link(nc.gpsimd.tensor_tensor(scale[0:n, :], lg1[0:n, :], scale[0:n, :], ALU.mult))

                def frame(t, b):
                    if there(t + 1):
                        split_lo(t + 1, 1 - b)
                    if is0(t):
                        pool.wait_ge(s_sc2, 1)
                        fold_rows(sc2, sh2, x1[1], P)
                        pool.sem_inc(s_nrow, 1)
                    if isinstance(t, int) and t == 3:
                        pool.wait_ge(s_sc2, 2)
                        fold_rows(sc2_s, sh2_s, tmp_s, NS)
                        pool.sem_inc(s_nrow, 1)
                    if there(t - 1):
                        add_biases(t - 1, 1 - b)

                nc.gpsimd.memset(lgT[:, :], 0.0).then_inc(s_lz, 1)
                split_lo(0, 0)
                frames(pool, frame)
                ch.restart()

            @block.vector
            def _(dve):
                ch = Chain(dve, s_chv)

                def norm_sums(t, b):
                    n = rows_of(t)
                    q = slice(0, n)
                    dve.wait_ge(s_mix, t + 1)
                    ch.link(nc.vector.tensor_tensor(t_r[q, :], ps2[b][q, :], (g1_s if n == NS else g1)[q, :], ALU.mult))
                    dve.sem_inc(s_mixr, 1)
                    dve.wait_ge(s_xr[b], (t - b) * 8 + 16)
                    ch.link(nc.vector.scalar_tensor_tensor(t_r[q, :], x_r[b][q, :], ALPHA, t_r[q, :], ALU.mult, ALU.add))
                    dve.sem_inc(s_xu, 1)
                    for h in range(2):
                        ch.add(nc.vector.bn_stats(bst[q, h, :], t_r[q, h * BANK:(h + 1) * BANK]))
                    ch.wait()
                    nc.vector.bn_aggr(mv[q, :], bst[q, :, :].rearrange("p a s -> p (a s)")).then_inc(s_v1, 1)

                def moments(t):
                    q = slice(0, rows_of(t))
                    dve.wait_ge(s_s1, t + 1)
                    ch.link(nc.vector.reciprocal(inv[q, :], std[q, :]))
                    nc.vector.tensor_scalar(nb1[q, :], mv[q, 0:1], inv[q, 0:1], -1.0, ALU.mult, ALU.mult).then_inc(s_mo, 1)

                def norm_scale(t, b):
                    n = rows_of(t)
                    q = slice(0, n)
                    dve.wait_ge(s_nrm, t + 1)
                    if not (isinstance(t, int) and t < 2):
                        dve.wait_ge(s_x1s[b], (t - b) * 8)
                    ch.link(nc.vector.tensor_tensor(x1[b][q, :], t_r[q, :], lg1[q, :], ALU.mult))
                    dve.sem_inc(s_x1p, 1)
                    if not (isinstance(t, int) and t < 2):
                        dve.wait_ge(s_h2s[b], (t - b) * 8)
                        dve.wait_ge(s_h2p, t - 1)
                    ch.link(nc.vector.tensor_tensor(h2[b][q, :], t_r[q, :], (sc2_s if n == NS else sc2)[q, :], ALU.mult))
                    dve.sem_inc(s_h2q, 1)

                def route(t, rows=P):
                    q = slice(0, rows)
                    gl, gt, et = (top[q, n, :] for n in range(3))
                    dve.wait_ge(s_lg, t + 1)
                    ch.add(nc.vector.tensor_tensor(gl[:, 0:NRG], bank[7][q, 0:NRG], rb[q, 0:NRG], ALU.add))
                    ch.link(nc.vector.tensor_tensor(el[q, :], bank[7][q, NRG:NR], rb[q, NRG:NR], ALU.add))
                    ch.link(nc.vector.max(gt, gl))
                    ch.link(nc.vector.max_index(gidx[q, :], gt, gl))
                    ch.link(nc.vector.tensor_copy(gidf[q, :], gidx[q, 0:1]))
                    ch.link(nc.vector.tensor_scalar(gm[q, :], iota[q, 0:NRG], gidf[q, 0:1], -BIG, ALU.not_equal, ALU.mult))
                    ch.link(nc.vector.tensor_tensor(el[q, :].rearrange("p (g e) -> p g e", g=NRG),
                                                    el[q, :].rearrange("p (g e) -> p g e", g=NRG),
                                                    gm[q, :].unsqueeze(2).to_broadcast([rows, NRG, EPG]), ALU.add))
                    ch.link(nc.vector.max(et, el[q, :]))
                    ch.link(nc.vector.max_index(eidx[q, :], et, el[q, :]))
                    ch.add(nc.vector.tensor_copy(tops[q, ds(t, 1), :, :].rearrange("p a m n -> p (a m n)"),
                                                 top[q, :, :].rearrange("p m n -> p (m n)")))
                    ch.link(nc.vector.tensor_copy(eidf[q, :], eidx[q, 0:2]))
                    for n in range(2):
                        ch.add(nc.vector.tensor_scalar(pick(t, n, q), iota[q, 0:NE], eidf[q, n:n + 1], None, ALU.is_equal))
                    ch.wait()
                    nc.vector.tensor_tensor(m_b[q, :], pick(t, 0, q), pick(t, 1, q), ALU.add).then_inc(s_m, 1)

                def read_rank(t, rows=P):
                    q = slice(0, rows)
                    dve.wait_ge(s_rk, t + 1)
                    for n in range(2):
                        ch.add(nc.vector.tensor_tensor(rk[q, n, :], pick(t, n, q), bank[7][q, P:P + NE], ALU.mult))
                    ch.link(nc.vector.tensor_tensor(seen[q, :], seen[q, :], m_b[q, :], ALU.add))
                    ch.add(nc.vector.tensor_copy(seen_b[q, :], seen[q, :]))
                    ch.add(nc.vector.tensor_reduce(rank[q, ds(t, 1), :].rearrange("p a n -> p (a n)"), rk[q, :, :], AX_X, ALU.add))
                    ch.wait()
                    dve.sem_inc(s_rkr, 1)

                def pick(t, n, q):
                    return picked[q, ds(t, 1), n, :].rearrange("p a e -> p (a e)")

                def frame(t, b):
                    if there(t - 1):
                        norm_sums(t - 1, 1 - b)
                    if there(t - 4):
                        read_rank(t - 4, rows_of(t - 4))
                    if there(t - 1):
                        moments(t - 1)
                    if there(t - 3):
                        route(t - 3, rows_of(t - 3))
                    if is0(t - 1):
                        dve.wait_ge(s_nrow, 1)
                    if isinstance(t, int) and t == NT + 1:
                        dve.wait_ge(s_nrow, 2)
                    if there(t - 1):
                        norm_scale(t - 1, 1 - b)
                    if isinstance(t, int) and t == 2:
                        dve.wait_ge(s_bcs, 48)
                        ch.add(nc.vector.tensor_scalar_add(g1_s[:, :], g1_s[:, :], 1.0))
                        ch.link(nc.vector.tensor_scalar_add(sc2_s[:, :], sc2_s[:, :], 1.0))
                        dve.sem_inc(s_sc2, 1)
                    ch.restart()

                for k in range(KD):
                    dve.wait_ge(s_woh, k + 1)
                    nc.vector.tensor_tensor(wo_lo[k][:, :], w_out_raw[:, k, :], wo_hi[k][:, :].bitcast(F32),
                                            ALU.subtract).then_inc(s_wol, 1)
                dve.wait_ge(s_bc, 80)
                ch.add(nc.vector.tensor_scalar_add(g1[:, :], g1[:, :], 1.0))
                ch.link(nc.vector.tensor_scalar_add(sc2[:, :], sc2[:, :], 1.0))
                dve.sem_inc(s_sc2, 1)
                frames(dve, frame)

            @block.scalar
            def _(act):
                def split_hi(t, b):
                    rows = rows_of(t)
                    if rows == P:
                        act.wait_ge(s_mr[b], (t - b) * 8 + 16)
                    src = mixT_s if rows == NS else mix_r[b]
                    if not (isinstance(t, int) and t < 2):
                        act.wait_ge(s_mix, t - 1)
                    nc.scalar.copy(mix_hi[b][:, :, 0:rows], src[:, :, 0:rows]).then_inc(s_mh, 1)

                def normalise(t):
                    n = rows_of(t)
                    act.wait_ge(s_v1, t + 1)
                    nc.scalar.activation(std[0:n, :], mv[0:n, 1:2], ACT.Sqrt, bias=eps[0:n, :]).then_inc(s_s1, 1)
                    act.wait_ge(s_mo, t + 1)
                    nc.scalar.activation(t_r[0:n, :], t_r[0:n, :], ACT.Identity, bias=nb1[0:n, :],
                                         scale=inv[0:n, :]).then_inc(s_nrm, 1)

                def save_h2T(t):
                    n = rows_of(t)
                    act.wait_ge(s_h2p, t + 1)
                    if not is0(t):
                        act.wait_ge(s_rt, t)
                    nc.scalar.copy(h2T[:, :, 0:n],
                                   ps2[2][:, :].rearrange("p (k t) -> p k t", k=KD)[:, :, 0:n]).then_inc(s_h2T, 1)

                def save_lgT(t):
                    n = rows_of(t)
                    act.wait_ge(s_rt, t + 1)
                    if not is0(t):
                        act.wait_ge(s_lg, t)
                    nc.scalar.copy(lgT[0:NR, 0:n], bank[6][0:NR, 0:n]).then_inc(s_lgT, 1)

                def frame(t, b):
                    if there(t + 1):
                        split_hi(t + 1, 1 - b)
                    if there(t - 1):
                        normalise(t - 1)
                    if there(t - 2):
                        save_h2T(t - 2)
                        save_lgT(t - 2)

                split_hi(0, 0)
                for k in range(KD):
                    act.wait_ge(s_wo[k // 2], 16)
                    nc.scalar.copy(wo_hi[k][:, :], w_out_raw[:, k, :]).then_inc(s_woh, 1)
                act.wait_ge(s_lz, 1)
                frames(act, frame)

        s_cnt = sem("counts_in_psum")
        s_oh = sem("one_hots_ready")
        s_tok = sem("slot_table_in_psum")
        s_tab = sem("tables_ready")
        s_exi = sem("exponents_ready")
        s_exo = sem("exponentials_ready")
        s_inval = sem("unused_marked")

        M = NTT * 2
        with nc.Block() as block:
            @block.tensor
            def _(pe):
                nc.tensor.matmul(bank[0][:, 0:NE], ones[:, :], seen_b[:, :], start=True, stop=True).then_inc(s_cnt, 1)
                pe.wait_ge(s_oh, 1)
                for m in range(M):
                    ins = nc.tensor.matmul(bank[1][:, 0:2 * NB], oh_lo[:, m, :], oh_hi[:, m, :, :].rearrange("p a b -> p (a b)"),
                                           start=(m == 0), stop=(m == M - 1))
                ins.then_inc(s_tok, 1)

            @block.gpsimd
            def _(pool):
                ch = Chain(pool, s_chp)
                ch.link(nc.gpsimd.iota(lo_i[:, :], pattern=[[1, NTT], [0, 2]], base=0, channel_multiplier=0))
                ch.link(nc.gpsimd.tensor_copy(tile_f[:, :], lo_i[:, :]))
                ch.link(nc.gpsimd.iota(cnt_i[:, 0:1], pattern=[[1, 1]], base=0, channel_multiplier=1))
                ch.link(nc.gpsimd.tensor_copy(pcol[:, :], cnt_i[:, 0:1]))
                ch.restart()
                pool.sem_inc(s_inval, 1)

            @block.vector
            def _(dve):
                ch = Chain(dve, s_chv)
                V = nc.vector
                dve.wait_ge(s_inval, 1)
                dve.wait_ge(s_cnt, 1)
                ch.link(V.tensor_scalar(cnt[:, :], bank[0][:, 0:NE], float(P - 1), float(P), ALU.add, ALU.max))
                ch.link(V.tensor_copy(cnt_i[:, :], cnt[:, :]))
                ch.link(V.tensor_scalar(cnt_i[:, :], cnt_i[:, :], 7, None, ALU.arith_shift_right))
                ch.add(V.tensor_copy(nblk[:, :], cnt_i[:, :]))
                ch.link(V.memset(zero[:, :], 0.0))
                ch.link(V.tensor_tensor_scan(cum_f[:, :], nblk[:, :], zero[:, :], 0.0, ALU.add, ALU.add))
                ch.link(V.tensor_tensor(first[:, :], cum_f[:, :], nblk[:, :], ALU.subtract))
                ch.link(V.tensor_scalar(first[:, :], first[:, :], float(P), None, ALU.mult))
                pf = picked[:, :, :, :].rearrange("p t n e -> p (t n) e")
                po = pos[:, :, :, :].rearrange("p t n e -> p (t n) e")
                ch.link(V.tensor_tensor(po, pf, first[:, :].unsqueeze(1).to_broadcast([P, M, NE]), ALU.mult))
                ch.link(V.tensor_reduce(dest[:, :], po, AX_X, ALU.add))
                ch.link(V.tensor_tensor(dest[:, :], dest[:, :], rank[:, :, :].rearrange("p t n -> p (t n)"), ALU.add))
                di = dest_i[:, :, :].rearrange("p t n -> p (t n)")
                ch.link(V.tensor_copy(di, dest[:, :]))
                ch.add(V.tensor_scalar(lo_i[:, :], di, P - 1, None, ALU.bitwise_and))
                ch.add(V.tensor_scalar(hi_i[:, :], di, 7, None, ALU.arith_shift_right))
                ch.wait()
                ch.add(V.tensor_copy(lo_f[:, :], lo_i[:, :]))
                ch.add(V.tensor_copy(hi_f[:, :], hi_i[:, :]))
                ch.add(V.tensor_scalar(gsum[:, 0:1], pcol[:, :], float(NS), 1.0e4, ALU.is_ge, ALU.mult))
                ch.wait()
                ch.link(V.tensor_scalar(hi_f[:, M - 2:M], hi_f[:, M - 2:M], gsum[:, 0:1], None, ALU.add))
                ch.add(V.tensor_tensor(oh_lo[:, :, :], iota[:, :].unsqueeze(1).to_broadcast([P, M, P]),
                                       lo_f[:, :].unsqueeze(2).to_broadcast([P, M, P]), ALU.is_equal))
                ch.add(V.tensor_tensor(oh_hi[:, :, 0, :], iota[:, 0:NB].unsqueeze(1).to_broadcast([P, M, NB]),
                                       hi_f[:, :].unsqueeze(2).to_broadcast([P, M, NB]), ALU.is_equal))
                ch.wait()
                ch.link(V.tensor_tensor(oh_hi[:, :, 1, :], oh_hi[:, :, 0, :],
                                        tile_f[:, :].unsqueeze(2).to_broadcast([P, M, NB]), ALU.mult))
                ch.link(V.tensor_scalar(oh_hi[:, :, 0, :], oh_hi[:, :, 0, :], pcol[:, 0:1], None, ALU.mult))
                dve.sem_inc(s_oh, 1)
                ch.link(V.tensor_tensor(cmp[:, :, :], cum_f[0:1, :].unsqueeze(1).to_broadcast([1, NB, NE]),
                                        iota[0:1, 0:NB].unsqueeze(2).to_broadcast([1, NB, NE]), ALU.is_le))
                ch.link(V.tensor_reduce(blk_f[:, :], cmp[:, :, :], AX_X, ALU.add))
                ch.link(V.tensor_scalar(blk_f[:, :], blk_f[:, :], float(NE - 1), None, ALU.min))
                ch.link(V.tensor_copy(blk_e[:, :], blk_f[:, :]))
                ch.link(V.tensor_copy(cum_i[:, :], cum_f[0:1, :]))
                dve.wait_ge(s_tok, 1)
                ch.link(V.tensor_copy(tok_a[:, :, :], bank[1][:, 0:2 * NB].rearrange("p (a b) -> p a b", a=2)))
                ch.link(V.scalar_tensor_tensor(tok_a[:, 0, :], tok_a[:, 1, :], float(P), tok_a[:, 0, :], ALU.mult, ALU.add))
                ch.link(V.tensor_copy(tok_i[:, :], tok_a[:, 0, :]))
                dve.sem_inc(s_tab, 1)
                ch.add(V.tensor_tensor(gd[:, :, :], tops[:, :, 0, :], tops[:, :, 1, 0:1].to_broadcast([P, NTT, 8]), ALU.subtract))
                ch.add(V.tensor_tensor(ex[:, :], tops[:, :, 2, 1], tops[:, :, 2, 0], ALU.subtract))
                ch.wait()
                dve.sem_inc(s_exi, 1)
                dve.wait_ge(s_exo, 2)
                ch.link(V.tensor_reduce(gsum[:, :], gd[:, :, 0:NRG], AX_X, ALU.add))
                ch.link(V.tensor_scalar(den[:, :], ex[:, :], 1.0, None, ALU.add))
                ch.link(V.tensor_tensor(den[:, :], den[:, :], gsum[:, :], ALU.mult))
                ch.link(V.reciprocal(wt[:, :, 0], den[:, :]))
                ch.link(V.tensor_tensor(wt[:, :, 1], wt[:, :, 0], ex[:, :], ALU.mult))
                ch.restart()

            @block.scalar
            def _(act):
                act.wait_ge(s_exi, 1)
                nc.scalar.activation(gd[:, :, :], gd[:, :, :], ACT.Exp).then_inc(s_exo, 1)
                nc.scalar.activation(ex[:, :], ex[:, :], ACT.Exp).then_inc(s_exo, 1)

            @block.sync
            def _(sp):
                for pair in range(EARLY, NU // 2):
                    load_units(sp, 0, pair)

        s_hi = [sem("gate_up_hi_ready"), sem("down_hi_ready")]
        s_lo = [sem("gate_up_lo_ready"), sem("down_lo_ready")]
        s_gu = sem("gate_up_units_passed")
        s_dn = sem("down_units_passed")
        s_xg = [sem(f"rows_gathered{i}") for i in range(2)]
        s_xTp = sem("xT_in_psum")
        s_xh = sem("xT_hi_ready")
        s_xT = sem("xT_ready")
        s_sg = sem("silu_ready")
        s_act = sem("act_ready")
        s_aTp = sem("actT_in_psum")
        s_ah = sem("actT_hi_ready")
        s_aT = sem("actT_ready")
        s_y = sem("y_saved")
        s_ys = [sem(f"y_stored{i}") for i in range(2)]

        def halves_count(j, e):
            return (0, e * GU + j + 1) if j < GU else (1, e * DN + j - GU + 1)

        def pairs(eng, step):
            blocks = eng.value_load(cum_i[0:1, NE - 1:NE], min_val=NE, max_val=MAXB)
            step(0, 0)
            step(1, 1)
            with eng.Fori(1, PAIRS) as i:
                with eng.If(i * 2 < blocks + 1):
                    for b in range(2):
                        step(i * 2 + b, b)

        def expert_of(eng, s):
            return eng.value_load(blk_e[0:1, ds(s, 1)], min_val=0, max_val=NE - 1)

        def refills(eng, split, s, e, gate_up):
            if gate_up:
                nxt = expert_of(eng, s + 1)
                with eng.If(e < nxt):
                    for j in range(GU):
                        eng.wait_ge(s_gu, s * GU + j + 1)
                        split(j, nxt)
            else:
                prev = expert_of(eng, s - 1)
                with eng.If(prev < e):
                    for j in range(DN):
                        eng.wait_ge(s_dn, (s - 1) * DN + j + 1)
                        split(GU + j, e)

        with nc.Block() as block:
            @block.sync
            def _(sp):
                def load(e, units):
                    for pair in range(units.start // 2, units.stop // 2):
                        kind, count = halves_count(2 * pair + 1, e - 1)
                        sp.wait_ge(s_lo[kind], count)
                        load_units(sp, e, pair)

                load(1, range(0, GU))
                with sp.Fori(1, NE - 1) as e:
                    load(e + 1, range(0, GU))
                    load(e, range(GU, NU))
                load(NE - 1, range(GU, NU))

            @block.tensor
            def _(pe):
                def x_transposes(s, b):
                    pe.wait_ge(s_xg[b], (s - b) * 8 + 16)
                    if not is0(s):
                        pe.wait_ge(s_xT, s)
                    for k in range(KD):
                        ins = nc.tensor.transpose(ps2[0][:, k * P:(k + 1) * P], xg[b][:, k * P:(k + 1) * P], ident[:, :])
                    ins.then_inc(s_xTp, 1)

                def unit(outs, a_hi, a_lo, u, first, last):
                    for n in range(2):
                        q = slice(n * BANK, (n + 1) * BANK)
                        nc.tensor.matmul(outs[n], a_hi, w_hi[u][:, q], start=first, stop=False)
                    for n in range(2):
                        q = slice(n * BANK, (n + 1) * BANK)
                        nc.tensor.matmul(outs[n], a_hi, w_lo[u][:, q], start=False, stop=False)
                    for n in range(2):
                        q = slice(n * BANK, (n + 1) * BANK)
                        ins = nc.tensor.matmul(outs[n], a_lo, w_hi[u][:, q], start=False, stop=last)
                    return ins

                def step(s, b):
                    e = expert_of(pe, s)
                    pe.wait_ge(s_xT, s + 1)
                    if not is0(s):
                        pe.wait_ge(s_sg, s)
                        pe.wait_ge(s_act, s)
                    for k in range(GU):
                        pe.wait_ge(s_lo[0], e * GU + k + 1)
                        unit((bank[2], bank[3]), xT_hi[b][:, k, :], xT_lo[b][:, k, :], k, k == 0, k == GU - 1).then_inc(s_gu, 1)
                    x_transposes(s + 1, 1 - b)
                    if not is0(s):
                        prev = expert_of(pe, s - 1)
                        pe.wait_ge(s_aT, s)
                        if not (isinstance(s, int) and s == 1):
                            pe.wait_ge(s_y, s - 1)
                        for k in range(DN):
                            pe.wait_ge(s_lo[1], prev * DN + k + 1)
                            unit((bank[4], bank[5]), actT_hi[:, k, :], actT_lo[:, k, :], GU + k, k == 0, k == DN - 1).then_inc(s_dn, 1)
                    pe.wait_ge(s_act, s + 1)
                    if not is0(s):
                        pe.wait_ge(s_aT, s)
                    for k in range(KF):
                        ins = nc.tensor.transpose(bank[6][:, k * P:(k + 1) * P], act_t[:, k * P:(k + 1) * P], ident[:, :])
                    ins.then_inc(s_aTp, 1)

                x_transposes(0, 0)
                pairs(pe, step)

            @block.scalar
            def _(act):
                def split_hi(j, e):
                    act.wait_ge(s_raw[j // 2], raw_count(j // 2, e))
                    nc.scalar.copy(w_hi[j][:, :], wraw[:, j, :]).then_inc(s_hi[j >= GU], 1)

                def save_xT(s, b):
                    act.wait_ge(s_xTp, s + 1)
                    if not (isinstance(s, int) and s < 2):
                        act.wait_ge(s_gu, (s - 1) * GU)
                    nc.scalar.copy(xT_hi[b][:, :, :], ps2[0][:, :].rearrange("p (k t) -> p k t", k=KD)).then_inc(s_xh, 1)

                def step(s, b):
                    e = expert_of(act, s)
                    refills(act, split_hi, s, e, True)
                    act.wait_ge(s_gu, s * GU + GU)
                    if not is0(s):
                        act.wait_ge(s_act, s)
                    nc.scalar.activation(sgate[:, :], bank[2], ACT.Silu).then_inc(s_sg, 1)
                    save_xT(s + 1, 1 - b)
                    if not is0(s):
                        refills(act, split_hi, s, e, False)
                        act.wait_ge(s_dn, s * DN)
                        if not (isinstance(s, int) and s < 3):
                            act.wait_ge(s_ys[1 - b], (s - 1 - (1 - b)) * 8)
                        nc.scalar.copy(y_sb[1 - b][:, :], ps2[2][:, :]).then_inc(s_y, 1)
                    act.wait_ge(s_aTp, s + 1)
                    nc.scalar.copy(actT_hi[:, :, :], bank[6].rearrange("p (k t) -> p k t", k=KF)).then_inc(s_ah, 1)

                save_xT(0, 0)
                for j in range(NU):
                    split_hi(j, 0)
                pairs(act, step)

            @block.vector
            def _(dve):
                def split_lo(j, e):
                    kind, count = halves_count(j, e)
                    dve.wait_ge(s_hi[kind], count)
                    nc.vector.tensor_tensor(w_lo[j][:, :], wraw[:, j, :], w_hi[j][:, :].bitcast(F32), ALU.subtract).then_inc(s_lo[kind], 1)

                def save_xT(s, b):
                    dve.wait_ge(s_xh, s + 1)
                    if not (isinstance(s, int) and s < 2):
                        dve.wait_ge(s_gu, (s - 1) * GU)
                    nc.vector.tensor_tensor(xT_lo[b][:, :, :], ps2[0][:, :].rearrange("p (k t) -> p k t", k=KD),
                                            xT_hi[b][:, :, :].bitcast(F32), ALU.subtract).then_inc(s_xT, 1)

                def step(s, b):
                    e = expert_of(dve, s)
                    refills(dve, split_lo, s, e, True)
                    dve.wait_ge(s_sg, s + 1)
                    dve.wait_ge(s_gu, s * GU + GU)
                    if not is0(s):
                        dve.wait_ge(s_aTp, s)
                    nc.vector.tensor_tensor(act_t[:, :], sgate[:, :], bank[3], ALU.mult).then_inc(s_act, 1)
                    save_xT(s + 1, 1 - b)
                    if not is0(s):
                        refills(dve, split_lo, s, e, False)
                        dve.wait_ge(s_dn, s * DN)
                    dve.wait_ge(s_ah, s + 1)
                    nc.vector.tensor_tensor(actT_lo[:, :, :], bank[6].rearrange("p (k t) -> p k t", k=KF),
                                            actT_hi[:, :, :].bitcast(F32), ALU.subtract).then_inc(s_aT, 1)

                save_xT(0, 0)
                for j in range(NU):
                    split_lo(j, 0)
                pairs(dve, step)

            @block.gpsimd
            def _(pool):
                ch = Chain(pool, s_chp)

                def gather(s, b):
                    if not (isinstance(s, int) and s < 2):
                        pool.wait_ge(s_xTp, s - 1)
                        pool.wait_ge(s_xg[b], (s - b) * 8)
                    ch.link(nc.gpsimd.tensor_copy(idx[b][:, :], tok_i[:, ds(s, 1)]))
                    nc.gpsimd.indirect_dma_start(out=xg[b][:, :], out_offset=None, in_=h2_d[:, :],
                                                 in_offset=bass.IndirectOffsetOnAxis(ap=idx[b][:, 0:1], axis=0)).then_inc(s_xg[b], 16)

                def step(s, b):
                    gather(s + 2, b)
                    if not is0(s):
                        pool.wait_ge(s_y, s)
                        pool.dma_start(ye_d[ds((s - 1) * P, P), :], y_sb[1 - b][:, :]).then_inc(s_ys[1 - b], 16)
                    ch.restart()

                gather(0, 0)
                gather(1, 1)
                pairs(pool, step)
                blocks = pool.value_load(cum_i[0:1, NE - 1:NE], min_val=NE, max_val=MAXB)
                more = pool.snap(blocks // 2)
                pool.wait_ge(s_ys[0], more * 16 + 16)
                pool.wait_ge(s_ys[1], more * 16)
                pool.wait_ge(s_xg[0], more * 16 + 32)
                pool.wait_ge(s_xg[1], more * 16 + 32)

        s_tb = sem("last_rows_loaded")
        s_ya = [sem(f"y_rows_gathered{i}") for i in range(2)]
        s_xl = [sem(f"x1_loaded{i}") for i in range(2)]
        s_g2 = sem("gate2_ready")
        s_g2s = sem("sample_gate2_loaded")
        s_f1 = sem("rows_combined")
        s_v2 = sem("x2_var_ready")
        s_s2 = sem("x2_std_ready")
        s_n2 = sem("x2_scale_ready")
        s_nm = sem("x2_normed")
        s_u0 = sem("first_pick_weighted")
        s_x2 = sem("x2_scaled")
        s_fo = sem("out_ready")
        s_fs = [sem(f"out_stored{i}") for i in range(2)]

        with nc.Block() as block:
            @block.sync
            def _(sp):
                sp.dma_start(g2[:, :], mod_row(5)).then_inc(s_tb, 16)
                sp.dma_start(lg2[:, :], row(ln2_g[0])).then_inc(s_tb, 16)
                sp.dma_start(lb2[:, :], row(ln2_b[0])).then_inc(s_tb, 16)
                for b in range(2):
                    sp.dma_start(xf[b][:, :], x1_d[b * P:(b + 1) * P, :]).then_inc(s_xl[b], 16)
                with sp.Fori(0, NT // 2 - 1) as i:
                    for b in range(2):
                        t = i * 2 + b
                        sp.wait_ge(s_f1, t + 1)
                        sp.dma_start(xf[b][:, :], x1_d[ds((t + 2) * P, P), :]).then_inc(s_xl[b], 16)
                        sp.wait_ge(s_fo, t + 1)
                        sp.dma_start(y_prompt[0, ds(t * P, P), :], fo[b][:, :]).then_inc(s_fs[b], 16)
                sp.wait_ge(s_f1, NT - 1)
                sp.dma_start(xf[0][0:NS, :], x1_d[NT * P:NT * P + NS, :]).then_inc(s_xl[0], 16)
                sp.wait_ge(s_f1, NT)
                sp.dma_start(g2[0:NS, :], mod_d[0:NS, 5 * D:6 * D]).then_inc(s_g2s, 16)
                for b in range(2):
                    sp.wait_ge(s_fo, NT - 1 + b)
                    sp.dma_start(y_prompt[0, (NT - 2 + b) * P:(NT - 1 + b) * P, :], fo[b][:, :]).then_inc(s_fs[b], 16)
                sp.wait_ge(s_fo, NT + 1)
                sp.dma_start(y_sample[:, 0, :], fo[0][0:NS, :]).then_inc(s_fs[0], 16)
                sp.wait_ge(s_fs[0], 16 * (NT // 2 + 1))
                sp.wait_ge(s_fs[1], 16 * (NT // 2))

            @block.gpsimd
            def _(pool):
                ch = Chain(pool, s_chp)

                def gathers(t, b, rows=P):
                    if not (isinstance(t, int) and t < 2):
                        pool.wait_ge(s_f1, t - 1)
                    ch.link(nc.gpsimd.tensor_copy(idy[b][0:rows, :], dest_i[0:rows, ds(t, 1), :].rearrange("p a n -> p (a n)")))
                    for n, y in enumerate((ya, yb)):
                        nc.gpsimd.indirect_dma_start(out=y[b][0:rows, :], out_offset=None, in_=ye_d[:, :],
                                                     in_offset=bass.IndirectOffsetOnAxis(ap=idy[b][0:rows, n:n + 1], axis=0)).then_inc(s_ya[b], 16)
                    ch.restart()

                def add_bias(t, b, rows=P):
                    pool.wait_ge(s_x2, t + 1)
                    if not (isinstance(t, int) and t < 2):
                        pool.wait_ge(s_fs[b], (t - b) * 8)
                    nc.gpsimd.tensor_tensor(fo[b][0:rows, :], f_b[b][0:rows, :], lb2[0:rows, :], ALU.add).then_inc(s_fo, 1)

                pool.wait_ge(s_tb, 48)
                gathers(0, 0)
                gathers(1, 1)
                with pool.Fori(1, NT // 2) as i:
                    for b in range(2):
                        gathers(i * 2 + b, b)
                        add_bias(i * 2 + b - 2, b)
                gathers(NT, 0, NS)
                add_bias(NT - 2, 0)
                add_bias(NT - 1, 1)
                add_bias(NT, 0, NS)

            @block.vector
            def _(dve):
                ch = Chain(dve, s_chv)

                def weight(t, n, q):
                    return wt[q, ds(t, 1), n:n + 1].rearrange("p a n -> p (a n)")

                def combine(t, b, rows=P):
                    q = slice(0, rows)
                    dve.wait_ge(s_ya[b], (t - b) * 16 + 32)
                    dve.wait_ge(s_u0, t + 1)
                    ch.link(nc.vector.scalar_tensor_tensor(f_a[q, :], yb[b][q, :], weight(t, 1, q), ya[b][q, :], ALU.mult, ALU.add))
                    ch.link(nc.vector.tensor_tensor(f_a[q, :], f_a[q, :], g2[q, :], ALU.mult))
                    dve.wait_ge(s_xl[b], (t - b) * 8 + 16)
                    if not (isinstance(t, int) and t < 2):
                        dve.wait_ge(s_fo, t - 1)
                    ch.link(nc.vector.scalar_tensor_tensor(f_b[b][q, :], xf[b][q, :], ALPHA, f_a[q, :], ALU.mult, ALU.add))
                    dve.sem_inc(s_f1, 1)
                    for n in range(2):
                        ch.add(nc.vector.bn_stats(bs2[q, n, :], f_b[b][q, n * BANK:(n + 1) * BANK]))
                    ch.wait()
                    nc.vector.bn_aggr(mv2[b][q, :], bs2[q, :, :].rearrange("p a s -> p (a s)")).then_inc(s_v2, 1)

                def scale(t, b, rows=P):
                    q = slice(0, rows)
                    dve.wait_ge(s_nm, t + 1)
                    ch.link(nc.vector.tensor_tensor(f_b[b][q, :], f_b[b][q, :], lg2[q, :], ALU.mult))
                    dve.sem_inc(s_x2, 1)

                def moments(t, b, rows=P):
                    q = slice(0, rows)
                    dve.wait_ge(s_s2, t + 1)
                    ch.link(nc.vector.reciprocal(iv2[b][q, :], sd2[q, :]))
                    nc.vector.tensor_scalar(nb2[b][q, :], mv2[b][q, 0:1], iv2[b][q, 0:1], -1.0, ALU.mult, ALU.mult).then_inc(s_n2, 1)

                def tile(t, b):
                    combine(t, b)
                    if not is0(t):
                        scale(t - 1, 1 - b)
                    moments(t, b)
                    ch.restart()

                dve.wait_ge(s_tb, 48)
                ch.link(nc.vector.tensor_scalar_add(g2[:, :], g2[:, :], 1.0))
                tile(0, 0)
                tile(1, 1)
                with dve.Fori(1, NT // 2) as i:
                    for b in range(2):
                        tile(i * 2 + b, b)
                dve.wait_ge(s_g2s, 16)
                ch.link(nc.vector.tensor_scalar_add(g2[0:NS, :], g2[0:NS, :], 1.0))
                combine(NT, 0, NS)
                scale(NT - 1, 1)
                moments(NT, 0, NS)
                scale(NT, 0, NS)
                ch.restart()

            @block.scalar
            def _(act):
                def first_pick(t, b, rows=P):
                    act.wait_ge(s_ya[b], (t - b) * 16 + 32)
                    nc.scalar.activation(ya[b][0:rows, :], ya[b][0:rows, :], ACT.Copy,
                                         scale=wt[0:rows, ds(t, 1), 0:1].rearrange("p a n -> p (a n)")).then_inc(s_u0, 1)

                def norm(t, b, rows=P):
                    act.wait_ge(s_v2, t + 1)
                    nc.scalar.activation(sd2[0:rows, :], mv2[b][0:rows, 1:2], ACT.Sqrt, bias=eps[0:rows, :]).then_inc(s_s2, 1)
                    act.wait_ge(s_n2, t + 1)
                    nc.scalar.activation(f_b[b][0:rows, :], f_b[b][0:rows, :], ACT.Identity, bias=nb2[b][0:rows, :],
                                         scale=iv2[b][0:rows, :]).then_inc(s_nm, 1)

                first_pick(0, 0)
                for t in range(2):
                    first_pick(t + 1, 1 - t)
                    norm(t, t)
                with act.Fori(1, NT // 2 - 1) as i:
                    for b in range(2):
                        first_pick(i * 2 + b + 1, 1 - b)
                        norm(i * 2 + b, b)
                first_pick(NT - 1, 1)
                norm(NT - 2, 0)
                first_pick(NT, 0, NS)
                norm(NT - 1, 1)
                norm(NT, 0, NS)


_INS = ["x_prompt", "x_sample", "state_pool", "c_prompt", "c_sample", "w_ada", "b_ada", "w_in", "pool_w", "pool_scale",
        "sgu_norm_g", "sgu_w", "sgu_b", "w_out", "ln1_g", "ln1_b", "router_g_w", "router_g_b", "router_e_w",
        "router_e_b", "exp_w_gate", "exp_w_up", "exp_w_down", "ln2_g", "ln2_b"]
_OUTS = [(1, 2048, 1024), (8, 1, 1024), (1, 1, 15, 512), (1, 8, 15, 512), (1, 8, 1, 512)]


def kernel(**inputs):
    import numpy as _np
    import concourse.bacc as _bacc
    from concourse import mybir as _mybir
    from concourse.bass_utils import run_bass_kernel_spmd as _run

    nc = _bacc.Bacc("TRN2", target_bir_lowering=False, num_devices=1)
    arrays, args = {}, []
    for name in _INS:
        a = _np.ascontiguousarray(inputs[name])
        arrays[f"in_{name}_dram"] = a
        args.append(nc.dram_tensor(f"in_{name}_dram", a.shape, _mybir.dt.from_np(a.dtype), kind="ExternalInput").ap())
    for i, shape in enumerate(_OUTS):
        args.append(nc.dram_tensor(f"out_{i}_dram", shape, _mybir.dt.float32, kind="ExternalOutput").ap())
    hybrid_trunk(nc, *args)
    r = _run(nc, [arrays], core_ids=[0])
    return tuple(r.results[0][f"out_{i}_dram"] for i in range(len(_OUTS)))
```

```python
import concourse.bass as bass
from concourse import mybir
from contextlib import ExitStack

ALU = mybir.AluOpType
ACT = mybir.ActivationFunctionType
AX_X = mybir.AxisListType.X
F32 = mybir.dt.float32
F32R = mybir.dt.float32r
BF16 = mybir.dt.bfloat16
I32 = mybir.dt.int32
U32 = mybir.dt.uint32
ds = bass.ds

P = 128
BANK = 512
WINDOWS = (2, 4, 8, 16)
LN_EPS = 1e-5
ALPHA = 2.0 ** 0.25
BIG = 1.0e30


class Region:

    def __init__(self, nc, start, end):
        self.nc, self.at, self.end = nc, start, end

    def take(self, name, shape, dtype):
        n = mybir.dt.size(dtype)
        for s in shape[1:]:
            n *= s
        t = self.nc.alloc_sbuf_tensor_at(name, shape, dtype, offset=self.at)
        self.at += (n + 31) // 32 * 32
        assert self.at <= self.end, (name, self.at - self.end)
        return t


class Chain:

    def __init__(self, eng, sem):
        self.eng, self.sem, self.n = eng, sem, 0

    def add(self, ins):
        self.n += 1
        ins.then_inc(self.sem, 1)

    def wait(self):
        self.eng.wait_ge(self.sem, self.n)

    def link(self, ins):
        self.add(ins)
        self.wait()

    def restart(self):
        if self.n:
            self.wait()
            self.eng.sem_clear(self.sem)
            self.n = 0


def hybrid_trunk(nc, x_prompt, x_sample, state_pool, c_prompt, c_sample, w_ada, b_ada, w_in, pool_w, pool_scale,
                 sgu_norm_g, sgu_w, sgu_b, w_out, ln1_g, ln1_b, router_g_w, router_g_b, router_e_w, router_e_b,
                 exp_w_gate, exp_w_up, exp_w_down, ln2_g, ln2_b,
                 y_prompt, y_sample, pool_prompt, pool_sample, sgu_v):
    SEQ, D = x_prompt.shape[1:]
    NS = x_sample.shape[0]
    NT = SEQ // P
    KD = D // P
    DP = state_pool.shape[3]
    BUF = state_pool.shape[2]
    NG = pool_w.shape[1]
    NH = sgu_w.shape[1]
    NRG = router_g_w.shape[2]
    NE = router_e_w.shape[2]
    EPG = NE // NRG
    FE = exp_w_gate.shape[3]
    KF = FE // P
    NC = NS + 1
    NA = 3
    NR = NRG + NE
    NTT = NT + 1
    MAXB = (2 * (SEQ + NS) - NE) // P + NE + 1
    PAIRS = (MAXB + 2) // 2
    NB = 2 * PAIRS + 2
    assert D == 8 * P and DP == BANK and FE == BANK and NG == NH == 4 and NT % 2 == 0 and NB <= P

    xp = x_prompt[0]
    w_in_v = w_in[0].rearrange("(k p) n -> p k n", p=P)
    w_out_v = w_out[0].rearrange("(k p) n -> p k n", p=P)
    w_ada_v = w_ada[0].rearrange("(k p) (g n) -> k g p n", p=P, g=NA)
    gate_v = exp_w_gate[0].rearrange("e (k p) n -> e p k n", p=P)
    up_v = exp_w_up[0].rearrange("e (k p) n -> e p k n", p=P)
    down_v = exp_w_down[0].rearrange("e (k p) n -> e p k n", p=P)

    mod_d = nc.dram_tensor("mod_rows", [NC, 6 * D], F32).ap()
    mix_d = nc.dram_tensor("mixer_tiles", [NT * P, KD * P], F32).ap()
    h2_d = nc.dram_tensor("h2_rows", [SEQ + NS, D], F32).ap()
    x1_d = nc.dram_tensor("x1_rows", [SEQ + NS, D], F32).ap()
    ye_d = nc.dram_tensor("expert_rows", [NB * P, D], F32).ap()

    ctx = ExitStack()
    with ctx:
        sems = []

        def sem(name):
            sems.append(nc.alloc_semaphore(name=name))
            return sems[-1]

        def psum(name, cols=BANK):
            return ctx.enter_context(nc.psum_tensor(name, [P, cols], F32))

        base = (nc.sbuf_base + 127) // 128 * 128
        last = Region(nc, base, base + 21504)
        MIX0 = last.end
        W0 = MIX0 + 2 * KD * D * 4 + 64
        W1 = W0 + 3 * KD * FE * 4
        W2 = W1 + 3 * KD * FE * 4
        END = nc.sbuf_usable_end // 32 * 32 - KD * NS * 4

        ident = last.take("ident", [P, P], F32)
        ones = last.take("ones", [P, P], BF16)
        before = last.take("before", [P, P], BF16)
        iota = last.take("iota", [P, P], F32)
        iota_i = last.take("iota_i", [P, P], I32)
        pcol = last.take("pcol", [P, 1], F32)
        eps = last.take("eps", [P, 1], F32)
        cT = last.take("cT", [P, KD, NC], F32)
        cT_k = last.take("cT_k", [P, NC], F32)
        acc = last.take("acc", [P, NA, BANK], F32)
        rw = last.take("rw", [P, KD, NR], F32)
        rb = last.take("rb", [P, NR], F32)
        picked = last.take("picked", [P, NTT, 2, NE], F32)
        rank = last.take("rank", [P, NTT, 2], F32)
        tops = last.take("tops", [P, NTT, 3, 8], F32)
        top = last.take("top", [P, 3, 8], F32)
        seen = last.take("seen", [P, NE], F32)
        seen_b = last.take("seen_b", [P, NE], BF16)
        wt = last.take("wt", [P, NTT, 2], F32)
        dest_i = last.take("dest_i", [P, NTT, 2], I32)
        cum_f = last.take("cum_f", [P, NE], F32)
        cum_i = last.take("cum_i", [1, NE], I32)
        blk_e = last.take("blk_e", [1, NB], I32)
        tok_i = last.take("tok_i", [P, NB], I32)

        mixT_s = nc.alloc_sbuf_tensor_at("mixT_s", [P, KD, NS], F32, offset=END)
        ada0 = nc.alloc_sbuf_tensor_at("ada0", [P, KD, 4 * BANK], F32, offset=MIX0)

        r = Region(nc, MIX0, END)
        wi_hi = [r.take(f"wi_hi{k}", [P, 3 * BANK], F32R) for k in range(KD)]
        wi_lo = [r.take(f"wi_lo{k}", [P, 3 * BANK], F32R) for k in range(KD)]
        x_t = [r.take(f"x_t{i}", [P, D], F32) for i in range(2)]
        h_t = r.take("h_t", [P, D], F32)
        hT_place = r.at + D * 4
        hT_hi = [r.take(f"hT_hi{i}", [P, KD, P], F32R) for i in range(2)]
        hT_lo = [r.take(f"hT_lo{i}", [P, KD, P], F32R) for i in range(2)]
        RING = KD // 2
        w_in_raw = nc.alloc_sbuf_tensor_at("w_in_raw", [P, RING, 3 * BANK], F32, offset=r.at)
        ring_end = r.at + RING * 3 * BANK * 4
        ada_st = [r.take(f"ada_st{i}", [P, 4 * BANK], F32) for i in range(2)]
        mix_o = r.take("mix_o", [P, KD, P], F32)
        vn = r.take("vn", [P, DP], F32)
        g_place = r.at
        g_sb = r.take("g_sb", [P, DP], F32)
        assert r.at == ring_end
        sc1 = r.take("sc1", [P, D], F32)
        sh1 = r.take("sh1", [P, D], F32)
        sg_bc = r.take("sg_bc", [P, DP], F32)
        p_sb = [r.take(f"p_sb{i}", [P, DP], F32) for i in range(2)]
        u_place = r.at
        u_sb = r.take("u_sb", [P, DP], F32)
        dT = r.take("dT", [P, NG, P], F32)
        band = r.take("band", [P, NG, P], F32)
        band0 = r.take("band0", [P, NG, P], F32)
        bandp = r.take("bandp", [P, NG, P], F32)
        vstat = r.take("vstat", [P, NH, 6], F32)
        vmv = r.take("vmv", [P, NH, 2], F32)
        vstd = r.take("vstd", [P, NH], F32)
        vinv = r.take("vinv", [P, NH], F32)
        bt = r.take("bt", [P, NH], F32)
        psc = r.take("psc", [P, NG], F32)
        b0s = r.take("b0s", [P, NH], F32)
        w0s = r.take("w0s", [P, NH], F32)
        wsT = r.take("wsT", [P, NH, P], F32)
        pw = r.take("pw", [P, NG, P], F32)
        invc = r.take("invc", [P, P], F32)
        z_place = r.at
        zrow = r.take("zrow", [P, D], F32)
        wst_raw = nc.alloc_sbuf_tensor_at("wst_raw", [P, NH, P], F32, offset=MIX0 + KD * 4 * BANK * 4)
        c_raw = nc.alloc_sbuf_tensor_at("c_raw", [NC, D], F32, offset=MIX0 + KD * 4 * BANK * 4 + 4096)
        rs = Region(nc, MIX0 + KD * 4 * BANK * 4 + 2 * D * 4, MIX0 + 2 * KD * 3 * BANK * 4)
        hist_len = [w - 1 for w in WINDOWS]
        hist = [rs.take(f"hist{g}", [NS, hist_len[g], P], F32) for g in range(NG)]
        sel = rs.take("sel", [P, P], F32)
        hsum = r.take("hsum", [NS, DP], F32)
        p_s = r.take("p_s", [NS, DP], F32)
        hT_s = [r.take(f"hT_s{i}", [P, KD, NS], F32R) for i in range(2)]
        dT_s = r.take("dT_s", [P, NG, NS], F32)
        stat_s = r.take("stat_s", [NS, NH * 10], F32)

        def place_of(name, t, shape):
            return nc.alloc_sbuf_tensor_at(name, shape, F32, offset=places[t])

        places = {"hT_hi1": hT_place, "hT_lo1": hT_place + 2 * D * 4, "x_t1": MIX0 + 2 * KD * 3 * BANK * 4 + D * 4,
                  "u_dT": u_place, "zrow": z_place, "g_sb": g_place}
        x_s = place_of("x_s", "hT_hi1", [NS, D])
        h_s = place_of("h_s", "hT_lo1", [NS, D])
        sc1_s = place_of("sc1_s", "u_dT", [NS, D])
        sh1_s = place_of("sh1_s", "x_t1", [NS, D])
        uv_s = place_of("uv_s", "zrow", [NS, 2, DP])
        g_s = place_of("g_s", "g_sb", [NS, DP])

        EARLY = 2
        r = Region(nc, MIX0, W0)
        wo_hi = [r.take(f"wo_hi{k}", [P, D], F32R) for k in range(KD)]
        wo_lo = [r.take(f"wo_lo{k}", [P, D], F32R) for k in range(KD)]
        w_out_raw = nc.alloc_sbuf_tensor_at("w_out_raw", [P, KD, D], F32, offset=W0)
        OH0 = END - NTT * 2 * P * 2
        oh_lo = nc.alloc_sbuf_tensor_at("oh_lo", [P, NTT, 2, P], BF16, offset=OH0)
        small = Region(nc, W0 + EARLY * 2 * 2 * FE * 4, OH0)
        g1_s = small.take("g1_s", [NS, D], F32)
        sc2_s = small.take("sc2_s", [NS, D], F32)
        sh2_s = small.take("sh2_s", [NS, D], F32)
        tmp_s = small.take("tmp_s", [NS, D], F32)
        assert small.at == W0 + KD * D * 4
        g1 = small.take("g1", [P, D], F32)
        sc2 = small.take("sc2", [P, D], F32)
        sh2 = small.take("sh2", [P, D], F32)
        lg1 = small.take("lg1", [P, D], F32)
        lb1 = small.take("lb1", [P, D], F32)
        x_r = [small.take(f"x_r{i}", [P, D], F32) for i in range(2)]
        t_r = small.take("t_r", [P, D], F32)
        x1 = [small.take(f"x1_{i}", [P, D], F32) for i in range(2)]
        h2 = [small.take(f"h2_{i}", [P, D], F32) for i in range(2)]
        h2T = small.take("h2T", [P, KD, P], F32)
        mix_r = [small.take(f"mix_r{i}", [P, KD, P], F32) for i in range(2)]
        mix_hi = [small.take(f"mix_hi{i}", [P, KD, P], F32R) for i in range(2)]
        mix_lo = [small.take(f"mix_lo{i}", [P, KD, P], F32R) for i in range(2)]
        nb1 = small.take("nb1", [P, 1], F32)
        rk_i = small.take("rk_i", [P, 2], I32)
        lo_i = small.take("lo_i", [P, 2], I32)
        lo_f = small.take("lo_f", [P, 2], F32)
        bst = small.take("bst", [P, 2, 6], F32)
        mv = small.take("mv", [P, 2], F32)
        std = small.take("std", [P, 1], F32)
        inv = small.take("inv", [P, 1], F32)
        lgT = small.take("lgT", [P, P], F32)
        el = small.take("el", [P, NE], F32)
        gidx = small.take("gidx", [P, 8], U32)
        gidf = small.take("gidf", [P, 1], F32)
        gm = small.take("gm", [P, NRG], F32)
        eidx = small.take("eidx", [P, 8], U32)
        eidf = small.take("eidf", [P, 2], F32)
        m_b = small.take("m_b", [P, NE], BF16)
        rk = small.take("rk", [P, 2, NE], F32)

        UNIT = 2 * FE
        GU, DN = KD, KF
        NU = GU + DN
        LOW_UNITS = 6
        BLK_END = W0 - LOW_UNITS * UNIT * 4
        r = Region(nc, MIX0, BLK_END)
        pos = r.take("pos", [P, NTT, 2, NE], F32)
        cnt = r.take("cnt", [P, NE], F32)
        cnt_i = r.take("cnt_i", [P, NE], I32)
        nblk = r.take("nblk", [P, NE], F32)
        first = r.take("first", [P, NE], F32)
        zero = r.take("zero", [P, NE], F32)
        dest = r.take("dest", [P, NTT * 2], F32)
        hi_i = r.take("hi_i", [P, NTT * 2], I32)
        hi_f = r.take("hi_f", [P, NTT * 2], F32)
        oh_blk = r.take("oh_blk", [P, NTT * 2, NB], BF16)
        oh_hi = r.take("oh_hi", [P, NTT * 2, 2, NB], BF16)
        tile_f = r.take("tile_f", [P, NTT * 2], F32)
        tile_i = r.take("tile_i", [P, NTT * 2], I32)
        cmp = r.take("cmp", [1, NB, NE], F32)
        blk_f = r.take("blk_f", [1, NB], F32)
        ex = r.take("ex", [P, NTT], F32)
        tok_a = r.take("tok_a", [P, 2, NB], F32)
        gd = r.take("gd", [P, NTT, 8], F32)
        gsum = r.take("gsum", [P, NTT], F32)
        den = r.take("den", [P, NTT], F32)

        wraw = nc.alloc_sbuf_tensor_at("wraw", [P, NU, UNIT], F32, offset=W0)
        lows = Region(nc, BLK_END, W0)
        highs = Region(nc, W0 + NU * UNIT * 4, END)
        halves = [(lows if n < LOW_UNITS else highs).take(f"w_half{n}", [P, UNIT], F32R) for n in range(2 * NU)]
        w_hi, w_lo = halves[0::2], halves[1::2]
        r = Region(nc, MIX0, BLK_END)
        xg = [r.take(f"xg{i}", [P, D], F32) for i in range(2)]
        xT_hi = [r.take(f"xT_hi{i}", [P, KD, P], F32R) for i in range(2)]
        xT_lo = [r.take(f"xT_lo{i}", [P, KD, P], F32R) for i in range(2)]
        sgate = r.take("sgate", [P, FE], F32)
        act_t = r.take("act_t", [P, FE], F32)
        actT_hi = r.take("actT_hi", [P, KF, P], F32R)
        actT_lo = r.take("actT_lo", [P, KF, P], F32R)
        y_sb = [r.take(f"y_sb{i}", [P, D], F32) for i in range(2)]
        idx = [r.take(f"idx{i}", [P, 1], I32) for i in range(2)]

        r = Region(nc, W0, END)
        LB = 4
        xf = [r.take(f"xf{i}", [P, D], F32) for i in range(LB)]
        g2 = r.take("g2", [P, D], F32)
        lg2 = r.take("lg2", [P, D], F32)
        lb2 = r.take("lb2", [P, D], F32)
        assert r.at <= W0 + NU * UNIT * 4
        ya = [r.take(f"ya{i}", [P, D], F32) for i in range(LB)]
        yb = [r.take(f"yb{i}", [P, D], F32) for i in range(LB)]
        f_b = [r.take(f"f_b{i}", [P, D], F32) for i in range(LB)]
        fo = [r.take(f"fo{i}", [P, D], F32) for i in range(2)]
        f_a = r.take("f_a", [P, D], F32)
        dg = [[r.take(f"dg{i}_{n}", [P, P], F32) for n in range(2)] for i in range(LB)]
        idy = [r.take(f"idy{i}", [P, 2], I32) for i in range(LB)]
        bs2 = r.take("bs2", [P, 2, 6], F32)
        mv2 = [r.take(f"mv2_{i}", [P, 2], F32) for i in range(2)]
        sd2 = r.take("sd2", [P, 1], F32)
        iv2 = [r.take(f"iv2_{i}", [P, 1], F32) for i in range(2)]
        nb2 = [r.take(f"nb2_{i}", [P, 1], F32) for i in range(2)]

        ps2 = [ctx.enter_context(nc.psum_tensor(f"ps2_{i}", [P, 2 * BANK], F32)) for i in range(4)]
        bank = [ps2[i // 2][:, (i % 2) * BANK:(i % 2 + 1) * BANK] for i in range(8)]

        def mod_row(j):
            return mod_d[NS:NS + 1, j * D:(j + 1) * D].partition_broadcast(P)

        def is0(s):
            return isinstance(s, int) and s == 0

        def row(v, n=P):
            return v.rearrange("(a n) -> a n", a=1).partition_broadcast(n)

        s_small = sem("small_loaded")
        s_ws = sem("sgu_w_loaded")
        s_c = sem("c_loaded")
        s_win = [sem(f"w_in_loaded{k}") for k in range(RING)]
        s_ada0 = [sem(f"ada0_loaded{k}") for k in range(KD)]
        s_const = sem("constants_built")
        s_chp = sem("pool_chain")
        s_chv = sem("vector_chain")
        s_cha = sem("scalar_chain")
        s_cs = sem("c_silu")
        s_cTp = sem("cT_in_psum")
        s_cT = sem("cT_ready")
        s_wsp = sem("wsT_in_psum")
        s_wsT = sem("wsT_ready")
        s_adap = sem("ada_in_psum")
        s_modr = sem("mod_rows_ready")
        s_mods = sem("mod_rows_stored")
        s_wih = sem("w_in_hi_ready")
        s_wil = sem("w_in_lo_ready")
        SETUP_UNITS = 2

        def split_w_in_hi(act, k):
            act.wait_ge(s_win[k % RING], k // RING * 16 + 16)
            nc.scalar.copy(wi_hi[k][:, :], w_in_raw[:, k % RING, :]).then_inc(s_wih, 1)

        def split_w_in_lo(dve, k):
            dve.wait_ge(s_wih, k + 1)
            nc.vector.tensor_tensor(wi_lo[k][:, :], w_in_raw[:, k % RING, :], wi_hi[k][:, :].bitcast(F32),
                                    ALU.subtract).then_inc(s_wil, 1)
        s_hist = sem("history_loaded")
        s_modb = sem("shift1_scale1_in_psum")
        s_sh1 = sem("shift1_ready")
        s_sc1 = sem("scale1_ready")
        s_x = [sem(f"x_loaded{i}") for i in range(2)]

        with nc.Block() as block:
            @block.sync
            def _(sp):
                sp.dma_start(c_raw[0:NS, :], c_sample).then_inc(s_c, 16)
                sp.dma_start(c_raw[NS:NC, :], c_prompt).then_inc(s_c, 16)
                for k in range(KD):
                    if k >= 3:
                        sp.wait_ge(s_ada0[k - 3], 16)
                    sp.dma_start(ada0[:, k, :], w_ada_v[k, 0]).then_inc(s_ada0[k], 16)
                    if k == 2:
                        for g in range(NG):
                            sp.dma_start(hist[g][:, :, :],
                                         state_pool[0, :, BUF - hist_len[g]:BUF, g * P:(g + 1) * P]).then_inc(s_hist, 16)
                for k in range(2):
                    sp.wait_ge(s_ada0[KD - 2 + k], 16)
                    sp.dma_start(w_in_raw[:, k, :], w_in_v[:, k, :]).then_inc(s_win[k], 16)
                sp.dma_start(x_t[0][:, :], xp[0:P, :]).then_inc(s_x[0], 16)
                sp.wait_ge(s_modr, 1)
                for j in range(4):
                    sp.dma_start(mod_d[:, j * BANK:(j + 1) * BANK], acc[32 * j:32 * j + NC, 0, :]).then_inc(s_mods, 16)
                for k in range(2, RING):
                    sp.dma_start(w_in_raw[:, k, :], w_in_v[:, k, :]).then_inc(s_win[k], 16)
                for k in range(RING, RING + SETUP_UNITS):
                    sp.wait_ge(s_wil, k - RING + 1)
                    sp.dma_start(w_in_raw[:, k - RING, :], w_in_v[:, k, :]).then_inc(s_win[k - RING], 16)
                sp.wait_ge(s_mods, 64)

            @block.scalar
            def _(act):
                act.dma_start(wst_raw[:, :, :], sgu_w[0].rearrange("h t s -> t h s")).then_inc(s_ws, 16)
                act.wait_ge(s_c, 32)
                nc.scalar.activation(c_raw[:, :], c_raw[:, :], ACT.Silu).then_inc(s_cs, 1)
                for g in range(NA):
                    if g == 1:
                        act.wait_ge(s_cTp, 1)
                        nc.scalar.copy(cT[:, :, :],
                                       bank[0][:, 0:KD * NC].rearrange("p (k c) -> p k c", c=NC)).then_inc(s_cT, 1)
                        act.wait_ge(s_wsp, 1)
                        nc.scalar.copy(wsT[:, :, :], bank[1].rearrange("p (h s) -> p h s", s=P)).then_inc(s_wsT, 1)
                    for j in range(4):
                        at = (4 * g + j) * BANK
                        act.dma_start(acc[32 * j:32 * j + NC, g, :],
                                      row(b_ada[0, at:at + BANK], NC)).then_inc(s_small, 16)
                act.dma_start(pw[:, :, :], pool_w[0].rearrange("g c d -> c g d")).then_inc(s_small, 16)
                act.dma_start(psc[:, :], pool_scale[0].rearrange("(g d) -> d g", g=NG),
                              allow_slow_non_contiguous=True).then_inc(s_small, 16)
                act.dma_start(bt[:, :], sgu_b[0].rearrange("h t -> t h"),
                              allow_slow_non_contiguous=True).then_inc(s_small, 16)
                act.dma_start(b0s[0:NS, :], sgu_b[0, :, 0:1].rearrange("h a -> a h").partition_broadcast(NS),
                              allow_slow_non_contiguous=True).then_inc(s_small, 16)
                act.dma_start(w0s[0:NS, :], sgu_w[0, :, 0, 0:1].rearrange("h a -> a h").partition_broadcast(NS),
                              allow_slow_non_contiguous=True).then_inc(s_small, 16)
                act.dma_start(sg_bc[:, :], row(sgu_norm_g[0])).then_inc(s_small, 16)
                act.dma_start(rw[:, :, 0:NRG], router_g_w[0].rearrange("(k p) n -> p k n", p=P)).then_inc(s_small, 16)
                act.dma_start(rw[:, :, NRG:NR], router_e_w[0].rearrange("(k p) n -> p k n", p=P)).then_inc(s_small, 16)
                act.dma_start(rb[:, 0:NRG], row(router_g_b[0])).then_inc(s_small, 16)
                act.dma_start(rb[:, NRG:NR], row(router_e_b[0])).then_inc(s_small, 16)
                act.wait_ge(s_adap, 1)
                for k in range(SETUP_UNITS):
                    split_w_in_hi(act, k)
                act.wait_ge(s_modb, 1)
                nc.scalar.copy(sh1[:, :], ps2[2][:, :]).then_inc(s_sh1, 1)

            @block.gpsimd
            def _(pool):
                ch = Chain(pool, s_chp)
                ch.add(nc.gpsimd.memset(ident[:, :], 0.0))
                ch.add(nc.gpsimd.memset(before[:, :], 1.0))
                ch.add(nc.gpsimd.memset(ones[:, :], 1.0))
                for g, w in enumerate(WINDOWS):
                    ch.add(nc.gpsimd.memset(band[:, g, :], 1.0))
                    ch.add(nc.gpsimd.memset(bandp[:, g, :], 1.0 / w))
                ch.add(nc.gpsimd.iota(iota_i[:, :], pattern=[[1, P]], base=0, channel_multiplier=0))
                ch.add(nc.gpsimd.memset(p_sb[1][:, :], 0.0))
                ch.add(nc.gpsimd.memset(picked[:, NT, :, :], 0.0))
                ch.add(nc.gpsimd.memset(rank[:, NT, :], 0.0))
                ch.add(nc.gpsimd.memset(tops[:, NT, :, :], 0.0))
                ch.add(nc.gpsimd.memset(top[:, :, :], -BIG))
                ch.add(nc.gpsimd.memset(seen[:, :], 0.0))
                ch.add(nc.gpsimd.memset(seen_b[:, :], 0.0))
                ch.add(nc.gpsimd.memset(eps[:, :], LN_EPS))
                ch.wait()
                ch.add(nc.gpsimd.affine_select(out=ident[:, :], in_=ident[:, :], compare_op=ALU.not_equal, fill=1.0,
                                               base=0, pattern=[[-1, P]], channel_multiplier=1))
                ch.add(nc.gpsimd.affine_select(out=before[:, :], in_=before[:, :], compare_op=ALU.is_gt, fill=0.0,
                                               base=0, pattern=[[1, P]], channel_multiplier=-1))
                for g, w in enumerate(WINDOWS):
                    ch.add(nc.gpsimd.affine_select(out=bandp[:, g, :], in_=bandp[:, g, :], compare_op=ALU.is_ge,
                                                   fill=0.0, base=w - 1 - P, pattern=[[-1, P]], channel_multiplier=1))
                    ch.link(nc.gpsimd.affine_select(out=band[:, g, :], in_=band[:, g, :], compare_op=ALU.is_ge,
                                                    fill=0.0, base=0, pattern=[[1, P]], channel_multiplier=-1))
                    ch.add(nc.gpsimd.affine_select(out=band[:, g, :], in_=band[:, g, :], compare_op=ALU.is_ge,
                                                   fill=0.0, base=w - 1, pattern=[[-1, P]], channel_multiplier=1))
                ch.link(nc.gpsimd.memset(sel[:, :], 0.0))
                for j in range(4):
                    ch.link(nc.gpsimd.affine_select(out=sel[:, :], in_=sel[:, :], compare_op=ALU.not_equal, fill=1.0,
                                                    base=-(32 * j + NS), pattern=[[0, P]], channel_multiplier=1))
                pool.sem_inc(s_const, 1)
                pool.wait_ge(s_wsT, 1)
                nc.gpsimd.affine_select(out=wsT[:, :, :], in_=wsT[:, :, :], compare_op=ALU.is_ge, fill=0.0,
                                        base=0, pattern=[[0, NH], [1, P]], channel_multiplier=-1).then_inc(s_const, 1)
                pool.wait_ge(s_const, 2)
                ch.restart()

            @block.vector
            def _(dve):
                ch = Chain(dve, s_chv)
                dve.wait_ge(s_const, 1)
                ch.link(nc.vector.tensor_copy(iota[:, :], iota_i[:, :]))
                for g, w in enumerate(WINDOWS):
                    ch.link(nc.vector.tensor_scalar(invc[:, :], iota[:, :], 1.0, float(w), ALU.add, ALU.min))
                    ch.link(nc.vector.reciprocal(invc[:, :], invc[:, :]))
                    ch.link(nc.vector.tensor_tensor(band0[:, g, :], band[:, g, :], invc[:, :], ALU.mult))
                    ch.add(nc.vector.tensor_tensor(band0[:, g, :], band0[:, g, :], ident[:, :], ALU.subtract))
                    ch.add(nc.vector.scalar_tensor_tensor(band[:, g, :], band[:, g, :], 1.0 / w, ident[:, :],
                                                          ALU.mult, ALU.subtract))
                dve.wait_ge(s_hist, 16 * NG)
                for g in range(NG):
                    ch.add(nc.vector.tensor_reduce(hsum[:, g * P:(g + 1) * P],
                                                   hist[g][:, :, :].rearrange("b w c -> b c w"), AX_X, ALU.add))
                dve.wait_ge(s_small, 16 * (4 * NA + 10))
                dve.wait_ge(s_adap, 1)
                for j in range(4):
                    q = slice(32 * j, 32 * j + NC)
                    ch.add(nc.vector.tensor_tensor(acc[q, 0, :], bank[2][q, :], acc[q, 0, :], ALU.add))
                ch.restart()
                dve.sem_inc(s_modr, 1)
                for k in range(SETUP_UNITS):
                    split_w_in_lo(dve, k)
                dve.wait_ge(s_modb, 2)
                nc.vector.tensor_scalar_add(sc1[:, :], ps2[3][:, :], 1.0).then_inc(s_sc1, 1)

            @block.tensor
            def _(pe):
                pe.wait_ge(s_const, 1)
                pe.wait_ge(s_ws, 16)
                for h in range(NH):
                    ins = nc.tensor.transpose(bank[1][:, h * P:(h + 1) * P], wst_raw[:, h, :], ident[:, :])
                ins.then_inc(s_wsp, 1)
                pe.wait_ge(s_cs, 1)
                for k in range(KD):
                    ins = nc.tensor.transpose(bank[0][:, k * NC:(k + 1) * NC], c_raw[:, k * P:(k + 1) * P],
                                              ident[0:NC, 0:NC])
                ins.then_inc(s_cTp, 1)
                pe.wait_ge(s_cT, 1)
                for k in range(KD):
                    pe.wait_ge(s_ada0[k], 16)
                    for j in range(4):
                        ins = nc.tensor.matmul(bank[2][32 * j:32 * j + NC, :], cT[:, k, :],
                                               ada0[:, k, j * BANK:(j + 1) * BANK], start=(k == 0), stop=(k == KD - 1))
                ins.then_inc(s_adap, 1)
                pe.wait_ge(s_modr, 1)
                for j in range(4):
                    q = slice(32 * j, 32 * j + NC)
                    ins = nc.tensor.matmul(bank[4 + j], sel[q, :], acc[q, 0, :], start=True, stop=True)
                    if j % 2:
                        ins.then_inc(s_modb, 1)

        s_adal = [sem(f"ada_loaded{i}") for i in range(2)]
        s_ck = sem("c_tile_ready")
        s_h = sem("h_ready")
        s_hTp = sem("hT_in_psum")
        s_hTh = sem("hT_hi_ready")
        s_hT = sem("hT_ready")
        s_pp = sem("p_in_psum")
        s_up = sem("u_in_psum")
        s_vp = sem("v_in_psum")
        s_p = sem("p_saved")
        s_u = sem("u_saved")
        s_bd = sem("band_done")
        s_dT = sem("dT_saved")
        s_am = sem("pool_mm_done")
        s_a = sem("a_saved")
        s_var = sem("v_var_ready")
        s_std = sem("v_std_ready")
        s_vn = sem("vn_ready")
        s_z = sem("z_done")
        s_g = sem("g_ready")
        s_gTp = sem("gT_in_psum")
        s_gT = sem("gT_saved")
        s_ad = sem("ada_unit_done")
        s_aa = sem("ada_unit_added")
        s_ps = sem("pool_state_stored")
        s_sld = sem("sample_rows_loaded")
        s_ssc = sem("sample_scale1_ready")
        s_sh = sem("sample_h_ready")
        s_shTp = sem("sample_hT_in_psum")
        s_shTh = sem("sample_hT_hi_ready")
        s_shT = sem("sample_hT_ready")
        s_sin = sem("sample_projection_in_psum")
        s_sp = sem("sample_p_saved")
        s_su = sem("sample_u_saved")
        s_svar = sem("sample_v_var_ready")
        s_sstd = sem("sample_v_std_ready")
        s_svn = sem("sample_vn_ready")
        s_sd = sem("sample_d_ready")
        s_sdp = sem("sample_dT_in_psum")
        s_sdT = sem("sample_dT_ready")
        s_sam = sem("sample_pool_mm_done")
        s_sa = sem("sample_a_saved")
        s_sg = sem("sample_g_ready")
        s_sgp = sem("sample_gT_in_psum")
        s_sgT = sem("sample_gT_saved")
        s_vs = sem("sample_states_stored")
        s_woh = sem("w_out_hi_ready")
        s_wol = sem("w_out_lo_ready")
        s_wo = [sem(f"w_out_loaded{k}") for k in range(KD // 2)]
        s_zf = sem("spare_blocks_zeroed")
        s_zr = sem("zero_rows_ready")
        s_mos = sem("mixer_tile_stored")
        PER = (NB - NE) // NT

        with nc.Block() as block:
            @block.gpsimd
            def _(pool):
                def zero_block(n):
                    pool.dma_start(ye_d[ds((n + NE) * P, P), :], zrow[:, :]).then_inc(s_zf, 16)

                pool.wait_ge(s_sgp, 1)
                pool.wait_ge(s_sg, 1)
                pool.wait_ge(s_vs, 32)
                nc.gpsimd.memset(zrow[:, :], 0.0).then_inc(s_zr, 1)
                pool.wait_ge(s_zr, 1)
                for n in range(NT * PER, NB - NE):
                    zero_block(n)
                with pool.Fori(0, NT) as t:
                    for n in range(PER):
                        zero_block(t * PER + n)
                    pool.wait_ge(s_a, t + 1)
                    pool.wait_ge(s_gT, t + 1)
                    pool.dma_start(mix_d[ds(t * P, P), :], mix_o[:, :, :].rearrange("p k c -> p (k c)")).then_inc(s_mos, 16)
                pool.wait_ge(s_zf, 16 * (NB - NE))
                pool.wait_ge(s_mos, 16 * NT)

            @block.sync
            def _(sp):
                sp.dma_start(x_s[:, :], x_sample[:, 0, :]).then_inc(s_sld, 16)
                sp.dma_start(sh1_s[:, :], mod_d[0:NS, 0:D]).then_inc(s_sld, 16)
                sp.dma_start(sc1_s[:, :], mod_d[0:NS, D:2 * D]).then_inc(s_sld, 16)
                for k in range(RING + SETUP_UNITS, KD):
                    sp.wait_ge(s_wil, k - RING + 1)
                    sp.dma_start(w_in_raw[:, k - RING, :], w_in_v[:, k, :]).then_inc(s_win[k - RING], 16)
                sp.wait_ge(s_sh, 1)
                sp.dma_start(x_t[1][:, :], xp[P:2 * P, :]).then_inc(s_x[1], 16)
                sp.wait_ge(s_wil, KD)
                for t in range(2):
                    sp.dma_start(ada_st[t][:, :], w_ada_v[0, 1 + t]).then_inc(s_adal[t], 16)

                sp.dma_start(pool_sample[0, :, 0:BUF - 1, :], state_pool[0, :, 1:BUF, :]).then_inc(s_ps, 16)
                sp.wait_ge(s_sp, 1)
                sp.dma_start(pool_sample[0, :, BUF - 1, :], p_s[:, :]).then_inc(s_vs, 16)
                sp.wait_ge(s_svn, 1)
                sp.dma_start(sgu_v[0, :, 0, :], uv_s[:, 1, :]).then_inc(s_vs, 16)

                with sp.Fori(0, NT // 2 - 1) as i:
                    for b in range(2):
                        sp.wait_ge(s_h, i * 2 + b + 1)
                        sp.dma_start(x_t[b][:, :], xp[ds((i * 2 + b + 2) * P, P), :]).then_inc(s_x[b], 16)
                        sp.wait_ge(s_ad, i * 2 + b + 1)
                        sp.dma_start(ada_st[b][:, :], w_ada_v[ds(i + 1, 1), 1 + b].rearrange("a p n -> p (a n)")).then_inc(s_adal[b], 16)
                sp.wait_ge(s_vp, NT)
                for k in range(KD // 2):
                    sp.dma_start(w_out_raw[:, 2 * k:2 * k + 2, :], w_out_v[:, 2 * k:2 * k + 2, :]).then_inc(s_wo[k], 16)
                sp.wait_ge(s_p, NT)
                sp.dma_start(pool_prompt[0, 0], p_sb[(NT - 1) % 2][P - BUF:P, :]).then_inc(s_ps, 16)
                sp.wait_ge(s_aa, NT)
                for g in range(1, NA):
                    for j in range(4):
                        at = (4 * g + j) * BANK
                        sp.dma_start(mod_d[:, at:at + BANK], acc[32 * j:32 * j + NC, g, :]).then_inc(s_mods, 16)
                sp.wait_ge(s_mods, 64 * NA)
                sp.wait_ge(s_ps, 32)

            @block.tensor
            def _(pe):
                def sample_projections():
                    pe.wait_ge(s_sh, 1)
                    for k in range(KD):
                        ins = nc.tensor.transpose(bank[7][:, k * NS:(k + 1) * NS], h_s[:, k * P:(k + 1) * P],
                                                  ident[0:NS, 0:NS])
                    ins.then_inc(s_shTp, 1)
                    pe.wait_ge(s_shT, 1)
                    for k in range(KD):
                        pe.wait_ge(s_wil, k + 1)
                        for m, (a, w) in enumerate(((0, wi_hi), (0, wi_lo), (1, wi_hi))):
                            for part in range(3):
                                ins = nc.tensor.matmul(bank[5 + part][0:NS, :], hT_s[a][:, k, :],
                                                       w[k][:, part * BANK:(part + 1) * BANK],
                                                       start=(k == 0 and m == 0), stop=(k == KD - 1 and m == 2))
                    ins.then_inc(s_sin, 1)

                def sample_d_transposes():
                    pe.wait_ge(s_sd, 1)
                    pe.wait_ge(s_sp, 1)
                    for g in range(NG):
                        ins = nc.tensor.transpose(bank[5][:, g * NS:(g + 1) * NS], hsum[:, g * P:(g + 1) * P],
                                                  ident[0:NS, 0:NS])
                    ins.then_inc(s_sdp, 1)

                def sample_pool_linear():
                    pe.wait_ge(s_sdT, 1)
                    pe.wait_ge(s_svn, 1)
                    for g in range(NG):
                        ins = nc.tensor.matmul(bank[7][:, g * NS:(g + 1) * NS], pw[:, g, :], dT_s[:, g, :],
                                               start=True, stop=True)
                    ins.then_inc(s_sam, 1)

                def sample_g_transposes():
                    pe.wait_ge(s_sg, 1)
                    for h in range(NH):
                        ins = nc.tensor.transpose(bank[5][:, (NG + h) * NS:(NG + h + 1) * NS], g_s[:, h * P:(h + 1) * P],
                                                  ident[0:NS, 0:NS])
                    ins.then_inc(s_sgp, 1)

                def h_transposes(t, b, rows=P):
                    pe.wait_ge(s_h, t + 1)
                    if not (isinstance(t, int) and t == 0):
                        pe.wait_ge(s_hT, t)
                    for k in range(KD):
                        ins = nc.tensor.transpose(ps2[0][:, k * P:k * P + rows], h_t[0:rows, k * P:(k + 1) * P],
                                                  ident[0:rows, 0:rows])
                    ins.then_inc(s_hTp, 1)

                def project(t, b, part, out, signal, free, rows=P):
                    if free is not None:
                        pe.wait_ge(free, t)
                    q = slice(part * BANK, (part + 1) * BANK)
                    for k in range(KD):
                        for m, (a, w) in enumerate(((hT_hi, wi_hi), (hT_hi, wi_lo), (hT_lo, wi_hi))):
                            ins = nc.tensor.matmul(out[0:rows, :], a[b][:, k, 0:rows], w[k][:, q],
                                                   start=(k == 0 and m == 0), stop=(k == KD - 1 and m == 2))
                    ins.then_inc(signal, 1)

                def bands(t, b, mats):
                    pe.wait_ge(s_p, t + 1)
                    if is0(t):
                        pe.wait_ge(s_sgT, 1)
                    else:
                        pe.wait_ge(s_gT, t)
                    for g in range(NG):
                        q = slice(g * P, (g + 1) * P)
                        nc.tensor.matmul(bank[5][:, q], p_sb[b][:, q], mats[:, g, :], start=True, stop=False)
                        ins = nc.tensor.matmul(bank[5][:, q], p_sb[1 - b][:, q], bandp[:, g, :], start=False, stop=True)
                    ins.then_inc(s_bd, 1)

                def pool_linear(t):
                    pe.wait_ge(s_dT, t + 1)
                    if is0(t):
                        pe.wait_ge(s_sa, 1)
                    else:
                        pe.wait_ge(s_a, t)
                    for g in range(NG):
                        ins = nc.tensor.matmul(bank[7][:, g * P:(g + 1) * P], pw[:, g, :], dT[:, g, :],
                                               start=True, stop=True)
                    ins.then_inc(s_am, 1)

                def gating(t):
                    pe.wait_ge(s_vn, t + 1)
                    pe.wait_ge(s_aa, t + 1)
                    for h in range(NH):
                        q = slice(h * P, (h + 1) * P)
                        ins = nc.tensor.matmul(bank[6][:, q], wsT[:, h, :], vn[:, q], start=True, stop=True)
                    ins.then_inc(s_z, 1)

                def g_transposes(t):
                    pe.wait_ge(s_g, t + 1)
                    pe.wait_ge(s_dT, t + 1)
                    for h in range(NH):
                        ins = nc.tensor.transpose(bank[5][:, h * P:(h + 1) * P], g_sb[:, h * P:(h + 1) * P], ident[:, :])
                    ins.then_inc(s_gTp, 1)

                def ada_pair_unit(i, b):
                    pe.wait_ge(s_adal[b], i * 16 + 16)
                    for j in range(4):
                        ins = nc.tensor.matmul(bank[6][32 * j:32 * j + NC, :], cT_k[:, :],
                                               ada_st[b][:, j * BANK:(j + 1) * BANK], start=True, stop=True)
                    ins.then_inc(s_ad, 1)

                def tile(t, b, i):
                    pe.wait_ge(s_hT, t + 1)
                    lead = isinstance(t, int) and t == 0
                    project(t, b, 0, bank[2], s_pp, None if lead else s_p)
                    if lead:
                        sample_d_transposes()
                    else:
                        bands(t - 1, 1 - b, band0 if isinstance(t, int) and t == 1 else band)
                    project(t, b, 1, bank[3], s_up, None if lead else s_u)
                    if lead:
                        sample_pool_linear()
                    else:
                        pool_linear(t - 1)
                        gating(t - 1)
                    if not (isinstance(t, int) and t == NT - 1):
                        h_transposes(t + 1, 1 - b)
                    project(t, b, 2, bank[4], s_vp, None if lead else s_vn)
                    if lead:
                        sample_g_transposes()
                        pe.wait_ge(s_su, 1)
                    else:
                        g_transposes(t - 1)
                        pe.wait_ge(s_g, t)
                    pe.wait_ge(s_ck, t + 1)
                    ada_pair_unit(i, b)

                h_transposes(0, 0)
                sample_projections()
                tile(0, 0, 0)
                tile(1, 1, 0)
                with pe.Fori(1, NT // 2 - 1) as i:
                    for b in range(2):
                        tile(i * 2 + b, b, i)
                tile(NT - 2, 0, NT // 2 - 1)
                tile(NT - 1, 1, NT // 2 - 1)
                bands(NT - 1, 1, band)
                pool_linear(NT - 1)
                gating(NT - 1)
                g_transposes(NT - 1)

            @block.vector
            def _(dve):
                ch = Chain(dve, s_chv)

                def modulate(t, b, rows=P):
                    dve.wait_ge(s_x[b], x_count(t, b))
                    if not (isinstance(t, int) and t == 0):
                        dve.wait_ge(s_hTp, t)
                    ch.link(nc.vector.tensor_tensor(h_t[0:rows, :], x_t[b][0:rows, :], sc1[0:rows, :], ALU.mult))
                    nc.vector.tensor_tensor(h_t[0:rows, :], h_t[0:rows, :], sh1[0:rows, :], ALU.add).then_inc(s_h, 1)

                def save_hT_lo(t, b, rows=P):
                    dve.wait_ge(s_hTh, t + 1)
                    nc.vector.tensor_tensor(hT_lo[b][:, :, 0:rows],
                                            ps2[0][:, :].rearrange("p (k t) -> p k t", k=KD)[:, :, 0:rows],
                                            hT_hi[b][:, :, 0:rows].bitcast(F32), ALU.subtract).then_inc(s_hT, 1)

                def x_count(t, b):
                    return (t - b) * 8 + 16

                def save_dT(t):
                    dve.wait_ge(s_bd, t + 1)
                    if not (isinstance(t, int) and t == 0):
                        dve.wait_ge(s_am, t)
                    nc.vector.tensor_copy(dT[:, :, :], bank[5].rearrange("p (g t) -> p g t", g=NG)).then_inc(s_dT, 1)

                def gate(t):
                    dve.wait_ge(s_z, t + 1)
                    dve.wait_ge(s_u, t + 1)
                    if not (isinstance(t, int) and t == 0):
                        dve.wait_ge(s_gTp, t)
                    for h in range(NH):
                        q = slice(h * P, (h + 1) * P)
                        ch.add(nc.vector.scalar_tensor_tensor(g_sb[:, q], bank[6][:, q], bt[:, h:h + 1], u_sb[:, q],
                                                              ALU.add, ALU.mult))
                    ch.wait()
                    dve.sem_inc(s_g, 1)

                def add_unit(t, b):
                    dve.wait_ge(s_ad, t + 1)
                    for j in range(4):
                        q = slice(32 * j, 32 * j + NC)
                        ch.add(nc.vector.tensor_tensor(acc[q, 1 + b, :], bank[6][q, :], acc[q, 1 + b, :], ALU.add))
                    ch.wait()
                    dve.sem_inc(s_aa, 1)

                def sample_gating():
                    stats = stat_s[:, 0:NH * 6].rearrange("p (h n) -> p h n", h=NH)
                    moments = stat_s[:, NH * 6:NH * 8].rearrange("p (h n) -> p h n", h=NH)
                    std, inv = stat_s[:, NH * 8:NH * 9], stat_s[:, NH * 9:NH * 10]
                    v = bank[7]
                    for h in range(NH):
                        ch.add(nc.vector.bn_stats(stats[:, h, :], v[0:NS, h * P:(h + 1) * P]))
                    ch.wait()
                    for h in range(NH):
                        ch.add(nc.vector.bn_aggr(moments[:, h, :], stats[:, h, :]))
                    ch.wait()
                    dve.sem_inc(s_svar, 1)
                    dve.wait_ge(s_sstd, 1)
                    ch.link(nc.vector.reciprocal(inv, std))
                    for h in range(NH):
                        q = slice(h * P, (h + 1) * P)
                        ch.add(nc.vector.tensor_scalar(uv_s[:, 1, q], v[0:NS, q], moments[:, h, 0:1], inv[:, h:h + 1],
                                                       ALU.subtract, ALU.mult))
                    ch.wait()
                    ch.link(nc.vector.tensor_tensor(uv_s[:, 1, :], uv_s[:, 1, :], sg_bc[0:NS, :], ALU.mult))
                    dve.sem_inc(s_svn, 1)
                    dve.wait_ge(s_su, 1)
                    for h in range(NH):
                        q = slice(h * P, (h + 1) * P)
                        ch.add(nc.vector.tensor_scalar(g_s[:, q], uv_s[:, 1, q], w0s[0:NS, h:h + 1], b0s[0:NS, h:h + 1],
                                                       ALU.mult, ALU.add))
                    ch.wait()
                    ch.link(nc.vector.tensor_tensor(g_s[:, :], uv_s[:, 0, :], g_s[:, :], ALU.mult))
                    dve.sem_inc(s_sg, 1)

                def copy_c(i):
                    nc.vector.tensor_scalar(cT_k[:, :], cT[:, ds(i, 1), :].rearrange("p a c -> p (a c)"), 1.0, None,
                                            ALU.mult).then_inc(s_ck, 1)

                def head_norm(t, rows=P):
                    dve.wait_ge(s_vp, t + 1)
                    if not (isinstance(t, int) and t == 0):
                        dve.wait_ge(s_z, t)
                    v = bank[4]
                    for h in range(NH):
                        ch.add(nc.vector.bn_stats(vstat[0:rows, h, :], v[0:rows, h * P:(h + 1) * P]))
                    ch.wait()
                    for h in range(NH):
                        ch.add(nc.vector.bn_aggr(vmv[0:rows, h, :], vstat[0:rows, h, :]))
                    ch.wait()
                    dve.sem_inc(s_var, 1)
                    dve.wait_ge(s_std, t + 1)
                    ch.link(nc.vector.reciprocal(vinv[0:rows, :], vstd[0:rows, :]))
                    for h in range(NH):
                        q = slice(h * P, (h + 1) * P)
                        ch.add(nc.vector.tensor_scalar(vn[0:rows, q], v[0:rows, q], vmv[0:rows, h, 0:1],
                                                       vinv[0:rows, h:h + 1], ALU.subtract, ALU.mult))
                    ch.wait()
                    nc.vector.tensor_tensor(vn[0:rows, :], vn[0:rows, :], sg_bc[0:rows, :], ALU.mult).then_inc(s_vn, 1)

                def tile(t, b, i):
                    lead = isinstance(t, int) and t == 0
                    if not lead:
                        save_dT(t - 1)
                        dve.wait_ge(s_ad, t)
                    copy_c(i)
                    if not (isinstance(t, int) and t == NT - 1):
                        modulate(t + 1, 1 - b)
                    if not lead:
                        gate(t - 1)
                    if not (isinstance(t, int) and t == NT - 1):
                        save_hT_lo(t + 1, 1 - b)
                    add_unit(t, b)
                    head_norm(t)
                    ch.restart()

                dve.wait_ge(s_sh1, 1)
                modulate(0, 0)
                dve.wait_ge(s_sld, 48)
                nc.vector.tensor_scalar_add(sc1_s[:, :], sc1_s[:, :], 1.0).then_inc(s_ssc, 1)
                dve.wait_ge(s_ssc, 1)
                ch.link(nc.vector.tensor_tensor(h_s[:, :], x_s[:, :], sc1_s[:, :], ALU.mult))
                nc.vector.tensor_tensor(h_s[:, :], h_s[:, :], sh1_s[:, :], ALU.add).then_inc(s_sh, 1)
                save_hT_lo(0, 0)
                dve.wait_ge(s_shTh, 1)
                nc.vector.tensor_tensor(hT_s[1][:, :, :], bank[7][:, 0:KD * NS].rearrange("p (k c) -> p k c", c=NS),
                                        hT_s[0][:, :, :].bitcast(F32), ALU.subtract).then_inc(s_shT, 1)
                for k in range(SETUP_UNITS, KD):
                    split_w_in_lo(dve, k)
                dve.wait_ge(s_sp, 1)
                ch.link(nc.vector.tensor_tensor(hsum[:, :], hsum[:, :], p_s[:, :], ALU.add))
                for g, w in enumerate(WINDOWS):
                    q = slice(g * P, (g + 1) * P)
                    ch.add(nc.vector.scalar_tensor_tensor(hsum[:, q], hsum[:, q], 1.0 / w, p_s[:, q], ALU.mult, ALU.subtract))
                ch.wait()
                dve.sem_inc(s_sd, 1)
                sample_gating()
                dve.wait_ge(s_sdp, 1)
                nc.vector.tensor_copy(dT_s[:, :, :], bank[5][:, 0:NG * NS].rearrange("p (g t) -> p g t", g=NG)).then_inc(s_sdT, 1)
                tile(0, 0, 0)
                tile(1, 1, 0)
                with dve.Fori(1, NT // 2 - 1) as i:
                    for b in range(2):
                        tile(i * 2 + b, b, i)
                tile(NT - 2, 0, NT // 2 - 1)
                tile(NT - 1, 1, NT // 2 - 1)
                save_dT(NT - 1)
                def split_w_out_lo(k):
                    dve.wait_ge(s_woh, k + 1)
                    nc.vector.tensor_tensor(wo_lo[k][:, :], w_out_raw[:, k, :], wo_hi[k][:, :].bitcast(F32),
                                            ALU.subtract).then_inc(s_wol, 1)

                for k in range(KD // 4):
                    split_w_out_lo(k)
                gate(NT - 1)
                for k in range(KD // 4, KD):
                    split_w_out_lo(k)
                ch.restart()

            @block.scalar
            def _(act):
                ch = Chain(act, s_cha)

                def save_p(t, b, rows=P):
                    act.wait_ge(s_pp, t + 1)
                    if not (isinstance(t, int) and t == 0):
                        act.wait_ge(s_bd, t)
                    nc.scalar.copy(p_sb[b][0:rows, :], bank[2][0:rows, :]).then_inc(s_p, 1)

                def save_u(t, rows=P):
                    act.wait_ge(s_up, t + 1)
                    if not (isinstance(t, int) and t == 0):
                        act.wait_ge(s_g, t)
                    nc.scalar.copy(u_sb[0:rows, :], bank[3][0:rows, :]).then_inc(s_u, 1)

                def save_a(t, n=P):
                    act.wait_ge(s_am, t + 1)
                    if not is0(t):
                        act.wait_ge(s_mos, t * 16)
                    for g in range(NG):
                        ch.add(nc.scalar.activation(mix_o[:, g, :], bank[7][:, g * n:(g + 1) * n], ACT.Copy, scale=psc[:, g:g + 1]))
                    ch.wait()
                    act.sem_inc(s_a, 1)

                def save_gT(t):
                    act.wait_ge(s_gTp, t + 1)
                    nc.scalar.copy(mix_o[:, NG:NG + NH, :], bank[5].rearrange("p (h c) -> p h c", h=NH)).then_inc(s_gT, 1)

                def save_hT(t, b, rows=P):
                    act.wait_ge(s_hTp, t + 1)
                    if not (isinstance(t, int) and t < 2):
                        act.wait_ge(s_vp, t - 1)
                    nc.scalar.copy(hT_hi[b][:, :, 0:rows],
                                   ps2[0][:, :].rearrange("p (k t) -> p k t", k=KD)[:, :, 0:rows]).then_inc(s_hTh, 1)

                def std_v(t, rows=P):
                    act.wait_ge(s_var, t + 1)
                    nc.scalar.activation(vstd[0:rows, :], vmv[0:rows, :, 1], ACT.Sqrt, bias=eps[0:rows, :]).then_inc(s_std, 1)

                def tile(t, b):
                    lead = isinstance(t, int) and t == 0
                    save_p(t, b)
                    save_u(t)
                    if lead:
                        act.wait_ge(s_sam, 1)
                        for g in range(NG):
                            ch.add(nc.scalar.activation(mixT_s[:, g, :], bank[7][:, g * NS:(g + 1) * NS], ACT.Copy,
                                                        scale=psc[:, g:g + 1]))
                        ch.wait()
                        act.sem_inc(s_sa, 1)
                    else:
                        save_a(t - 1)
                    if not (isinstance(t, int) and t == NT - 1):
                        save_hT(t + 1, 1 - b)
                    if lead:
                        act.wait_ge(s_sgp, 1)
                        nc.scalar.copy(mixT_s[:, NG:NG + NH, :],
                                       bank[5][:, NG * NS:(NG + NH) * NS].rearrange("p (h c) -> p h c", h=NH)).then_inc(s_sgT, 1)
                    else:
                        save_gT(t - 1)
                    std_v(t)
                    ch.restart()

                for k in range(SETUP_UNITS, RING):
                    split_w_in_hi(act, k)
                save_hT(0, 0)
                act.wait_ge(s_shTp, 1)
                nc.scalar.copy(hT_s[0][:, :, :], bank[7][:, 0:KD * NS].rearrange("p (k c) -> p k c", c=NS)).then_inc(s_shTh, 1)
                for k in range(RING, KD):
                    split_w_in_hi(act, k)
                act.wait_ge(s_sin, 1)
                nc.scalar.copy(p_s[:, :], bank[5][0:NS, :]).then_inc(s_sp, 1)
                act.wait_ge(s_svar, 1)
                nc.scalar.activation(stat_s[:, NH * 8:NH * 9],
                                     stat_s[:, NH * 6:NH * 8].rearrange("p (h n) -> p h n", h=NH)[:, :, 1],
                                     ACT.Sqrt, bias=eps[0:NS, :]).then_inc(s_sstd, 1)
                nc.scalar.copy(uv_s[:, 0, :], bank[6][0:NS, :]).then_inc(s_su, 1)
                tile(0, 0)
                tile(1, 1)
                with act.Fori(1, NT // 2 - 1) as i:
                    for b in range(2):
                        tile(i * 2 + b, b)
                tile(NT - 2, 0)
                tile(NT - 1, 1)
                def split_w_out_hi(k):
                    act.wait_ge(s_wo[k // 2], 16)
                    nc.scalar.copy(wo_hi[k][:, :], w_out_raw[:, k, :]).then_inc(s_woh, 1)

                for k in range(KD // 2):
                    split_w_out_hi(k)
                save_a(NT - 1)
                split_w_out_hi(KD // 2)
                save_gT(NT - 1)
                for k in range(KD // 2 + 1, KD):
                    split_w_out_hi(k)
                ch.restart()

        spent = [s for s in sems if s not in (s_chp, s_chv, s_cha)]

        s_bc = sem("norm_rows_loaded")
        s_g1 = sem("gate_rows_ready")
        s_sc2 = sem("scale_rows_ready")
        s_nrow = sem("norm_rows_ready")
        s_lnr = sem("ln1_rows_loaded")
        s_mr = [sem(f"mix_loaded{i}") for i in range(2)]
        s_mh = sem("mix_hi_ready")
        s_ml = sem("mix_lo_ready")
        s_xr = [sem(f"x_reloaded{i}") for i in range(2)]
        s_mix = sem("mix_in_psum")
        s_mixr = sem("mix_read")
        s_xu = sem("x_used")
        s_v1 = sem("x1_var_ready")
        s_s1 = sem("x1_std_ready")
        s_mo = sem("x1_moments_ready")
        s_nrm = sem("x1_normed")
        s_x1p = sem("x1_scaled")
        s_x1 = sem("x1_ready")
        s_x1s = [sem(f"x1_stored{i}") for i in range(2)]
        s_h2q = sem("h2_scaled")
        s_h2 = sem("h2_ready")
        s_h2s = [sem(f"h2_stored{i}") for i in range(2)]
        s_h2p = sem("h2T_in_psum")
        s_h2T = sem("h2T_ready")
        s_rt = sem("router_in_psum")
        s_lgT = sem("logitsT_ready")
        s_lg = sem("logits_in_psum")
        s_m = sem("mask_ready")
        s_rk = sem("rank_in_psum")
        s_rkr = sem("rank_read")
        s_bcs = sem("sample_norm_rows_loaded")
        s_lz = sem("logitsT_zeroed")
        s_raw = [sem(f"raw_units_loaded{i}") for i in range(NU // 2)]

        def load_units(eng, e, pair):
            k = 2 * pair
            if k < GU:
                for half, w_v in enumerate((gate_v, up_v)):
                    eng.dma_start(wraw[:, k:k + 2, half * FE:(half + 1) * FE],
                                  w_v[ds(e, 1), :, k:k + 2, :].rearrange("a p k n -> p (a k) n")).then_inc(s_raw[pair], 16)
            else:
                k -= GU
                eng.dma_start(wraw[:, GU + k:GU + k + 2, :],
                              down_v[ds(e, 1), :, k:k + 2, :].rearrange("a p k n -> p (a k) n")).then_inc(s_raw[pair], 16)

        def raw_count(pair, e):
            return e * 32 + 32 if 2 * pair < GU else e * 16 + 16

        nc.clear_and_free_semaphores(spent)

        def rows_of(t):
            return NS if is0(t) else P

        def tile_of(t):
            return NT if is0(t) else t - 1

        def frames(eng, frame):
            for t in range(6):
                frame(t, t % 2)
            with eng.Fori(3, NT // 2 - 1) as i:
                for b in range(2):
                    frame(i * 2 + b, b)
            for t in range(NT - 2, NT + 5):
                frame(t, t % 2)

        def there(t):
            return not isinstance(t, int) or 0 <= t <= NT

        def fold_rows(engine, ch, scale, shift, tmp, n):
            ch.link(engine.tensor_tensor(tmp[0:n, :], lb1[0:n, :], scale[0:n, :], ALU.mult))
            ch.add(engine.tensor_tensor(shift[0:n, :], tmp[0:n, :], shift[0:n, :], ALU.add))
            ch.link(engine.tensor_tensor(scale[0:n, :], lg1[0:n, :], scale[0:n, :], ALU.mult))

        with nc.Block() as block:
            @block.sync
            def _(sp):
                for t in range(1, 3):
                    sp.dma_start(mix_r[t % 2][:, :, :].rearrange("p k c -> p (k c)"),
                                 mix_d[(t - 1) * P:t * P, :]).then_inc(s_mr[t % 2], 16)
                sp.dma_start(x_r[0][0:NS, :], x_sample[:, 0, :]).then_inc(s_xr[0], 16)
                for dst, j in ((g1_s, 2), (sc2_s, 4), (sh2_s, 3)):
                    sp.dma_start(dst[:, :], mod_d[0:NS, j * D:(j + 1) * D]).then_inc(s_bcs, 16)
                for n, (dst, src) in enumerate(((lg1, row(ln1_g[0])), (lb1, row(ln1_b[0])), (g1, mod_row(2)),
                                                (sc2, mod_row(4)), (sh2, mod_row(3)))):
                    sp.dma_start(dst[:, :], src).then_inc(s_lnr if n < 2 else s_bc, 16)
                sp.dma_start(x_r[1][:, :], xp[0:P, :]).then_inc(s_xr[1], 16)
                for pair in range(EARLY):
                    load_units(sp, 0, pair)

                def frame(t, b):
                    if not isinstance(t, int) or 1 <= t and t + 2 <= NT:
                        sp.wait_ge(s_ml, t + 1)
                        sp.dma_start(mix_r[b][:, :, :].rearrange("p k c -> p (k c)"),
                                     mix_d[ds(tile_of(t + 2) * P, P), :]).then_inc(s_mr[b], 16)
                    if isinstance(t, int) and (t < 1 or t > NT + 1):
                        return
                    if not (isinstance(t, int) and t >= NT):
                        sp.wait_ge(s_xu, t)
                        sp.dma_start(x_r[1 - b][:, :], xp[ds(tile_of(t + 1) * P, P), :]).then_inc(s_xr[1 - b], 16)
                    n = rows_of(t - 1)
                    sp.wait_ge(s_h2, t)
                    sp.dma_start(h2_d[ds(tile_of(t - 1) * P, n), :], h2[1 - b][0:n, :]).then_inc(s_h2s[1 - b], 16)
                    sp.wait_ge(s_x1, t)
                    sp.dma_start(x1_d[ds(tile_of(t - 1) * P, n), :], x1[1 - b][0:n, :]).then_inc(s_x1s[1 - b], 16)

                frames(sp, frame)
                for b in range(2):
                    sp.wait_ge(s_x1s[b], 16 * (NT // 2 + 1 - b))
                    sp.wait_ge(s_h2s[b], 16 * (NT // 2 + 1 - b))

            @block.tensor
            def _(pe):
                def project(t, b, units):
                    rows = rows_of(t)
                    if units.start == 0:
                        pe.wait_ge(s_ml, t + 1)
                        if not (isinstance(t, int) and t < 2):
                            pe.wait_ge(s_mixr, t - 1)
                    for k in units:
                        terms = ((mix_hi, wo_hi), (mix_hi, wo_lo), (mix_lo, wo_hi))
                        for m, (a, w) in enumerate(terms):
                            for n in range(2):
                                q = slice(n * BANK, (n + 1) * BANK)
                                ins = nc.tensor.matmul(ps2[b][0:rows, q], a[b][:, k, 0:rows], w[k][:, q],
                                                       start=(k == 0 and m == 0), stop=(k == KD - 1 and m == 2))
                    if units.stop == KD:
                        ins.then_inc(s_mix, 1)

                def h2_transposes(t, b):
                    rows = rows_of(t)
                    pe.wait_ge(s_h2, t + 1)
                    if not is0(t):
                        pe.wait_ge(s_h2T, t)
                    for k in range(KD):
                        ins = nc.tensor.transpose(ps2[2][:, k * P:k * P + rows], h2[b][0:rows, k * P:(k + 1) * P],
                                                  ident[0:rows, 0:rows])
                    ins.then_inc(s_h2p, 1)

                def router(t, rows=P):
                    pe.wait_ge(s_h2T, t + 1)
                    if not (isinstance(t, int) and t == 0):
                        pe.wait_ge(s_lgT, t)
                    for k in range(KD):
                        ins = nc.tensor.matmul(bank[6][0:NR, 0:rows], rw[:, k, :], h2T[:, k, 0:rows],
                                               start=(k == 0), stop=(k == KD - 1))
                    ins.then_inc(s_rt, 1)

                def logits(t, rows=P):
                    pe.wait_ge(s_lgT, t + 1)
                    if not (isinstance(t, int) and t == 0):
                        pe.wait_ge(s_rkr, t)
                    nc.tensor.transpose(bank[7][0:rows, 0:P], lgT[:, 0:rows], ident[:, :]).then_inc(s_lg, 1)

                def ranks(t, rows=P):
                    pe.wait_ge(s_m, t + 1)
                    q = bank[7][0:rows, P:P + NE]
                    nc.tensor.matmul(q, before[0:rows, 0:rows], m_b[0:rows, :], start=True, stop=False)
                    nc.tensor.matmul(q, ones[:, 0:rows], seen_b[:, :], start=False, stop=True).then_inc(s_rk, 1)

                def frame(t, b):
                    if there(t):
                        project(t, b, range(0, KD // 2))
                    if there(t - 2):
                        h2_transposes(t - 2, b)
                    if there(t - 3):
                        logits(t - 3, rows_of(t - 3))
                    if there(t):
                        project(t, b, range(KD // 2, KD))
                    if there(t - 2):
                        router(t - 2, rows_of(t - 2))
                    if there(t - 3):
                        ranks(t - 3, rows_of(t - 3))

                frames(pe, frame)

            @block.gpsimd
            def _(pool):
                ch = Chain(pool, s_chp)

                def split_lo(t, b):
                    rows = rows_of(t)
                    src = mixT_s if rows == NS else mix_r[b]
                    pool.wait_ge(s_mh, t + 1)
                    if not (isinstance(t, int) and t < 2):
                        pool.wait_ge(s_mix, t - 1)
                    nc.gpsimd.tensor_tensor(mix_lo[b][:, :, 0:rows], src[:, :, 0:rows],
                                            mix_hi[b][:, :, 0:rows].bitcast(F32), ALU.subtract).then_inc(s_ml, 1)

                def add_biases(t, b):
                    n = rows_of(t)
                    pool.wait_ge(s_h2q, t + 1)
                    nc.gpsimd.tensor_tensor(h2[b][0:n, :], h2[b][0:n, :], (sh2_s if n == NS else sh2)[0:n, :],
                                            ALU.add).then_inc(s_h2, 1)
                    pool.wait_ge(s_x1p, t + 1)
                    nc.gpsimd.tensor_tensor(x1[b][0:n, :], x1[b][0:n, :], lb1[0:n, :], ALU.add).then_inc(s_x1, 1)

                def frame(t, b):
                    if there(t + 1):
                        split_lo(t + 1, 1 - b)
                    if is0(t):
                        pool.wait_ge(s_sc2, 1)
                        fold_rows(nc.gpsimd, ch, sc2, sh2, x1[1], P)
                        pool.sem_inc(s_nrow, 1)
                    if there(t - 1):
                        add_biases(t - 1, 1 - b)

                nc.gpsimd.memset(lgT[:, :], 0.0).then_inc(s_lz, 1)
                split_lo(0, 0)
                frames(pool, frame)
                ch.restart()

            @block.vector
            def _(dve):
                ch = Chain(dve, s_chv)

                def norm_sums(t, b):
                    n = rows_of(t)
                    q = slice(0, n)
                    dve.wait_ge(s_mix, t + 1)
                    ch.link(nc.vector.tensor_tensor(t_r[q, :], ps2[b][q, :], (g1_s if n == NS else g1)[q, :], ALU.mult))
                    dve.sem_inc(s_mixr, 1)
                    dve.wait_ge(s_xr[b], (t - b) * 8 + 16)
                    ch.link(nc.vector.scalar_tensor_tensor(t_r[q, :], x_r[b][q, :], ALPHA, t_r[q, :], ALU.mult, ALU.add))
                    dve.sem_inc(s_xu, 1)
                    for h in range(2):
                        ch.add(nc.vector.bn_stats(bst[q, h, :], t_r[q, h * BANK:(h + 1) * BANK]))
                    ch.wait()
                    nc.vector.bn_aggr(mv[q, :], bst[q, :, :].rearrange("p a s -> p (a s)")).then_inc(s_v1, 1)

                def moments(t):
                    q = slice(0, rows_of(t))
                    dve.wait_ge(s_s1, t + 1)
                    ch.link(nc.vector.reciprocal(inv[q, :], std[q, :]))
                    nc.vector.tensor_scalar(nb1[q, :], mv[q, 0:1], inv[q, 0:1], -1.0, ALU.mult, ALU.mult).then_inc(s_mo, 1)

                def norm_scale(t, b):
                    n = rows_of(t)
                    q = slice(0, n)
                    dve.wait_ge(s_nrm, t + 1)
                    if not (isinstance(t, int) and t < 2):
                        dve.wait_ge(s_h2s[b], (t - b) * 8)
                        dve.wait_ge(s_h2p, t - 1)
                    ch.link(nc.vector.tensor_tensor(h2[b][q, :], t_r[q, :], (sc2_s if n == NS else sc2)[q, :], ALU.mult))
                    dve.sem_inc(s_h2q, 1)
                    if not (isinstance(t, int) and t < 2):
                        dve.wait_ge(s_x1s[b], (t - b) * 8)
                    ch.link(nc.vector.tensor_tensor(x1[b][q, :], t_r[q, :], lg1[q, :], ALU.mult))
                    dve.sem_inc(s_x1p, 1)

                def route(t, rows=P):
                    q = slice(0, rows)
                    gl, gt, et = (top[q, n, :] for n in range(3))
                    dve.wait_ge(s_lg, t + 1)
                    ch.add(nc.vector.tensor_tensor(gl[:, 0:NRG], bank[7][q, 0:NRG], rb[q, 0:NRG], ALU.add))
                    ch.link(nc.vector.tensor_tensor(el[q, :], bank[7][q, NRG:NR], rb[q, NRG:NR], ALU.add))
                    ch.link(nc.vector.max(gt, gl))
                    ch.link(nc.vector.max_index(gidx[q, :], gt, gl))
                    ch.link(nc.vector.tensor_copy(gidf[q, :], gidx[q, 0:1]))
                    ch.link(nc.vector.tensor_scalar(gm[q, :], iota[q, 0:NRG], gidf[q, 0:1], -BIG, ALU.not_equal, ALU.mult))
                    ch.link(nc.vector.tensor_tensor(el[q, :].rearrange("p (g e) -> p g e", g=NRG),
                                                    el[q, :].rearrange("p (g e) -> p g e", g=NRG),
                                                    gm[q, :].unsqueeze(2).to_broadcast([rows, NRG, EPG]), ALU.add))
                    ch.link(nc.vector.max(et, el[q, :]))
                    ch.link(nc.vector.max_index(eidx[q, :], et, el[q, :]))
                    ch.add(nc.vector.tensor_copy(tops[q, ds(tile_of(t), 1), :, :].rearrange("p a m n -> p (a m n)"),
                                                 top[q, :, :].rearrange("p m n -> p (m n)")))
                    ch.link(nc.vector.tensor_copy(eidf[q, :], eidx[q, 0:2]))
                    for n in range(2):
                        ch.add(nc.vector.tensor_scalar(pick(t, n, q), iota[q, 0:NE], eidf[q, n:n + 1], None, ALU.is_equal))
                    ch.wait()
                    nc.vector.tensor_tensor(m_b[q, :], pick(t, 0, q), pick(t, 1, q), ALU.add).then_inc(s_m, 1)

                def read_rank(t, rows=P):
                    q = slice(0, rows)
                    dve.wait_ge(s_rk, t + 1)
                    for n in range(2):
                        ch.add(nc.vector.tensor_tensor(rk[q, n, :], pick(t, n, q), bank[7][q, P:P + NE], ALU.mult))
                    ch.link(nc.vector.tensor_tensor(seen[q, :], seen[q, :], m_b[q, :], ALU.add))
                    ch.add(nc.vector.tensor_copy(seen_b[q, :], seen[q, :]))
                    ch.add(nc.vector.tensor_reduce(rank[q, ds(tile_of(t), 1), :].rearrange("p a n -> p (a n)"), rk[q, :, :], AX_X, ALU.add))
                    ch.wait()
                    dve.sem_inc(s_rkr, 1)

                def place_one_hots(t):
                    ch.link(nc.vector.tensor_scalar(lo_f[:, :], rank[:, ds(tile_of(t), 1), :].rearrange("p a n -> p (a n)"), 1.0,
                                                    None, ALU.mult))
                    ch.link(nc.vector.tensor_copy(rk_i[:, :], lo_f[:, :]))
                    ch.link(nc.vector.tensor_scalar(lo_i[:, :], rk_i[:, :], P - 1, None, ALU.bitwise_and))
                    ch.link(nc.vector.tensor_copy(lo_f[:, :], lo_i[:, :]))
                    for n in range(2):
                        ch.add(nc.vector.tensor_scalar(oh_lo[:, ds(tile_of(t), 1), n, :].rearrange("p a i -> p (a i)"), iota[:, :],
                                                       lo_f[:, n:n + 1], None, ALU.is_equal))

                def pick(t, n, q):
                    return picked[q, ds(tile_of(t), 1), n, :].rearrange("p a e -> p (a e)")

                def frame(t, b):
                    if there(t - 4):
                        read_rank(t - 4, rows_of(t - 4))
                    if there(t - 1):
                        norm_sums(t - 1, 1 - b)
                    if there(t - 1):
                        moments(t - 1)
                    norm_first = isinstance(t, int) and t == NT
                    if there(t - 3) and not norm_first:
                        route(t - 3, rows_of(t - 3))
                    if isinstance(t, int) and t == 2:
                        dve.wait_ge(s_nrow, 1)
                    if there(t - 1):
                        norm_scale(t - 1, 1 - b)
                    if there(t - 3) and norm_first:
                        route(t - 3, rows_of(t - 3))
                    if there(t - 4):
                        place_one_hots(t - 4)
                    ch.restart()

                dve.wait_ge(s_bcs, 48)
                ch.add(nc.vector.tensor_scalar_add(g1_s[:, :], g1_s[:, :], 1.0))
                ch.link(nc.vector.tensor_scalar_add(sc2_s[:, :], sc2_s[:, :], 1.0))
                dve.wait_ge(s_lnr, 32)
                fold_rows(nc.vector, ch, sc2_s, sh2_s, tmp_s, NS)
                dve.wait_ge(s_bc, 48)
                ch.add(nc.vector.tensor_scalar_add(g1[:, :], g1[:, :], 1.0))
                ch.link(nc.vector.tensor_scalar_add(sc2[:, :], sc2[:, :], 1.0))
                dve.sem_inc(s_sc2, 1)
                frames(dve, frame)

            @block.scalar
            def _(act):
                def split_hi(t, b):
                    rows = rows_of(t)
                    if rows == P:
                        act.wait_ge(s_mr[b], (t + b) * 8)
                    src = mixT_s if rows == NS else mix_r[b]
                    if not (isinstance(t, int) and t < 2):
                        act.wait_ge(s_mix, t - 1)
                    nc.scalar.copy(mix_hi[b][:, :, 0:rows], src[:, :, 0:rows]).then_inc(s_mh, 1)

                def normalise(t):
                    n = rows_of(t)
                    act.wait_ge(s_v1, t + 1)
                    nc.scalar.activation(std[0:n, :], mv[0:n, 1:2], ACT.Sqrt, bias=eps[0:n, :]).then_inc(s_s1, 1)
                    act.wait_ge(s_mo, t + 1)
                    nc.scalar.activation(t_r[0:n, :], t_r[0:n, :], ACT.Identity, bias=nb1[0:n, :],
                                         scale=inv[0:n, :]).then_inc(s_nrm, 1)

                def save_h2T(t):
                    n = rows_of(t)
                    act.wait_ge(s_h2p, t + 1)
                    if not is0(t):
                        act.wait_ge(s_rt, t)
                    nc.scalar.copy(h2T[:, :, 0:n],
                                   ps2[2][:, :].rearrange("p (k t) -> p k t", k=KD)[:, :, 0:n]).then_inc(s_h2T, 1)

                def save_lgT(t):
                    n = rows_of(t)
                    act.wait_ge(s_rt, t + 1)
                    if not is0(t):
                        act.wait_ge(s_lg, t)
                    nc.scalar.copy(lgT[0:NR, 0:n], bank[6][0:NR, 0:n]).then_inc(s_lgT, 1)

                def frame(t, b):
                    if there(t + 1):
                        split_hi(t + 1, 1 - b)
                    copy_first = isinstance(t, int) and t > NT
                    if there(t - 2) and copy_first:
                        save_h2T(t - 2)
                    if there(t - 1):
                        normalise(t - 1)
                    if there(t - 2) and not copy_first:
                        save_h2T(t - 2)
                    if there(t - 2):
                        save_lgT(t - 2)

                split_hi(0, 0)
                act.wait_ge(s_lz, 1)
                frames(act, frame)

        s_cnt = sem("counts_in_psum")
        s_oh = sem("one_hots_ready")
        s_tok = sem("slot_table_in_psum")
        s_tab = sem("tables_ready")
        s_exi = sem("exponents_ready")
        s_exo = sem("exponentials_ready")
        s_inval = sem("numbers_ready")
        s_ohb = sem("block_one_hots_ready")
        s_oha = sem("token_partitions_ready")
        s_hi = [sem("gate_up_hi_ready"), sem("down_hi_ready")]
        s_lo = [sem("gate_up_lo_ready"), sem("down_lo_ready")]
        s_xg = [sem(f"rows_gathered{i}") for i in range(2)]
        POOL_UNITS = 5
        SPLIT_EARLY = 6

        def halves_count(j, e):
            return (0, e * GU + j + 1) if j < GU else (1, e * DN + j - GU + 1)

        def split_hi_unit(act, j, e):
            act.wait_ge(s_raw[j // 2], raw_count(j // 2, e))
            nc.scalar.copy(w_hi[j][:, :], wraw[:, j, :]).then_inc(s_hi[j >= GU], 1)

        def split_lo_unit(eng, engine, j, e):
            kind, count = halves_count(j, e)
            eng.wait_ge(s_hi[kind], count)
            engine.tensor_tensor(w_lo[j][:, :], wraw[:, j, :], w_hi[j][:, :].bitcast(F32), ALU.subtract).then_inc(s_lo[kind], 1)

        def gather_rows(b):
            nc.gpsimd.indirect_dma_start(out=xg[b][:, :], out_offset=None, in_=h2_d[:, :],
                                         in_offset=bass.IndirectOffsetOnAxis(ap=idx[b][:, 0:1], axis=0)).then_inc(s_xg[b], 16)

        M = NTT * 2
        CHUNK = M // 2
        with nc.Block() as block:
            @block.tensor
            def _(pe):
                nc.tensor.matmul(bank[0][:, 0:NE], ones[:, :], seen_b[:, :], start=True, stop=True).then_inc(s_cnt, 1)
                for m in range(M):
                    if m % CHUNK == 0:
                        pe.wait_ge(s_oh, m // CHUNK + 1)
                        pe.wait_ge(s_oha, m // CHUNK + 1)
                    ins = nc.tensor.matmul(bank[1][:, 0:2 * NB], oh_lo[:, m // 2, m % 2, :], oh_hi[:, m, :, :].rearrange("p a b -> p (a b)"),
                                           start=(m == 0), stop=(m == M - 1))
                ins.then_inc(s_tok, 1)

            @block.gpsimd
            def _(pool):
                ch = Chain(pool, s_chp)
                ch.link(nc.gpsimd.iota(tile_i[:, :], pattern=[[1, NTT], [0, 2]], base=0, channel_multiplier=0))
                ch.link(nc.gpsimd.tensor_copy(tile_f[:, :], tile_i[:, :]))
                ch.link(nc.gpsimd.iota(cnt_i[:, 0:1], pattern=[[1, 1]], base=0, channel_multiplier=1))
                ch.link(nc.gpsimd.tensor_copy(pcol[:, :], cnt_i[:, 0:1]))
                ch.restart()
                pool.sem_inc(s_inval, 1)
                for j in range(POOL_UNITS):
                    split_lo_unit(pool, nc.gpsimd, j, 0)
                pool.wait_ge(s_tab, 1)
                for b in range(2):
                    ch.link(nc.gpsimd.tensor_copy(idx[b][:, :], tok_i[:, b:b + 1]))
                    gather_rows(b)
                ch.restart()

            @block.vector
            def _(dve):
                ch = Chain(dve, s_chv)
                V = nc.vector
                ch.add(V.tensor_tensor(gd[:, :, :], tops[:, :, 0, :], tops[:, :, 1, 0:1].to_broadcast([P, NTT, 8]), ALU.subtract))
                ch.add(V.tensor_tensor(ex[:, :], tops[:, :, 2, 1], tops[:, :, 2, 0], ALU.subtract))
                ch.wait()
                dve.sem_inc(s_exi, 1)
                dve.wait_ge(s_inval, 1)
                dve.wait_ge(s_cnt, 1)
                ch.link(V.tensor_scalar(cnt[:, :], bank[0][:, 0:NE], float(P - 1), float(P), ALU.add, ALU.max))
                ch.link(V.tensor_copy(cnt_i[:, :], cnt[:, :]))
                ch.link(V.tensor_scalar(cnt_i[:, :], cnt_i[:, :], 7, None, ALU.arith_shift_right))
                ch.add(V.tensor_copy(nblk[:, :], cnt_i[:, :]))
                ch.link(V.memset(zero[:, :], 0.0))
                ch.link(V.tensor_tensor_scan(cum_f[:, :], nblk[:, :], zero[:, :], 0.0, ALU.add, ALU.add))
                ch.link(V.tensor_tensor(first[:, :], cum_f[:, :], nblk[:, :], ALU.subtract))
                ch.link(V.tensor_scalar(first[:, :], first[:, :], float(P), None, ALU.mult))
                pf = picked[:, :, :, :].rearrange("p t n e -> p (t n) e")
                po = pos[:, :, :, :].rearrange("p t n e -> p (t n) e")
                ch.link(V.tensor_tensor(po, pf, first[:, :].unsqueeze(1).to_broadcast([P, M, NE]), ALU.mult))
                ch.link(V.tensor_reduce(dest[:, :], po, AX_X, ALU.add))
                ch.link(V.tensor_tensor(dest[:, :], dest[:, :], rank[:, :, :].rearrange("p t n -> p (t n)"), ALU.add))
                di = dest_i[:, :, :].rearrange("p t n -> p (t n)")
                ch.link(V.tensor_copy(di, dest[:, :]))
                ch.link(V.tensor_scalar(hi_i[:, :], di, 7, None, ALU.arith_shift_right))
                ch.add(V.tensor_copy(hi_f[:, :], hi_i[:, :]))
                ch.add(V.tensor_scalar(gsum[:, 0:1], pcol[:, :], float(NS), 1.0e4, ALU.is_ge, ALU.mult))
                ch.wait()
                ch.link(V.tensor_scalar(hi_f[:, M - 2:M], hi_f[:, M - 2:M], gsum[:, 0:1], None, ALU.add))
                for c in range(0, M, CHUNK):
                    m = slice(c, c + CHUNK)
                    ch.link(V.tensor_tensor(oh_blk[:, m, :], iota[:, 0:NB].unsqueeze(1).to_broadcast([P, CHUNK, NB]),
                                            hi_f[:, m].unsqueeze(2).to_broadcast([P, CHUNK, NB]), ALU.is_equal))
                    dve.sem_inc(s_ohb, 1)
                    ch.link(V.tensor_tensor(oh_hi[:, m, 1, :], oh_blk[:, m, :],
                                            tile_f[:, m].unsqueeze(2).to_broadcast([P, CHUNK, NB]), ALU.mult))
                    dve.sem_inc(s_oh, 1)
                ch.link(V.tensor_tensor(cmp[:, :, :], cum_f[0:1, :].unsqueeze(1).to_broadcast([1, NB, NE]),
                                        iota[0:1, 0:NB].unsqueeze(2).to_broadcast([1, NB, NE]), ALU.is_le))
                dve.wait_ge(s_tok, 1)
                ch.link(V.tensor_copy(tok_a[:, :, :], bank[1][:, 0:2 * NB].rearrange("p (a b) -> p a b", a=2)))
                ch.link(V.scalar_tensor_tensor(tok_a[:, 0, :], tok_a[:, 1, :], float(P), tok_a[:, 0, :], ALU.mult, ALU.add))
                ch.link(V.tensor_copy(tok_i[:, :], tok_a[:, 0, :]))
                dve.sem_inc(s_tab, 1)
                ch.link(V.tensor_reduce(blk_f[:, :], cmp[:, :, :], AX_X, ALU.add))
                ch.link(V.tensor_scalar(blk_f[:, :], blk_f[:, :], float(NE - 1), None, ALU.min))
                ch.link(V.tensor_copy(blk_e[:, :], blk_f[:, :]))
                ch.link(V.tensor_copy(cum_i[:, :], cum_f[0:1, :]))
                dve.wait_ge(s_exo, 2)
                ch.link(V.tensor_reduce(gsum[:, :], gd[:, :, 0:NRG], AX_X, ALU.add))
                ch.link(V.tensor_scalar(den[:, :], ex[:, :], 1.0, None, ALU.add))
                ch.link(V.tensor_tensor(den[:, :], den[:, :], gsum[:, :], ALU.mult))
                ch.link(V.reciprocal(wt[:, :, 0], den[:, :]))
                ch.link(V.tensor_tensor(wt[:, :, 1], wt[:, :, 0], ex[:, :], ALU.mult))
                for j in range(POOL_UNITS, SPLIT_EARLY):
                    split_lo_unit(dve, V, j, 0)
                ch.restart()

            @block.scalar
            def _(act):
                act.wait_ge(s_exi, 1)
                nc.scalar.activation(gd[:, :, :], gd[:, :, :], ACT.Exp).then_inc(s_exo, 1)
                nc.scalar.activation(ex[:, :], ex[:, :], ACT.Exp).then_inc(s_exo, 1)
                EARLY_UNITS = 2 * EARLY
                for j in range(EARLY_UNITS):
                    split_hi_unit(act, j, 0)
                for c in range(0, M, CHUNK):
                    act.wait_ge(s_ohb, c // CHUNK + 1)
                    nc.scalar.activation(oh_hi[:, c:c + CHUNK, 0, :], oh_blk[:, c:c + CHUNK, :], ACT.Copy,
                                         scale=pcol[:, 0:1]).then_inc(s_oha, 1)
                for j in range(EARLY_UNITS, NU - 1):
                    split_hi_unit(act, j, 0)
                act.wait_ge(s_tok, 1)
                split_hi_unit(act, NU - 1, 0)

            @block.sync
            def _(sp):
                for pair in range(EARLY, NU // 2):
                    load_units(sp, 0, pair)

        s_gu = sem("gate_up_units_passed")
        s_tb = sem("last_rows_loaded")
        s_xl = [sem(f"x1_loaded{i}") for i in range(LB)]
        s_dn = sem("down_units_passed")
        s_xTp = sem("xT_in_psum")
        s_xh = sem("xT_hi_ready")
        s_xT = sem("xT_ready")
        s_sg = sem("silu_ready")
        s_act = sem("act_ready")
        s_aTp = sem("actT_in_psum")
        s_ah = sem("actT_hi_ready")
        s_aT = sem("actT_ready")
        s_y = sem("y_saved")
        s_ys = [sem(f"y_stored{i}") for i in range(2)]

        SURE = NE // 2 + 1
        GROUP = 4
        assert (PAIRS - SURE) % GROUP == 0

        def pairs(eng, step):
            blocks = eng.value_load(cum_i[0:1, NE - 1:NE], min_val=NE, max_val=MAXB)
            for s in range(4):
                step(s, s % 2)
            with eng.Fori(2, SURE) as i:
                for b in range(2):
                    step(i * 2 + b, b)
            with eng.Fori(0, (PAIRS - SURE) // GROUP) as g:
                with eng.If(g * (2 * GROUP) + 2 * SURE < blocks + 1):
                    with eng.Fori(0, GROUP) as j:
                        s = g * (2 * GROUP) + j * 2 + 2 * SURE
                        with eng.If(s < blocks + 1):
                            for b in range(2):
                                step(s + b, b)

        def expert_of(eng, s):
            return eng.value_load(blk_e[0:1, ds(s, 1)], min_val=0, max_val=NE - 1)

        def refills(eng, split, s, e, gate_up):
            if gate_up:
                nxt = expert_of(eng, s + 1)
                with eng.If(e < nxt):
                    for j in range(GU):
                        eng.wait_ge(s_gu, s * GU + j + 1)
                        split(j, nxt)
            else:
                prev = expert_of(eng, s - 1)
                with eng.If(prev < e):
                    for j in range(DN):
                        eng.wait_ge(s_dn, (s - 1) * DN + j + 1)
                        split(GU + j, e)

        with nc.Block() as block:
            @block.sync
            def _(sp):
                def load(e, units):
                    for pair in range(units.start // 2, units.stop // 2):
                        kind, count = halves_count(2 * pair + 1, e - 1)
                        sp.wait_ge(s_lo[kind], count)
                        load_units(sp, e, pair)

                load(1, range(0, GU))
                with sp.Fori(1, NE - 1) as e:
                    load(e + 1, range(0, GU))
                    load(e, range(GU, NU))
                load(NE - 1, range(GU, NU))
                for j in (GU - 1, NU - 1):
                    kind, count = halves_count(j, NE - 1)
                    sp.wait_ge(s_lo[kind], count)
                sp.dma_start(g2[:, :], mod_row(5)).then_inc(s_tb, 16)
                sp.dma_start(lg2[:, :], row(ln2_g[0])).then_inc(s_tb, 16)
                sp.dma_start(lb2[:, :], row(ln2_b[0])).then_inc(s_tb, 16)
                for b in range(LB):
                    sp.dma_start(xf[b][:, :], x1_d[b * P:(b + 1) * P, :]).then_inc(s_xl[b], 16)

            @block.tensor
            def _(pe):
                def x_transposes(s, b):
                    pe.wait_ge(s_xg[b], (s - b) * 8 + 16)
                    if not is0(s):
                        pe.wait_ge(s_xT, s)
                    for k in range(KD):
                        ins = nc.tensor.transpose(ps2[0][:, k * P:(k + 1) * P], xg[b][:, k * P:(k + 1) * P], ident[:, :])
                    ins.then_inc(s_xTp, 1)

                def unit(outs, a_hi, a_lo, u, first, last):
                    for n in range(2):
                        q = slice(n * BANK, (n + 1) * BANK)
                        nc.tensor.matmul(outs[n], a_hi, w_hi[u][:, q], start=first, stop=False)
                    for n in range(2):
                        q = slice(n * BANK, (n + 1) * BANK)
                        nc.tensor.matmul(outs[n], a_hi, w_lo[u][:, q], start=False, stop=False)
                    for n in range(2):
                        q = slice(n * BANK, (n + 1) * BANK)
                        ins = nc.tensor.matmul(outs[n], a_lo, w_hi[u][:, q], start=False, stop=last)
                    return ins

                def step(s, b):
                    e = expert_of(pe, s)
                    pe.wait_ge(s_xT, s + 1)
                    if not is0(s):
                        pe.wait_ge(s_sg, s)
                        pe.wait_ge(s_act, s)
                    for k in range(GU):
                        pe.wait_ge(s_lo[0], e * GU + k + 1)
                        unit((bank[2], bank[3]), xT_hi[b][:, k, :], xT_lo[b][:, k, :], k, k == 0, k == GU - 1).then_inc(s_gu, 1)
                    x_transposes(s + 1, 1 - b)
                    if not is0(s):
                        prev = expert_of(pe, s - 1)
                        pe.wait_ge(s_aT, s)
                        if not (isinstance(s, int) and s == 1):
                            pe.wait_ge(s_y, s - 1)
                        for k in range(DN):
                            pe.wait_ge(s_lo[1], prev * DN + k + 1)
                            unit((bank[4], bank[5]), actT_hi[:, k, :], actT_lo[:, k, :], GU + k, k == 0, k == DN - 1).then_inc(s_dn, 1)
                    pe.wait_ge(s_act, s + 1)
                    if not is0(s):
                        pe.wait_ge(s_aT, s)
                    for k in range(KF):
                        ins = nc.tensor.transpose(bank[6][:, k * P:(k + 1) * P], act_t[:, k * P:(k + 1) * P], ident[:, :])
                    ins.then_inc(s_aTp, 1)

                x_transposes(0, 0)
                pairs(pe, step)

            @block.scalar
            def _(act):
                def save_xT(s, b):
                    act.wait_ge(s_xTp, s + 1)
                    if not (isinstance(s, int) and s < 2):
                        act.wait_ge(s_gu, (s - 1) * GU)
                    nc.scalar.copy(xT_hi[b][:, :, :], ps2[0][:, :].rearrange("p (k t) -> p k t", k=KD)).then_inc(s_xh, 1)

                def step(s, b):
                    e = expert_of(act, s)
                    refills(act, lambda j, e: split_hi_unit(act, j, e), s, e, True)
                    act.wait_ge(s_gu, s * GU + GU)
                    if not is0(s):
                        act.wait_ge(s_act, s)
                    nc.scalar.activation(sgate[:, :], bank[2], ACT.Silu).then_inc(s_sg, 1)
                    save_xT(s + 1, 1 - b)
                    if not is0(s):
                        refills(act, lambda j, e: split_hi_unit(act, j, e), s, e, False)
                        act.wait_ge(s_dn, s * DN)
                        if not (isinstance(s, int) and s < 3):
                            act.wait_ge(s_ys[1 - b], (s - 1 - (1 - b)) * 8)
                        nc.scalar.copy(y_sb[1 - b][:, :], ps2[2][:, :]).then_inc(s_y, 1)
                    act.wait_ge(s_aTp, s + 1)
                    nc.scalar.copy(actT_hi[:, :, :], bank[6].rearrange("p (k t) -> p k t", k=KF)).then_inc(s_ah, 1)

                save_xT(0, 0)
                pairs(act, step)

            @block.vector
            def _(dve):
                def save_xT(s, b):
                    dve.wait_ge(s_xh, s + 1)
                    if not (isinstance(s, int) and s < 2):
                        dve.wait_ge(s_gu, (s - 1) * GU)
                    nc.vector.tensor_tensor(xT_lo[b][:, :, :], ps2[0][:, :].rearrange("p (k t) -> p k t", k=KD),
                                            xT_hi[b][:, :, :].bitcast(F32), ALU.subtract).then_inc(s_xT, 1)

                def step(s, b):
                    e = expert_of(dve, s)
                    refills(dve, lambda j, e: split_lo_unit(dve, nc.vector, j, e), s, e, True)
                    dve.wait_ge(s_sg, s + 1)
                    dve.wait_ge(s_gu, s * GU + GU)
                    if not is0(s):
                        dve.wait_ge(s_aTp, s)
                    nc.vector.tensor_tensor(act_t[:, :], sgate[:, :], bank[3], ALU.mult).then_inc(s_act, 1)
                    save_xT(s + 1, 1 - b)
                    if not is0(s):
                        refills(dve, lambda j, e: split_lo_unit(dve, nc.vector, j, e), s, e, False)
                        dve.wait_ge(s_dn, s * DN)
                    dve.wait_ge(s_ah, s + 1)
                    nc.vector.tensor_tensor(actT_lo[:, :, :], bank[6].rearrange("p (k t) -> p k t", k=KF),
                                            actT_hi[:, :, :].bitcast(F32), ALU.subtract).then_inc(s_aT, 1)

                save_xT(0, 0)
                for j in range(SPLIT_EARLY, GU):
                    split_lo_unit(dve, nc.vector, j, 0)
                pairs(dve, step)

            @block.gpsimd
            def _(pool):
                ch = Chain(pool, s_chp)

                def gather(s, b):
                    if not (isinstance(s, int) and s < 2):
                        pool.wait_ge(s_xTp, s - 1)
                        pool.wait_ge(s_xg[b], (s - b) * 8)
                    ch.link(nc.gpsimd.tensor_copy(idx[b][:, :], tok_i[:, ds(s, 1)]))
                    gather_rows(b)

                def step(s, b):
                    gather(s + 2, b)
                    if not is0(s):
                        pool.wait_ge(s_y, s)
                        pool.dma_start(ye_d[ds((s - 1) * P, P), :], y_sb[1 - b][:, :]).then_inc(s_ys[1 - b], 16)
                    ch.restart()

                for j in range(GU, NU):
                    split_lo_unit(pool, nc.gpsimd, j, 0)
                pairs(pool, step)
                blocks = pool.value_load(cum_i[0:1, NE - 1:NE], min_val=NE, max_val=MAXB)
                more = pool.snap(blocks // 2)
                pool.wait_ge(s_ys[0], more * 16 + 16)
                pool.wait_ge(s_ys[1], more * 16)
                pool.wait_ge(s_xg[0], more * 16 + 32)
                pool.wait_ge(s_xg[1], more * 16 + 32)

        s_ya = [sem(f"y_rows_gathered{i}") for i in range(LB)]
        s_g2s = sem("sample_gate2_loaded")
        s_dg = sem("pick_weights_ready")
        s_pd = sem("rows_combined")
        s_f0 = sem("combined_rows_read")
        s_f1 = sem("x1_added")
        s_v2 = sem("x2_var_ready")
        s_s2 = sem("x2_std_ready")
        s_n2 = sem("x2_scale_ready")
        s_nm = sem("x2_normed")
        s_x2 = sem("x2_scaled")
        s_fo = sem("out_ready")
        s_fs = [sem(f"out_stored{i}") for i in range(2)]

        def rows_of(t):
            return NS if isinstance(t, int) and t == NT else P

        def groups(eng, frame):
            for t in range(LB):
                frame(t, t % LB)
            with eng.Fori(1, NT // LB - 1) as i:
                for b in range(LB):
                    frame(i * LB + b, b)
            for t in range(NT - LB, NT + 2):
                frame(t, t % LB)

        with nc.Block() as block:
            @block.sync
            def _(sp):
                def frame(t, b):
                    if there(t):
                        sp.wait_ge(s_f1, t + 1)
                    if is0(t - (NT - 1)):
                        sp.dma_start(g2[0:NS, :], mod_d[0:NS, 5 * D:6 * D]).then_inc(s_g2s, 16)
                    if not isinstance(t, int) or t + LB <= NT:
                        n = rows_of(t + LB)
                        sp.dma_start(xf[b][0:n, :], x1_d[ds((t + LB) * P, n), :]).then_inc(s_xl[b], 16)
                    if there(t - 1):
                        sp.wait_ge(s_fo, t)
                        if rows_of(t - 1) == NS:
                            sp.dma_start(y_sample[:, 0, :], fo[(b - 1) % 2][0:NS, :]).then_inc(s_fs[(b - 1) % 2], 16)
                        else:
                            sp.dma_start(y_prompt[0, ds((t - 1) * P, P), :], fo[(b - 1) % 2][:, :]).then_inc(s_fs[(b - 1) % 2], 16)

                groups(sp, frame)
                for b in range(2):
                    sp.wait_ge(s_fs[b], 16 * (NT // 2 + 1 - b))

            @block.gpsimd
            def _(pool):
                ch = Chain(pool, s_chp)

                def gathers(t, b):
                    n = rows_of(t)
                    if not (isinstance(t, int) and t < LB):
                        pool.wait_ge(s_pd, t - LB + 1)
                    ch.link(nc.gpsimd.tensor_copy(idy[b][0:n, :], dest_i[0:n, ds(t, 1), :].rearrange("p a n -> p (a n)")))
                    for m, y in enumerate((ya, yb)):
                        nc.gpsimd.indirect_dma_start(out=y[b][0:n, :], out_offset=None, in_=ye_d[:, :],
                                                     in_offset=bass.IndirectOffsetOnAxis(ap=idy[b][0:n, m:m + 1], axis=0)).then_inc(s_ya[b], 16)
                    ch.restart()

                def add_bias(t, b):
                    n = rows_of(t)
                    pool.wait_ge(s_x2, t + 1)
                    if not (isinstance(t, int) and t < 2):
                        pool.wait_ge(s_fs[b % 2], (t - b % 2) * 8)
                    nc.gpsimd.tensor_tensor(fo[b % 2][0:n, :], f_b[b][0:n, :], lb2[0:n, :], ALU.add).then_inc(s_fo, 1)

                def frame(t, b):
                    if not isinstance(t, int) or t + LB <= NT:
                        gathers(t + LB, b)
                    if there(t - 1):
                        add_bias(t - 1, (b - 1) % LB)

                for t in range(LB):
                    gathers(t, t)
                pool.wait_ge(s_tb, 48)
                groups(pool, frame)

            @block.tensor
            def _(pe):
                def frame(t, b):
                    if not there(t):
                        return
                    n = rows_of(t)
                    pe.wait_ge(s_dg, t + 1)
                    pe.wait_ge(s_ya[b], (t - b) * 8 + 32)
                    if not (isinstance(t, int) and t < LB):
                        pe.wait_ge(s_f0, t - LB + 1)
                    for h in range(2):
                        q = slice(h * BANK, (h + 1) * BANK)
                        nc.tensor.matmul(ps2[b][0:n, q], dg[b][0][0:n, 0:n], ya[b][0:n, q], start=True, stop=False)
                        ins = nc.tensor.matmul(ps2[b][0:n, q], dg[b][1][0:n, 0:n], yb[b][0:n, q], start=False, stop=True)
                    ins.then_inc(s_pd, 1)

                groups(pe, frame)

            @block.vector
            def _(dve):
                ch = Chain(dve, s_chv)

                def combine(t, b):
                    n = rows_of(t)
                    q = slice(0, n)
                    if n == NS:
                        dve.wait_ge(s_g2s, 16)
                        ch.link(nc.vector.tensor_scalar_add(g2[q, :], g2[q, :], 1.0))
                    dve.wait_ge(s_pd, t + 1)
                    ch.link(nc.vector.tensor_tensor(f_a[q, :], ps2[b][q, :], g2[q, :], ALU.mult))
                    dve.sem_inc(s_f0, 1)
                    dve.wait_ge(s_xl[b], (t - b) * 4 + 16)
                    if not (isinstance(t, int) and t < LB):
                        dve.wait_ge(s_fo, t - LB + 1)
                    ch.link(nc.vector.scalar_tensor_tensor(f_b[b][q, :], xf[b][q, :], ALPHA, f_a[q, :], ALU.mult, ALU.add))
                    dve.sem_inc(s_f1, 1)
                    for h in range(2):
                        ch.add(nc.vector.bn_stats(bs2[q, h, :], f_b[b][q, h * BANK:(h + 1) * BANK]))
                    ch.wait()
                    nc.vector.bn_aggr(mv2[b % 2][q, :], bs2[q, :, :].rearrange("p a s -> p (a s)")).then_inc(s_v2, 1)

                def scale(t, b):
                    q = slice(0, rows_of(t))
                    dve.wait_ge(s_nm, t + 1)
                    ch.link(nc.vector.tensor_tensor(f_b[b][q, :], f_b[b][q, :], lg2[q, :], ALU.mult))
                    dve.sem_inc(s_x2, 1)

                def moments(t, b):
                    q = slice(0, rows_of(t))
                    dve.wait_ge(s_s2, t + 1)
                    ch.link(nc.vector.reciprocal(iv2[b % 2][q, :], sd2[q, :]))
                    nc.vector.tensor_scalar(nb2[b % 2][q, :], mv2[b % 2][q, 0:1], iv2[b % 2][q, 0:1], -1.0,
                                            ALU.mult, ALU.mult).then_inc(s_n2, 1)

                def frame(t, b):
                    if there(t):
                        combine(t, b)
                    if there(t - 1):
                        scale(t - 1, (b - 1) % LB)
                    if there(t):
                        moments(t, b)
                    ch.restart()

                dve.wait_ge(s_tb, 48)
                ch.link(nc.vector.tensor_scalar_add(g2[:, :], g2[:, :], 1.0))
                groups(dve, frame)

            @block.scalar
            def _(act):
                ch = Chain(act, s_cha)

                def weights(t, b):
                    n = rows_of(t)
                    if not (isinstance(t, int) and t < LB):
                        act.wait_ge(s_pd, t - LB + 1)
                    for m in range(2):
                        ch.add(nc.scalar.activation(dg[b][m][0:n, 0:n], ident[0:n, 0:n], ACT.Copy,
                                                    scale=wt[0:n, ds(t, 1), m:m + 1].rearrange("p a n -> p (a n)")))
                    ch.wait()
                    act.sem_inc(s_dg, 1)

                def norm(t, b):
                    n = rows_of(t)
                    act.wait_ge(s_v2, t + 1)
                    nc.scalar.activation(sd2[0:n, :], mv2[b % 2][0:n, 1:2], ACT.Sqrt, bias=eps[0:n, :]).then_inc(s_s2, 1)
                    act.wait_ge(s_n2, t + 1)
                    nc.scalar.activation(f_b[b][0:n, :], f_b[b][0:n, :], ACT.Identity, bias=nb2[b % 2][0:n, :],
                                         scale=iv2[b % 2][0:n, :]).then_inc(s_nm, 1)

                def frame(t, b):
                    if not isinstance(t, int) or t + 3 <= NT:
                        weights(t + 3, (b + 3) % LB)
                    if there(t):
                        norm(t, b)
                    ch.restart()

                for t in range(3):
                    weights(t, t)
                groups(act, frame)


_INS = ["x_prompt", "x_sample", "state_pool", "c_prompt", "c_sample", "w_ada", "b_ada", "w_in", "pool_w", "pool_scale",
        "sgu_norm_g", "sgu_w", "sgu_b", "w_out", "ln1_g", "ln1_b", "router_g_w", "router_g_b", "router_e_w",
        "router_e_b", "exp_w_gate", "exp_w_up", "exp_w_down", "ln2_g", "ln2_b"]
_OUTS = [(1, 2048, 1024), (8, 1, 1024), (1, 1, 15, 512), (1, 8, 15, 512), (1, 8, 1, 512)]


def kernel(**inputs):
    import numpy as _np
    import concourse.bacc as _bacc
    from concourse import mybir as _mybir
    from concourse.bass_utils import run_bass_kernel_spmd as _run

    nc = _bacc.Bacc("TRN2", target_bir_lowering=False, num_devices=1)
    arrays, args = {}, []
    for name in _INS:
        a = _np.ascontiguousarray(inputs[name])
        arrays[f"in_{name}_dram"] = a
        args.append(nc.dram_tensor(f"in_{name}_dram", a.shape, _mybir.dt.from_np(a.dtype), kind="ExternalInput").ap())
    for i, shape in enumerate(_OUTS):
        args.append(nc.dram_tensor(f"out_{i}_dram", shape, _mybir.dt.float32, kind="ExternalOutput").ap())
    hybrid_trunk(nc, *args)
    r = _run(nc, [arrays], core_ids=[0])
    return tuple(r.results[0][f"out_{i}_dram"] for i in range(len(_OUTS)))
```
